# Optimizing a Trainium2 kernel written in Bass

```python
import jax, jax.numpy as jnp
from jax import lax
import numpy as np

D_MODEL = 2048
BATCH = 1
SEQ = 128
DEPTH = 1
DEC_BATCH = 1
DEC_SEQ = 128
PAST_LEN = 128

GRID_W = 64
NA_HEADS = 8
HEAD_DIM = 128
NA_WIDTH = NA_HEADS * HEAD_DIM
FOURIER_GROUPS = 4
FOURIER_GROUP_DIM = 256
FOURIER_WIDTH = FOURIER_GROUPS * FOURIER_GROUP_DIM
WIN_ROWS_MAX = 8
WIN_COLS = 16
N_GROUPS = 4
EXPERTS_PER_GROUP = 4
N_EXPERTS = N_GROUPS * EXPERTS_PER_GROUP
TOP_K_FINE = 2
EXPERT_HIDDEN = 512
N_MOD = 6
IN_WIDTH = FOURIER_WIDTH + 3 * NA_WIDTH + 2 * D_MODEL
Q_BLOCK = 128
EPS = 1e-6
NEG_INF = -1e30

kernel_name = "hybrid_fnet_natten_hmoe_diffusion_step"

def _rmsnorm(x, g):
    xf = x.astype(jnp.float32)
    y = xf * lax.rsqrt(jnp.mean(xf * xf, axis=-1, keepdims=True) + EPS)
    return (y * g.astype(jnp.float32)).astype(x.dtype)

def _adaln(cvec, w_ada, b_ada):
    mod = jax.nn.silu(cvec) @ w_ada + b_ada
    return jnp.split(mod, N_MOD, axis=-1)

def _modulate(x, g, shift, scale):
    return _rmsnorm(x, g) * (1 + scale) + shift

def _project(h, w_in, b_in):
    b, n, _ = h.shape
    p = h @ w_in + b_in
    o = 0
    u_f = p[..., o:o + FOURIER_WIDTH]; o += FOURIER_WIDTH
    q = p[..., o:o + NA_WIDTH].reshape(b, n, NA_HEADS, HEAD_DIM); o += NA_WIDTH
    k = p[..., o:o + NA_WIDTH].reshape(b, n, NA_HEADS, HEAD_DIM); o += NA_WIDTH
    v = p[..., o:o + NA_WIDTH].reshape(b, n, NA_HEADS, HEAD_DIM); o += NA_WIDTH
    g_a = p[..., o:o + D_MODEL]; o += D_MODEL
    g_b = p[..., o:o + D_MODEL]
    return u_f, q, k, v, g_a, g_b

def _fourier_mix(u):
    b, n, _ = u.shape
    ug = u.reshape(b, n, FOURIER_GROUPS, FOURIER_GROUP_DIM).astype(jnp.float32)
    f = jnp.fft.fft2(ug, axes=(1, 3), norm="ortho").real
    return f.reshape(b, n, FOURIER_WIDTH).astype(u.dtype)

def _ctx_self_attention(q, k, v):
    b, l, h, d = q.shape
    nb = l // Q_BLOCK
    scale = HEAD_DIM ** -0.5
    qb = q.reshape(b, nb, Q_BLOCK, h, d).transpose(1, 0, 2, 3, 4)

    def blk(qi):
        s = jnp.einsum('bqhd,bkhd->bhqk', qi, k).astype(jnp.float32) * scale
        p = jax.nn.softmax(s, axis=-1).astype(v.dtype)
        return jnp.einsum('bhqk,bkhd->bqhd', p, v)

    o = lax.map(blk, qb)
    return o.transpose(1, 0, 2, 3, 4).reshape(b, l, h * d)

def _latent_na(q, k, v, k_ctx, v_ctx, rpb):
    b, n, h, d = q.shape
    rows = n // GRID_W
    kh = min(WIN_ROWS_MAX, rows)
    scale = HEAD_DIM ** -0.5
    qg = q.reshape(b, rows, GRID_W, h, d)
    kg = k.reshape(b, rows, GRID_W, h, d)
    vg = v.reshape(b, rows, GRID_W, h, d)
    col = np.arange(GRID_W)
    col_start = np.clip(col - WIN_COLS // 2, 0, GRID_W - WIN_COLS)
    col_ok = (col[None, :] >= col_start[:, None]) & (col[None, :] < col_start[:, None] + WIN_COLS)
    dc_idx = np.clip(col[None, :] - col[:, None] + WIN_COLS - 1, 0, 2 * WIN_COLS - 2)
    mask = jnp.asarray(np.broadcast_to(col_ok[:, None, :], (GRID_W, kh, GRID_W)).reshape(GRID_W, kh * GRID_W))

    def row_block(args):
        r, q_r = args
        start = jnp.clip(r - kh // 2, 0, rows - kh)
        k_r = lax.dynamic_slice_in_dim(kg, start, kh, axis=1).reshape(b, kh * GRID_W, h, d)
        v_r = lax.dynamic_slice_in_dim(vg, start, kh, axis=1).reshape(b, kh * GRID_W, h, d)
        dr_idx = start + jnp.arange(kh) - r + WIN_ROWS_MAX - 1
        bias = rpb[:, dr_idx][:, :, dc_idx]
        bias = bias.transpose(0, 2, 1, 3).reshape(h, GRID_W, kh * GRID_W).astype(jnp.float32)
        s_nb = jnp.einsum('bqhd,bkhd->bhqk', q_r, k_r).astype(jnp.float32) * scale + bias
        s_nb = jnp.where(mask, s_nb, NEG_INF)
        s_cx = jnp.einsum('bqhd,bchd->bhqc', q_r, k_ctx).astype(jnp.float32) * scale
        p = jax.nn.softmax(jnp.concatenate([s_nb, s_cx], axis=-1), axis=-1).astype(v.dtype)
        nk = kh * GRID_W
        return (jnp.einsum('bhqk,bkhd->bqhd', p[..., :nk], v_r)
                + jnp.einsum('bhqc,bchd->bqhd', p[..., nk:], v_ctx))

    o = lax.map(row_block, (jnp.arange(rows), qg.transpose(1, 0, 2, 3, 4)))
    return o.transpose(1, 0, 2, 3, 4).reshape(b, n, h * d)

def _merge(u_f, na_out, g_a, g_b, w_fourier, w_na_o, w_out):
    a = _fourier_mix(u_f) @ w_fourier
    bb = na_out @ w_na_o
    merged = jax.nn.sigmoid(g_a) * a + jax.nn.sigmoid(g_b) * bb
    return merged @ w_out

def _hier_moe(h, w_rg, b_rg, w_re, b_re, w_g, w_u, w_d):
    shp = h.shape
    t = h.reshape(-1, D_MODEL)
    lg = (t @ w_rg + b_rg).astype(jnp.float32)
    pg = jax.nn.softmax(lg, axis=-1)
    gsel = jnp.argmax(lg, axis=-1)
    p_sel = jnp.take_along_axis(pg, gsel[:, None], axis=1)
    lf = (t @ w_re + b_re).astype(jnp.float32).reshape(-1, N_GROUPS, EXPERTS_PER_GROUP)
    lf_sel = jnp.take_along_axis(lf, gsel[:, None, None], axis=1)[:, 0]
    tv, ti = lax.top_k(lf_sel, TOP_K_FINE)
    wf = jax.nn.softmax(tv, axis=-1) * p_sel
    eid = gsel[:, None] * EXPERTS_PER_GROUP + ti
    comb = jnp.sum(jax.nn.one_hot(eid, N_EXPERTS, dtype=jnp.float32) * wf[..., None], axis=1).astype(h.dtype)
    y = jnp.zeros_like(t)
    for e in range(N_EXPERTS):
        hid = jax.nn.silu(t @ w_g[e]) * (t @ w_u[e])
        y = y + comb[:, e:e + 1] * (hid @ w_d[e])
    return y.reshape(shp)

def setup_inputs(seed: int = 0) -> dict:
    key = jax.random.key(seed)
    ks = jax.random.split(key, 24)
    f32 = jnp.float32

    def nrm(k, shape, scale):
        return jax.random.normal(k, shape, f32) * scale

    cache_shape = (DEC_BATCH, DEPTH, PAST_LEN, NA_HEADS, HEAD_DIM)
    return {
        "x_prompt": nrm(ks[0], (BATCH, SEQ, D_MODEL), 1.0),
        "x_sample": nrm(ks[1], (DEC_BATCH, DEC_SEQ, D_MODEL), 1.0),
        "cache_k_ctx": nrm(ks[2], cache_shape, 1.0),
        "cache_v_ctx": nrm(ks[3], cache_shape, 1.0),
        "c": nrm(ks[4], (DEC_BATCH, D_MODEL), 1.0),
        "c_ctx": nrm(ks[5], (D_MODEL,), 1.0),
        "norm1_g": 1.0 + nrm(ks[6], (DEPTH, D_MODEL), 0.02),
        "norm2_g": 1.0 + nrm(ks[7], (DEPTH, D_MODEL), 0.02),
        "w_ada": nrm(ks[8], (DEPTH, D_MODEL, N_MOD * D_MODEL), 0.5 * D_MODEL ** -0.5),
        "b_ada": nrm(ks[9], (DEPTH, N_MOD * D_MODEL), 0.01),
        "w_in": nrm(ks[10], (DEPTH, D_MODEL, IN_WIDTH), D_MODEL ** -0.5),
        "b_in": nrm(ks[11], (DEPTH, IN_WIDTH), 0.01),
        "w_fourier": nrm(ks[12], (DEPTH, FOURIER_WIDTH, D_MODEL), FOURIER_WIDTH ** -0.5),
        "w_na_o": nrm(ks[13], (DEPTH, NA_WIDTH, D_MODEL), NA_WIDTH ** -0.5),
        "rpb": nrm(ks[14], (DEPTH, NA_HEADS, 2 * WIN_ROWS_MAX - 1, 2 * WIN_COLS - 1), 0.02),
        "w_out": nrm(ks[15], (DEPTH, D_MODEL, D_MODEL), D_MODEL ** -0.5),
        "w_router_group": nrm(ks[16], (DEPTH, D_MODEL, N_GROUPS), D_MODEL ** -0.5),
        "b_router_group": nrm(ks[17], (DEPTH, N_GROUPS), 0.01),
        "w_router_expert": nrm(ks[18], (DEPTH, D_MODEL, N_EXPERTS), D_MODEL ** -0.5),
        "b_router_expert": nrm(ks[19], (DEPTH, N_EXPERTS), 0.01),
        "w_exp_gate": nrm(ks[20], (DEPTH, N_EXPERTS, D_MODEL, EXPERT_HIDDEN), D_MODEL ** -0.5),
        "w_exp_up": nrm(ks[21], (DEPTH, N_EXPERTS, D_MODEL, EXPERT_HIDDEN), D_MODEL ** -0.5),
        "w_exp_down": nrm(ks[22], (DEPTH, N_EXPERTS, EXPERT_HIDDEN, D_MODEL), EXPERT_HIDDEN ** -0.5),
        "final_norm_g": 1.0 + nrm(ks[23], (D_MODEL,), 0.02),
    }

def reference(x_prompt, x_sample, cache_k_ctx, cache_v_ctx, c, c_ctx,
              norm1_g, norm2_g, w_ada, b_ada, w_in, b_in, w_fourier, w_na_o, rpb, w_out,
              w_router_group, b_router_group, w_router_expert, b_router_expert,
              w_exp_gate, w_exp_up, w_exp_down, final_norm_g):
    xp = x_prompt
    xs = x_sample
    k_list = []
    v_list = []
    for l in range(DEPTH):
        sh1c, sc1c, ga1c, sh2c, sc2c, ga2c = _adaln(c_ctx, w_ada[l], b_ada[l])
        mods = _adaln(c, w_ada[l], b_ada[l])
        sh1s, sc1s, ga1s, sh2s, sc2s, ga2s = [m[:, None, :] for m in mods]

        h = _modulate(xp, norm1_g[l], sh1c, sc1c)
        u_f, q, k, v, g_a, g_b = _project(h, w_in[l], b_in[l])
        k_list.append(k)
        v_list.append(v)
        na = _ctx_self_attention(q, k, v)
        xp = xp + ga1c * _merge(u_f, na, g_a, g_b, w_fourier[l], w_na_o[l], w_out[l])
        h2 = _modulate(xp, norm2_g[l], sh2c, sc2c)
        xp = xp + ga2c * _hier_moe(h2, w_router_group[l], b_router_group[l], w_router_expert[l],
                                   b_router_expert[l], w_exp_gate[l], w_exp_up[l], w_exp_down[l])

        h = _modulate(xs, norm1_g[l], sh1s, sc1s)
        u_f, q, k, v, g_a, g_b = _project(h, w_in[l], b_in[l])
        na = _latent_na(q, k, v, cache_k_ctx[:, l], cache_v_ctx[:, l], rpb[l])
        xs = xs + ga1s * _merge(u_f, na, g_a, g_b, w_fourier[l], w_na_o[l], w_out[l])
        h2 = _modulate(xs, norm2_g[l], sh2s, sc2s)
        xs = xs + ga2s * _hier_moe(h2, w_router_group[l], b_router_group[l], w_router_expert[l],
                                   b_router_expert[l], w_exp_gate[l], w_exp_up[l], w_exp_down[l])

    y_prompt = _rmsnorm(xp, final_norm_g)
    y_sample = _rmsnorm(xs, final_norm_g)
    new_k_ctx = jnp.stack(k_list, axis=1)
    new_v_ctx = jnp.stack(v_list, axis=1)
    return (y_prompt, y_sample, new_k_ctx, new_v_ctx)


_drawn_inputs = setup_inputs


def setup_inputs(seed=0):
    import zlib

    import numpy as np

    out = dict(_drawn_inputs(seed))
    spreads = {}
    factors = {'cache_k_ctx': 2.994,
     'norm1_g': 2.919,
     'norm2_g': 6.919,
     'b_ada': 4.295,
     'b_in': 6.191,
     'rpb': 8.0,
     'b_router_group': 8.0,
     'b_router_expert': 8.0,
     'final_norm_g': 2.877}
    for name, (base, spread) in spreads.items():
        noise = np.random.default_rng([zlib.crc32(name.encode()), seed]).standard_normal(out[name].shape)
        drawn = base * np.exp(spread * noise) if base else spread * noise
        out[name] = __import__('jax').numpy.asarray(drawn.astype(out[name].dtype))
    for name, factor in factors.items():
        out[name] = (out[name] * factor).astype(out[name].dtype)
    return out
```

```python
from contextlib import ExitStack

import numpy as np

import concourse.bass as bass
from concourse import mybir

ALU = mybir.AluOpType
ACT = mybir.ActivationFunctionType
F32 = mybir.dt.float32
F32R = mybir.dt.float32r
X = mybir.AxisListType.X

P = 128
TOK = 128
NS = 2
D = 2048
KD = D // P
COL = 512
HEADS, HD = 8, 128
NA = HEADS * HD
FW, FG, FGD = 1024, 4, 256
KF = FW // P
GRID_W, ROWS, WIN = 64, 2, 16
NG, EPG, NE, EH = 4, 4, 16, 512
KE = EH // P
SCALE = float(HD) ** -0.5
EPS = 1e-6

LOAD_K, UNIT_K = 4, 2
RAW, AHEAD = 4, 4
CHUNK_UNITS = KD // UNIT_K
ONE = 1

C_ID = 0
C_DFTN = C_ID + P
C_DFTC = C_DFTN + 2 * TOK
C_MASK = C_DFTC + 2 * 2 * FGD
C_SEL = C_MASK + TOK
C_SELB = C_SEL + NS
C_FIRST = C_SELB + NS * P
C_ALL = C_FIRST + EPG


def shape_constants():
    c = np.zeros((P, C_ALL), np.float64)
    c[:, C_ID:C_ID + P] = np.eye(P)
    n = np.arange(TOK)
    ang = 2 * np.pi * (np.outer(n, n) % TOK) / TOK
    c[:, C_DFTN:C_DFTN + TOK] = np.cos(ang) / np.sqrt(TOK)
    c[:, C_DFTN + TOK:C_DFTC] = np.sin(ang) / np.sqrt(TOK)
    m = np.arange(FGD)
    ang = 2 * np.pi * (np.outer(m, m) % FGD) / FGD
    both = np.stack([np.cos(ang), -np.sin(ang)], 1) / np.sqrt(FGD)
    c[:, C_DFTC:C_MASK] = both.reshape(2, P, 2, FGD).transpose(1, 0, 2, 3).reshape(P, -1)
    col = np.arange(GRID_W)
    start = np.clip(col - WIN // 2, 0, GRID_W - WIN)
    ok = (col[None, :] >= start[:, None]) & (col[None, :] < start[:, None] + WIN)
    c[:, C_MASK:C_SEL] = np.where(np.tile(ok, (ROWS, ROWS)), 0.0, -1e30)
    for r in range(4):
        c[r, C_SEL + r % NS] = 1.0
    for base in (0, 32):
        for r in range(5):
            for s in range(NS):
                if r == 4 or r % NS == s:
                    c[base + r, C_SELB + s * P:C_SELB + (s + 1) * P] = 1.0
    c[:, C_FIRST:C_ALL] = np.arange(EPG, 0, -1)
    return c.astype(np.float32)


class Tally:

    def __init__(self, engine, sem):
        self.engine, self.sem, self.base, self.n = engine, sem, 0, 0

    def mark(self, instruction):
        instruction.then_inc(self.sem, 1)
        self.n += 1

    def settle(self):
        self.engine.wait_ge(self.sem, self.base + self.n)

    def enter(self, i, per):
        self.start, self.per = self.base + self.n, per
        self.base, self.n = i * per + self.start, 0

    def leave(self, count):
        assert self.n == self.per, (self.n, self.per)
        self.base, self.n = self.start + count * self.per, 0


def backbone_step(nc, x_prompt, x_sample, cache_k, cache_v, c, c_ctx, norm1_g, norm2_g, w_ada, b_ada,
                  w_in, b_in, w_fourier, w_na_o, rpb, w_out, w_rg, b_rg, w_re, b_re, w_gate, w_up,
                  w_down, final_g, constants, y_prompt, y_sample, new_k, new_v):
    ada_v = w_ada.rearrange("l (p k) n -> p (l k) n", k=KD)
    in_v = w_in.rearrange("l (k p) n -> p (l k) n", p=P)
    fo_v = w_fourier.rearrange("l (k p) n -> p (l k) n", p=P)
    na_v = w_na_o.rearrange("l (k p) n -> p (l k) n", p=P)
    out_v = w_out.rearrange("l (k p) n -> p (l k) n", p=P)
    gate_v = w_gate.rearrange("l e (k p) n -> p (l e k) n", p=P)
    up_v = w_up.rearrange("l e (k p) n -> p (l e k) n", p=P)
    down_v = w_down.rearrange("l e (k p) n -> p (l e k) n", p=P)
    rg_v = w_rg.rearrange("l (k p) n -> p (l k) n", p=P)
    re_v = w_re.rearrange("l (k p) n -> p (l k) n", p=P)
    kc_v = cache_k.rearrange("a l t h d -> t (a l h) d")
    vc_v = cache_v.rearrange("a l t h d -> t (a l h) d")
    x_v = [x_prompt.rearrange("a t n -> (a t) n"), x_sample.rearrange("a t n -> (a t) n")]
    y_v = [y_prompt.rearrange("a t n -> (a t) n"), y_sample.rearrange("a t n -> (a t) n")]
    NR = HEADS * 3
    skew = nc.dram_tensor("bias_rows", [GRID_W, NR, P], F32, kind="Internal")

    with ExitStack() as ctx:
        at = [16512]

        def region(size):
            at[0] += size
            return at[0] - size

        def place(name, shape, offset, dt=F32):
            return nc.alloc_sbuf_tensor_at(name, shape, dt, offset=offset).ap()

        def own(name, shape, dt=F32):
            size = 4 * int(np.prod(shape[1:]))
            return place(name, shape, region((size + 31) // 32 * 32), dt)

        def sem(name):
            return ctx.enter_context(nc.semaphore(name))

        KB = 1024
        h_hi = own("h_hi", [P, KD, NS, TOK], F32R)
        h_lo = own("h_lo", [P, KD, NS, TOK], F32R)
        raw = own("raw", [P, RAW, LOAD_K, COL])
        w_hi = own("w_hi", [P, AHEAD, UNIT_K, COL], F32R)
        w_lo = own("w_lo", [P, AHEAD, UNIT_K, COL], F32R)
        A, F, B = region(32 * KB), region(32 * KB), region(16 * KB)
        x0 = place("x0", [P, NS, D], A)
        uqkv = place("uqkv", [P, NS, FW + 3 * NA], A)
        m_hi = place("m_hi", [P, KD, NS, TOK], A, F32R)
        m_lo = place("m_lo", [P, KD, NS, TOK], A + 16 * KB, F32R)
        sg = place("sg", [P, NS, EH], A)
        hid = place("hid", [P, NS, EH], A + 4 * KB)
        hid_hi = place("hid_hi", [P, KE, NS, TOK], A + 8 * KB, F32R)
        hid_lo = place("hid_lo", [P, KE, NS, TOK], A + 12 * KB, F32R)
        gfin = place("gfin", [P, D], A + 16 * KB)
        f_hi = place("f_hi", [P, KF, NS, TOK], F, F32R)
        f_lo = place("f_lo", [P, KF, NS, TOK], F + 8 * KB, F32R)
        o_hi = place("o_hi", [P, KF, NS, TOK], F + 16 * KB, F32R)
        o_lo = place("o_lo", [P, KF, NS, TOK], F + 24 * KB, F32R)
        x1 = place("x1", [P, NS, D], F)
        ysum = place("ysum", [P, NS, D], F + 16 * KB)
        squares = place("squares", [P, D], B)
        htmp = place("htmp", [P, 2, 4, TOK], B + 8 * KB)
        vecrows = place("vecrows", [6 * KD, P], B + 12 * KB)
        rpbpad = place("rpbpad", [NR, P], B + 12 * KB + 512)
        fa = place("fa", [P, 2, 2, FG, NS, TOK], B)
        st = place("st", [P, 2, NS, 3, HD], B)
        cst = place("cst", [P, 2, 2, HD], B + 6 * KB)
        qkT = place("qkT", [P, 4, TOK], B + 8 * KB)
        kcT = place("kcT", [P, TOK], B + 10 * KB)
        scr = place("scr", [P, 3, TOK], B + 10 * KB + 512)
        prb = place("prb", [P, 3, TOK], B + 12 * KB)
        prT = place("prT", [P, 3, TOK], B + 13 * KB + 512)
        ma = place("ma", [P, NS, COL], B)
        mb = place("mb", [P, NS, COL], B + 4 * KB)
        gab = place("gab", [P, 2, NS, COL], B)
        t2 = place("t2", [P, 2, NS, COL], B + 8 * KB)

        garow = own("garow", [37, D])
        bias = own("bias", [P, HEADS, ROWS, GRID_W])
        cst_all = own("cst_all", [P, C_ALL])
        bin_ = own("bin", [P, 2, COL])
        modrow = place("modrow", [4, COL], region(COL * 4))
        ccol = own("ccol", [P, NS, KD])
        csilu = own("csilu", [P, NS, KD])
        cvec = own("cvec", [P, 4 * (KD - 1) + P], F32R)
        mod = own("mod", [P, 4, KD, NS])
        vecT = own("vecT", [P, 6, KD])
        rms = own("rms", [P, 16])
        diag = own("diag", [P, NS, P])
        wr = place("wr", [P, KD, NG + NE], B + 13 * KB)
        wrs = own("wrs", [P, KD, 2, NG + NE], F32R)
        br = own("br", [P, NG + NE])
        lg = own("lg", [P, NS, NG + NE])
        rt = own("rt", [P, 160])
        comb = own("comb", [P, NE, NS])
        smx = own("smx", [P, 8])

        ident = cst_all[:, C_ID:C_ID + P]
        dftn = cst_all[:, C_DFTN:C_DFTC]
        dftc = cst_all[:, C_DFTC:C_MASK].rearrange("p (h c n) -> p h c n", h=2, c=2)
        mask = cst_all[:, C_MASK:C_SEL]
        first = cst_all[:, C_FIRST:C_ALL]

        bank = [ctx.enter_context(nc.psum_tensor(f"bank{i}", [P, COL], F32)) for i in range(8)]
        adaP, modP = bank[7], bank[6]

        raw_landed = [sem(f"raw_landed{i}") for i in range(RAW)]
        hi_ready, lo_ready, unit_used = sem("hi_ready"), sem("lo_ready"), sem("unit_used")
        slots_freed = sem("slots_freed")
        consts_in, cond_in, x_in, rows_in, router_in = (
            sem("consts_in"), sem("cond_in"), sem("x_in"), sem("rows_in"), sem("router_in"))
        rpb_in, skew_out, bias_in = sem("rpb_in"), sem("skew_out"), sem("bias_in")
        pad_zero, cvec_ready, csilu_ready = sem("pad_zero"), sem("cvec_ready"), sem("csilu_ready")
        vecT_done, vecT_ready = sem("vecT_done"), sem("vecT_ready")
        squares_done, diag_ready, mod_ready = sem("squares_done"), sem("diag_ready"), sem("mod_ready")
        var_ready, root_ready = sem("var_ready"), sem("root_ready")
        norm_done, htmp_ready, h_ready = sem("norm_done"), sem("htmp_ready"), sem("h_ready")
        ada_evac, modrow_ready, modT_done, modT_evac = (
            sem("ada_evac"), sem("modrow_ready"), sem("modT_done"), sem("modT_evac"))
        bin_landed = [sem("bin_landed0"), sem("bin_landed1")]
        proj_evac = sem("proj_evac")
        dft1_done, dft1_act, dft1_dve = sem("dft1_done"), sem("dft1_act"), sem("dft1_dve")
        dft2_done, dft2_hi, dft2_lo = sem("dft2_done"), sem("dft2_hi"), sem("dft2_lo")
        head_staged = sem("head_staged")
        ctx_landed = [sem("ctx_landed0"), sem("ctx_landed1")]
        qk_done, qkT_ready, kcT_ready = sem("qk_done"), sem("qkT_ready"), sem("kcT_ready")
        scores_done, scores_ready, exp_done, probs_ready = (
            sem("scores_done"), sem("scores_ready"), sem("exp_done"), sem("probs_ready"))
        prT_done, prT_ready, pv_done, o_hi_ready, o_ready = (
            sem("prT_done"), sem("prT_ready"), sem("pv_done"), sem("o_hi_ready"), sem("o_ready"))
        gate_pre, gate_sig, merged_ready = sem("gate_pre"), sem("gate_sig"), sem("merged_ready")
        mT_done, m_hi_ready, m_ready = sem("mT_done"), sem("m_hi_ready"), sem("m_ready")
        x1_in, gab_ready, x1_ready = (
            sem("x1_in"), sem("gab_ready"), sem("x1_ready"))
        wrs_ready, route_done, comb_ready, y_zero = (
            sem("wrs_ready"), sem("route_done"), sem("comb_ready"), sem("y_zero"))
        silu_ready, hid_ready = sem("silu_ready"), sem("hid_ready")
        hidT_done, hid_hi_ready, hid_lo_ready, down_done, y_added = (
            sem("hidT_done"), sem("hid_hi_ready"), sem("hid_lo_ready"), sem("down_done"), sem("y_added"))
        route_arg, route_exp = sem("route_arg"), sem("route_exp")
        gfin_in, ga2_done, y_ready, out_sent, kv_sent = (
            sem("gfin_in"), sem("ga2_done"), sem("y_ready"), sem("out_sent"), sem("kv_sent"))
        dve_step, act_step, pool_step = sem("dve_step"), sem("act_step"), sem("pool_step")

        U_ADA1 = 0
        U_PROJ = U_ADA1 + 8 * CHUNK_UNITS
        U_ATT = U_PROJ + 16 * CHUNK_UNITS
        U_MERGE = U_ATT + 8 * CHUNK_UNITS
        U_OUT = U_MERGE + 4 * 24
        U_MOE = U_OUT + 4 * CHUNK_UNITS
        U_END = U_MOE + NE * 24

        block = ctx.enter_context(nc.Block())

        @block.sync
        def _(sp):
            def load(view, k0, col, first_load, j, wait=True):
                if wait:
                    sp.wait_ge(lo_ready, 2 * (first_load + j - RAW + 1))
                    sp.sem_inc(slots_freed, 1)
                sp.dma_start(raw[:, j % RAW], view[:, bass.ds(k0, LOAD_K), bass.ds(col, COL)]
                             ).then_inc(raw_landed[j % RAW], 16)

            def chunk(view, tiles, col, first_load, j, k0=0, wait=True):
                for n in range(tiles // LOAD_K):
                    load(view, k0 + LOAD_K * n, col, first_load, j + n, wait)

            chunk(ada_v, KD, 0, 0, 0, wait=False)
            with sp.Fori(1, 8) as i:
                chunk(ada_v, KD, i * COL, i * 4, 0)
            with sp.Fori(0, 4) as i:
                base = i * 16 + U_PROJ // 2
                chunk(ada_v, KD, i * COL + 2 * D, base, 0)
                chunk(in_v, KD, i * (2 * COL), base, 4)
                chunk(ada_v, KD, i * COL + 3 * D, base, 8)
                chunk(in_v, KD, i * (2 * COL) + COL, base, 12)
            with sp.Fori(0, 4) as i:
                base = i * 8 + U_ATT // 2
                chunk(ada_v, KD, i * COL + 4 * D, base, 0)
                chunk(ada_v, KD, i * COL + 5 * D, base, 4)
            with sp.Fori(0, 4) as i:
                base = i * 12 + U_MERGE // 2
                chunk(in_v, KD, i * COL + FW + 3 * NA, base, 0)
                chunk(in_v, KD, i * COL + FW + 3 * NA + D, base, 4)
                chunk(fo_v, KF, i * COL, base, 8)
                chunk(na_v, KF, i * COL, base, 10)
            with sp.Fori(0, 4) as i:
                chunk(out_v, KD, i * COL, i * 4 + U_OUT // 2, 0)
            with sp.Fori(0, NE) as e:
                base = e * 12 + U_MOE // 2
                chunk(gate_v, KD, 0, base, 0, k0=e * KD)
                chunk(up_v, KD, 0, base, 4, k0=e * KD)
                for n in range(D // COL):
                    load(down_v, e * KE, n * COL, base, 8 + n)
            for n in range(D // COL):
                for s in range(NS):
                    sp.wait_ge(y_ready, n * NS + s + 1)
                    sp.dma_start(y_v[s][:, n * COL:(n + 1) * COL],
                                 x1[:, s, n * COL:(n + 1) * COL]).then_inc(out_sent, 16)
            sp.wait_ge(out_sent, 16 * NS * (D // COL))
            sp.wait_ge(kv_sent, 32)

        @block.gpsimd
        def _(pool):
            step = Tally(pool, pool_step)
            nc.gpsimd.memset(rpbpad[:], 0.0).then_inc(pad_zero, 1)
            pool.dma_start(cst_all[:], constants).then_inc(consts_in, 16)
            pool.wait_ge(pad_zero, 1)
            for h in range(HEADS):
                pool.dma_start(rpbpad[3 * h:3 * h + 3, 48:48 + 2 * WIN - 1], rpb[0, h, 6:9, :]).then_inc(rpb_in, 16)
            pool.dma_start(wr[:, :, 0:NG], rg_v).then_inc(router_in, 16)
            pool.dma_start(wr[:, :, NG:], re_v).then_inc(router_in, 16)
            pool.dma_start(br[:, 0:NG], b_rg[0].partition_broadcast(P)).then_inc(router_in, 16)
            pool.dma_start(br[:, NG:], b_re[0].partition_broadcast(P)).then_inc(router_in, 16)
            pool.wait_ge(rpb_in, 16 * HEADS)
            sk = skew.ap()
            pool.dma_start(sk.rearrange("c r j -> r c j"),
                           bass.AP(rpbpad.tensor, rpbpad.offset, [list(rpbpad.ap[0]), [0, GRID_W], [1, P]])
                           ).then_inc(skew_out, 16)
            pool.wait_ge(skew_out, 16)
            for r in range(ROWS):
                for kr in range(ROWS):
                    pool.dma_start(bias[r * GRID_W:(r + 1) * GRID_W, :, kr],
                                   bass.AP(sk.tensor, (1 - r + kr) * P + GRID_W - 1,
                                           [[NR * P - 1, GRID_W], [3 * P, HEADS], [1, GRID_W]])
                                   ).then_inc(bias_in, 16)

            def load_bin(col, j):
                pool.dma_start(bin_[:, j], b_in[0, bass.ds(col, COL)].partition_broadcast(P)
                               ).then_inc(bin_landed[j], 16)

            for j in range(2):
                load_bin(j * COL, j)
            with pool.Fori(0, 3) as i:
                for j in range(2):
                    pool.wait_ge(proj_evac, i * 2 + j + 1 + ONE)
                    load_bin(i * (2 * COL) + (2 + j) * COL, j)
            pool.wait_ge(proj_evac, 8 + ONE)
            for n, dst in enumerate((new_k, new_v)):
                pool.dma_start(dst.rearrange("a l t h d -> (a l t) (h d)"),
                               uqkv[:, 0, FW + (1 + n) * NA:FW + (2 + n) * NA]).then_inc(kv_sent, 16)

            heads = uqkv[:].rearrange("p s (c h d) -> p s c h d", c=4, h=HEADS)

            def stage(h, j):
                for s in range(NS):
                    copy = nc.gpsimd.tensor_copy(st[:, j, s].rearrange("p c (a d) -> p c a d", a=1), heads[:, s, 1:4, bass.ds(h, 1), :])
                copy.then_inc(head_staged, 1)
                pool.dma_start(cst[:, j, 0:1], kc_v[:, bass.ds(h, 1), :]).then_inc(ctx_landed[j], 16)
                pool.dma_start(cst[:, j, 1:2], vc_v[:, bass.ds(h, 1), :]).then_inc(ctx_landed[j], 16)

            pool.wait_ge(dft2_done, 4)
            for j in range(2):
                stage(j, j)
            with pool.Fori(0, 3) as i:
                for j in range(2):
                    pool.wait_ge(pv_done, i * 2 + j + 1)
                    stage(i * 2 + 2 + j, j)
            load_col = FW + 3 * NA
            for j in range(2):
                load_bin(load_col + j * D, j)
            with pool.Fori(0, 3) as i:
                for j in range(2):
                    pool.wait_ge(gate_pre, i * 2 + j + 1)
                    load_bin(i * COL + COL + load_col + j * D, j)
            pool.wait_ge(unit_used, U_OUT)
            for s in range(NS):
                pool.dma_start(x1[:, s], x_v[s]).then_inc(x1_in, 16)
            nc.gpsimd.memset(ysum[:], 0.0).then_inc(y_zero, 1)
            pool.wait_ge(unit_used, U_MOE)
            pool.dma_start(gfin[:], final_g.partition_broadcast(P)
                           ).then_inc(gfin_in, 16)
            pool.wait_ge(skew_out, 16)

        @block.tensor
        def _(pe):
            def unit(n0, u, products):
                pe.wait_ge(lo_ready, n0 + u + 1)
                for t in range(UNIT_K):
                    last = products(t, w_hi[:, u % AHEAD, t], w_lo[:, u % AHEAD, t])
                last.then_inc(unit_used, 1)
                return last

            def ada_chunk(n0, u0, chunk):
                pe.wait_ge(ada_evac, chunk + ONE)
                for u in range(CHUNK_UNITS):
                    def products(t, wh, wl):
                        k = UNIT_K * u + t
                        lhs = cvec[:, 4 * k:4 * k + P]
                        nc.tensor.matmul(adaP[:], lhs, wh, start=k == 0, stop=False)
                        return nc.tensor.matmul(adaP[:], lhs, wl, start=False, stop=k == KD - 1)
                    unit(n0, u0 + u, products)

            def split_units(n0, u0, units, hi, lo, banks, k_all, k0=0, done=None):
                for u in range(units):
                    def products(t, wh, wl):
                        k = UNIT_K * u + t
                        for s in range(NS):
                            o = bank[banks[s]][:]
                            nc.tensor.matmul(o, hi[:, k0 + k, s], wh, start=k == 0, stop=False)
                            nc.tensor.matmul(o, hi[:, k0 + k, s], wl, start=False, stop=False)
                            last = nc.tensor.matmul(o, lo[:, k0 + k, s], wh, start=False, stop=k == k_all - 1)
                        return last
                    unit(n0, u0 + u, products)

            for starts_at_one in (modT_done, mT_done):
                pe.sem_inc(starts_at_one, ONE)
            pe.wait_ge(consts_in, 16)
            pe.wait_ge(rows_in, 16 * 4)
            nc.tensor.transpose(bank[0][:, 0:6 * KD], vecrows[:], ident[0:6 * KD, 0:6 * KD]).then_inc(vecT_done, 1)
            pe.wait_ge(cvec_ready, 1)

            def modT(n):
                pe.wait_ge(modrow_ready, n + 1)
                pe.wait_ge(modT_evac, n + ONE)
                for b in range(COL // P):
                    last = nc.tensor.matmul(modP[:, b * NS:(b + 1) * NS], modrow[0:4, b * P:(b + 1) * P],
                                            cst_all[0:4, C_SEL:C_SEL + NS], start=True, stop=True)
                last.then_inc(modT_done, 1)

            with pe.Fori(0, 8) as i:
                ada_chunk(i * CHUNK_UNITS, 0, i)
                modT(i)

            def norm_transposes(x, n):
                pe.wait_ge(diag_ready, n)
                for b in range(8):
                    s, g = b % NS, b // NS
                    for j in range(4):
                        k = 4 * g + j
                        last = nc.tensor.matmul(bank[b][:, j * P:(j + 1) * P], x[:, s, k * P:(k + 1) * P],
                                                diag[:, s], start=True, stop=True)
                    last.then_inc(norm_done, 1)

            pe.wait_ge(ada_evac, 8 + ONE)
            pe.wait_ge(modT_evac, 8 + ONE)
            pe.wait_ge(vecT_ready, 1)
            norm_transposes(x0, 1)
            pe.wait_ge(h_ready, 8)
            with pe.Fori(0, 4) as i:
                n0 = i * (4 * CHUNK_UNITS) + U_PROJ
                for j in range(2):
                    ada_chunk(n0, 2 * j * CHUNK_UNITS, i * 2 + 8 + j)
                    pe.wait_ge(proj_evac, i * 2 + j - j + ONE)
                    split_units(n0, (2 * j + 1) * CHUNK_UNITS, CHUNK_UNITS, h_hi, h_lo, (2 * j, 2 * j + 1), KD)
                modT(i + 8)
            pe.wait_ge(proj_evac, 8 + ONE)
            pe.wait_ge(ada_evac, 16 + ONE)
            pe.wait_ge(modT_evac, 12 + ONE)
            for b in range(8):
                for s in range(NS):
                    last = nc.tensor.matmul(bank[b][:, s * 256:(s + 1) * 256], uqkv[:, s, b * P:(b + 1) * P],
                                            dftn, start=True, stop=True)
                last.then_inc(dft1_done, 1)
            pe.wait_ge(dft1_act, 4)
            pe.wait_ge(dft1_dve, 4)
            for o in range(4):
                hh, gp = o % 2, o // 2
                for n in range(4):
                    half, cs = n // 2, n % 2
                    last = nc.tensor.matmul(bank[o][:], dftc[:, half, cs, hh * P:(hh + 1) * P],
                                            fa[:, half, cs, 2 * gp:2 * gp + 2], start=n == 0, stop=n == 3)
                last.then_inc(dft2_done, 1)
            pe.wait_ge(dft2_lo, 4)
            with pe.Fori(0, 4) as i:
                n0 = i * (2 * CHUNK_UNITS) + U_ATT
                for j in range(2):
                    h = i * 2 + j
                    pe.wait_ge(ada_evac, i * 2 + 16 + j + ONE)
                    for u in range(CHUNK_UNITS):
                        if u == 0:
                            pe.wait_ge(head_staged, h + 1)
                            pe.wait_ge(ctx_landed[j], (i + 1) * 32)
                            for n in range(4):
                                nc.tensor.transpose(bank[0][:, n * P:(n + 1) * P], st[:, j, n // 2, n % 2], ident)
                            nc.tensor.transpose(bank[1][:, 0:P], cst[:, j, 0], ident).then_inc(qk_done, 1)
                        if u == 2:
                            pe.wait_ge(qkT_ready, h + 1)
                            pe.wait_ge(kcT_ready, h + 1)
                            nc.tensor.matmul(bank[2][:, 0:P], qkT[:, 0], qkT[:, 1], start=True, stop=True)
                            nc.tensor.matmul(bank[2][:, P:2 * P], qkT[:, 2], kcT[:], start=True, stop=True)
                            nc.tensor.matmul(bank[2][:, 2 * P:3 * P], qkT[:, 2], qkT[:, 3],
                                             start=True, stop=True).then_inc(scores_done, 1)
                        if u == 5:
                            pe.wait_ge(probs_ready, h + 1)
                            for n in range(3):
                                last = nc.tensor.transpose(bank[3][:, n * P:(n + 1) * P], prb[:, n], ident)
                            last.then_inc(prT_done, 1)
                        if u == 7:
                            pe.wait_ge(prT_ready, h + 1)
                            pe.wait_ge(o_ready, h + ONE)
                            nc.tensor.matmul(bank[4][:, 0:P], st[:, j, 0, 2], prT[:, 0], start=True, stop=True)
                            nc.tensor.matmul(bank[4][:, P:2 * P], cst[:, j, 1], prT[:, 1], start=True, stop=False)
                            nc.tensor.matmul(bank[4][:, P:2 * P], st[:, j, 1, 2], prT[:, 2],
                                             start=False, stop=True).then_inc(pv_done, 1)

                        def products(t, wh, wl):
                            k = UNIT_K * u + t
                            lhs = cvec[:, 4 * k:4 * k + P]
                            nc.tensor.matmul(adaP[:], lhs, wh, start=k == 0, stop=False)
                            return nc.tensor.matmul(adaP[:], lhs, wl, start=False, stop=k == KD - 1)
                        unit(n0, j * CHUNK_UNITS + u, products)
                    if j == 0:
                        modT(i + 12)
            pe.wait_ge(o_ready, HEADS + ONE)
            pe.wait_ge(ada_evac, 24 + ONE)
            pe.wait_ge(modT_evac, 16 + ONE)
            with pe.Fori(0, 4) as i:
                n0 = i * 24 + U_MERGE
                split_units(n0, 0, 8, h_hi, h_lo, (0, 1), KD)
                split_units(n0, 8, 8, h_hi, h_lo, (2, 3), KD)
                pe.wait_ge(m_ready, i * 2 + ONE)
                split_units(n0, 16, 4, f_hi, f_lo, (4, 5), KF)
                split_units(n0, 20, 4, o_hi, o_lo, (6, 7), KF)
                pe.wait_ge(merged_ready, i + 1)
                for s in range(NS):
                    for b in range(4):
                        last = nc.tensor.transpose(bank[4 + s][:, b * P:(b + 1) * P],
                                                   ma[:, s, b * P:(b + 1) * P], ident)
                    last.then_inc(mT_done, 1)
            pe.wait_ge(m_ready, 8 + ONE)
            with pe.Fori(0, 2) as i:
                for j in range(2):
                    n0 = i * 16 + U_OUT
                    pe.wait_ge(x1_ready, i * 2 + j - j + ONE)
                    for s in range(NS):
                        nc.tensor.matmul(bank[4 * j + 2 + s][:], cst_all[0:5, C_SELB + s * P:C_SELB + (s + 1) * P],
                                         garow[0:5, bass.ds(i * (2 * COL) + j * COL, COL)], start=True, stop=True)
                    split_units(n0, 8 * j, 8, m_hi, m_lo, (4 * j, 4 * j + 1), KD)
            pe.wait_ge(x1_ready, 4 + ONE)
            norm_transposes(x1, 2)
            pe.wait_ge(h_ready, 16)
            pe.wait_ge(wrs_ready, 1)
            for s in range(NS):
                for k in range(KD):
                    for part in (h_hi, h_lo):
                        last = nc.tensor.matmul(bank[s][:, 0:2 * (NG + NE)], part[:, k, s], wrs[:, k],
                                                start=k == 0 and part is h_hi, stop=k == KD - 1 and part is h_lo)
            last.then_inc(route_done, 1)
            pe.wait_ge(comb_ready, 1)
            with pe.Fori(0, NE) as e:
                n0 = e * 24 + U_MOE
                pe.wait_ge(y_added, e * 4 + ONE)
                split_units(n0, 0, 8, h_hi, h_lo, (0, 1), KD)
                split_units(n0, 8, 8, h_hi, h_lo, (2, 3), KD)
                pe.wait_ge(hid_ready, e + 1)
                for s in range(NS):
                    for b in range(KE):
                        last = nc.tensor.transpose(bank[4 + s][:, b * P:(b + 1) * P],
                                                   hid[:, s, b * P:(b + 1) * P], ident)
                    last.then_inc(hidT_done, 1)
                pe.wait_ge(hid_lo_ready, (e + 1) * 2)
                for n in range(4):
                    if n >= 2:
                        pe.wait_ge(y_added, e * 4 + n - 1 + ONE)
                    split_units(n0, 16 + 2 * n, 2, hid_hi, hid_lo, (6, 7) if n % 2 == 0 else (0, 1), KE)
            pe.wait_ge(y_added, NE * 4 + ONE)
            for n in range(D // COL):
                for s in range(NS):
                    nc.tensor.matmul(bank[NS * n + s][:], cst_all[32:37, C_SELB + s * P:C_SELB + (s + 1) * P],
                                     garow[32:37, n * COL:(n + 1) * COL], start=True, stop=True).then_inc(ga2_done, 1)

        @block.scalar
        def _(act):
            step = Tally(act, act_step)
            act.sem_inc(ada_evac, ONE)

            def high(n0, u, wait=True):
                if u % 2 == 0:
                    slot = (u // 2) % RAW
                    act.wait_ge(raw_landed[slot], landed(n0, u))
                if wait:
                    act.wait_ge(unit_used, n0 + u - AHEAD + 1)
                r = raw[:, (u // 2) % RAW, (u % 2) * UNIT_K:(u % 2) * UNIT_K + UNIT_K]
                nc.scalar.activation(w_hi[:, u % AHEAD], r, ACT.Copy).then_inc(hi_ready, 1)

            def landed(n0, u):
                return n0 * 2 + 16 * (u // (2 * RAW) + 1)

            for s in range(NS):
                act.dma_start(ccol[:, s], (c_ctx, c)[s].rearrange("(p k) -> p k", k=KD) if s == 0
                              else c.rearrange("a (p k) -> p (a k)", k=KD)).then_inc(cond_in, 16)
            for s in range(NS):
                act.dma_start(x0[:, s], x_v[s]).then_inc(x_in, 16)
            for n, src in enumerate((b_ada[0, 0:2 * D], b_ada[0, 3 * D:5 * D])):
                act.dma_start(vecrows[2 * KD * n:2 * KD * (n + 1)], src.rearrange("(r c) -> r c", c=P)
                              ).then_inc(rows_in, 16)
            for n, src in enumerate((norm1_g, norm2_g)):
                act.dma_start(vecrows[(4 + n) * KD:(5 + n) * KD], src.rearrange("l (r c) -> (l r) c", c=P)
                              ).then_inc(rows_in, 16)
            act.dma_start(garow[4:5], b_ada[0:1, 2 * D:3 * D]).then_inc(x_in, 16)
            act.dma_start(garow[36:37], b_ada[0:1, 5 * D:6 * D]).then_inc(x_in, 16)
            act.wait_ge(cond_in, 32)
            nc.scalar.activation(csilu[:], ccol[:], ACT.Silu).then_inc(csilu_ready, 1)

            def root(col, n):
                act.wait_ge(var_ready, n)
                nc.scalar.activation(rms[:, col + 2:col + 4], rms[:, col:col + 2], ACT.Sqrt).then_inc(root_ready, 1)

            def sum_squares(x, col, n):
                for s in range(NS):
                    ins = nc.scalar.activation(squares[:], x[:, s], ACT.Square, accum_out=rms[:, col + s:col + s + 1])
                    if s == 0:
                        step.mark(ins)
                        step.settle()
                ins.then_inc(squares_done, 1)
                root(col, n)

            for u in range(AHEAD):
                high(0, u, wait=False)
            act.wait_ge(x_in, 64)
            sum_squares(x0, 0, 1)

            def evac_mod_rows(end, n):
                act.wait_ge(unit_used, end)
                act.wait_ge(modT_done, n + ONE)
                nc.scalar.activation(modrow[0:4], adaP[0:4, :], ACT.Copy).then_inc(modrow_ready, 1)
                act.wait_ge(modrow_ready, n + 1)
                act.sem_inc(ada_evac, 1)

            def evac_gate_rows(end, row, col):
                act.wait_ge(unit_used, end)
                nc.scalar.activation(garow[row:row + 4, bass.ds(col, COL)], adaP[0:4, :], ACT.Copy
                                     ).then_inc(ada_evac, 1)

            with act.Fori(0, 8) as i:
                for u in range(CHUNK_UNITS):
                    high(i * CHUNK_UNITS, u + AHEAD)
                evac_mod_rows(i * CHUNK_UNITS + CHUNK_UNITS, i)

            def apply_norm(g, sh, n):
                act.wait_ge(mod_ready, n)
                for b in range(8):
                    s, kg = b % NS, b // NS
                    act.wait_ge(norm_done, 8 * (n - 1) + b + 1)
                    if b >= 2:
                        act.wait_ge(h_ready, 8 * (n - 1) + b - 1)
                    for j in range(4):
                        k = 4 * kg + j
                        ins = nc.scalar.activation(htmp[:, b % 2, j], bank[b][:, j * P:(j + 1) * P], ACT.Identity,
                                                   bias=mod[:, sh, k, s:s + 1], scale=mod[:, g, k, s:s + 1])
                    ins.then_inc(htmp_ready, 1)

            apply_norm(1, 0, 1)
            with act.Fori(0, 4) as i:
                n0 = i * (4 * CHUNK_UNITS) + U_PROJ
                for q in range(4):
                    for u in range(CHUNK_UNITS):
                        high(n0, q * CHUNK_UNITS + u + AHEAD)
                    if q == 0:
                        evac_gate_rows(n0 + CHUNK_UNITS, 0, i * COL)
                    if q == 2:
                        evac_mod_rows(n0 + 3 * CHUNK_UNITS, i + 8)
            for b in range(0, 8, 2):
                act.wait_ge(dft1_done, b + 1)
                nc.scalar.activation(fa[:, b % 2, :, b // 2].rearrange("p c s t -> p s c t"),
                                     bank[b][:].rearrange("p (s c t) -> p s c t", s=2, c=2), ACT.Copy
                                     ).then_inc(dft1_act, 1)
            for o in range(4):
                hh, gp = o % 2, o // 2
                act.wait_ge(dft2_done, o + 1)
                nc.scalar.activation(f_hi[:, 4 * gp + hh:4 * gp + hh + 3:2], bank[o][:].rearrange("p (g s t) -> p g s t", g=2, s=2),
                                     ACT.Copy).then_inc(dft2_hi, 1)
            with act.Fori(0, 4) as i:
                n0 = i * (2 * CHUNK_UNITS) + U_ATT
                for j in range(2):
                    h = i * 2 + j
                    for u in range(CHUNK_UNITS):
                        high(n0, j * CHUNK_UNITS + u + AHEAD)
                        if u == 0:
                            act.wait_ge(qk_done, h + 1)
                            nc.scalar.activation(qkT[:].rearrange("p c t -> p (c t)"), bank[0][:], ACT.Copy).then_inc(qkT_ready, 1)
                        if u == 3:
                            act.wait_ge(scores_ready, h + 1)
                            nc.scalar.activation(prb[:, 0], scr[:, 0], ACT.Exp, bias=smx[:, 0:1],
                                                 accum_out=smx[:, 2:3])
                            nc.scalar.activation(prb[:, 1:3], scr[:, 1:3], ACT.Exp, bias=smx[:, 1:2],
                                                 accum_out=smx[:, 3:4]).then_inc(exp_done, 1)
                        if u == 5:
                            act.wait_ge(prT_done, h + 1)
                            nc.scalar.activation(prT[:].rearrange("p c t -> p (c t)"), bank[3][:, 0:3 * P], ACT.Copy).then_inc(prT_ready, 1)
                        if u == 7:
                            act.wait_ge(pv_done, h + 1)
                            nc.scalar.activation(o_hi[:, bass.ds(h, 1)],
                                                 bank[4][:, 0:2 * P].rearrange("p (a s t) -> p a s t", a=1, s=2), ACT.Copy
                                                 ).then_inc(o_hi_ready, 1)
                    if j == 0:
                        evac_mod_rows(n0 + CHUNK_UNITS, i + 12)
                    else:
                        evac_gate_rows(n0 + 2 * CHUNK_UNITS, 32, i * COL)
            act.wait_ge(kv_sent, 32)
            with act.Fori(0, 4) as i:
                n0 = i * 24 + U_MERGE
                for u in range(24):
                    high(n0, u + AHEAD)
                    if u in (8, 16):
                        g = ma if u == 8 else mb
                        act.wait_ge(gate_pre, i * 2 + u // 8)
                        nc.scalar.activation(g[:], g[:], ACT.Sigmoid).then_inc(gate_sig, 1)
                for s in range(NS):
                    act.wait_ge(mT_done, i * 2 + s + 1 + ONE)
                    nc.scalar.activation(m_hi[:, bass.ds(i * 4, 4), s], bank[4 + s][:].rearrange("p (k t) -> p k t", k=4),
                                         ACT.Copy).then_inc(m_hi_ready, 1)
            with act.Fori(0, 2) as i:
                for j in range(2):
                    n0 = i * 16 + U_OUT
                    for u in range(CHUNK_UNITS):
                        high(n0, 8 * j + u + AHEAD)
                    act.wait_ge(unit_used, n0 + 8 * j + 8)
                    for s in range(NS):
                        ins = nc.scalar.activation(gab[:, j, s], bank[4 * j + 2 + s][:], ACT.Copy)
                    ins.then_inc(gab_ready, 1)
            act.wait_ge(x1_ready, 4 + ONE)
            sum_squares(x1, 4, 2)
            apply_norm(3, 2, 2)

            for n in range(2 * NS):
                act.wait_ge(route_arg, n + 1)
                nc.scalar.activation(rt[:, 16:20], rt[:, 12:16], ACT.Exp).then_inc(route_exp, 1)

            def expert(e, ahead):
                n0 = e * 24 + U_MOE
                for u in range(24):
                    if u < ahead:
                        high(n0, u + AHEAD)
                    if u == 7:
                        act.wait_ge(unit_used, n0 + 8)
                        for s in range(NS):
                            ins = nc.scalar.activation(sg[:, s], bank[s][:], ACT.Silu)
                        ins.then_inc(silu_ready, 1)
                    if u == 15:
                        for s in range(NS):
                            act.wait_ge(hidT_done, e * 2 + s + 1)
                            nc.scalar.activation(hid_hi[:, :, s], bank[4 + s][:].rearrange("p (k t) -> p k t", k=KE),
                                                 ACT.Copy).then_inc(hid_hi_ready, 1)

            with act.Fori(0, NE - 1) as e:
                expert(e, 24)
            expert(NE - 1, 24 - AHEAD)
            root(8, 3)

        @block.vector
        def _(dve):
            step = Tally(dve, dve_step)
            for starts_at_one in (modT_evac, proj_evac, m_ready, x1_ready, o_ready, y_added):
                dve.sem_inc(starts_at_one, ONE)
            v = nc.vector

            def low(n0, u):
                dve.wait_ge(hi_ready, n0 + u + 1)
                r = raw[:, (u // 2) % RAW, (u % 2) * UNIT_K:(u % 2) * UNIT_K + UNIT_K]
                v.tensor_tensor(w_lo[:, u % AHEAD], r, w_hi[:, u % AHEAD].bitcast(F32), ALU.subtract
                                ).then_inc(lo_ready, 1)

            def chained(ins):
                step.mark(ins)
                step.settle()

            chained(v.memset(cvec[:].bitcast(F32), 0.0))
            dve.wait_ge(csilu_ready, 1)
            parts = cvec[:, 0:4 * KD].rearrange("p (k c) -> p c k", c=4)
            chained(v.tensor_copy(parts[:, 0:2], csilu[:]))
            v.tensor_tensor(parts[:, 2:4], csilu[:], parts[:, 0:2].bitcast(F32), ALU.subtract).then_inc(cvec_ready, 1)
            for u in range(AHEAD):
                low(0, u)
            dve.wait_ge(vecT_done, 1)
            v.tensor_copy(vecT[:].rearrange("p v k -> p (v k)"), bank[0][:, 0:6 * KD]).then_inc(vecT_ready, 1)

            def inverse_rms(col, n):
                dve.wait_ge(squares_done, n)
                var, y, t = rms[:, col:col + 2], rms[:, col + 2:col + 4], rms[:, 12:14]
                v.tensor_scalar(var, var, 1.0 / D, EPS, ALU.mult, ALU.add).then_inc(var_ready, 1)
                dve.wait_ge(root_ready, n)
                chained(v.reciprocal(y, y))
                chained(v.tensor_tensor(t, y, y, ALU.mult))
                chained(v.tensor_tensor(t, t, var, ALU.mult))
                chained(v.tensor_scalar(t, t, -0.5, 1.5, ALU.mult, ALU.add))
                chained(v.tensor_tensor(y, y, t, ALU.mult))

            dve.wait_ge(consts_in, 16)
            inverse_rms(0, 1)
            for s in range(NS):
                chained(v.tensor_scalar(diag[:, s], ident, rms[:, 2 + s:3 + s], None, ALU.mult))
            dve.sem_inc(diag_ready, 1)
            dve.wait_ge(bias_in, 16 * ROWS * ROWS)
            for h in range(HEADS):
                b = bias[:, h].rearrange("p r c -> p (r c)")
                ins = v.tensor_tensor(b, b, mask, ALU.add)
            chained(ins)
            dve.wait_ge(router_in, 64)
            chained(v.tensor_copy(wrs[:, :, 0], wr[:]))
            v.tensor_tensor(wrs[:, :, 1], wr[:], wrs[:, :, 0].bitcast(F32), ALU.subtract).then_inc(wrs_ready, 1)

            def evac_modT(n):
                dve.wait_ge(modT_done, n + 1 + ONE)
                v.tensor_copy(modf[:, bass.ds(n * 4, 4)], modP[:, 0:4 * NS].rearrange("p (k s) -> p k s", s=NS)
                              ).then_inc(modT_evac, 1)

            modf = mod[:].rearrange("p v k s -> p (v k) s")

            def finish_mods(shift, scale, g, n):
                for s in range(NS):
                    v.tensor_tensor(mod[:, shift, :, s], mod[:, shift, :, s], vecT[:, shift], ALU.add)
                    chained(v.tensor_tensor(mod[:, scale, :, s], mod[:, scale, :, s], vecT[:, scale], ALU.add))
                    chained(v.scalar_tensor_tensor(out=mod[:, scale, :, s], in0=mod[:, scale, :, s], scalar=1.0,
                                                   in1=vecT[:, g], op0=ALU.add, op1=ALU.mult))
                dve.sem_inc(mod_ready, 1)

            with dve.Fori(0, 8) as i:
                for u in range(CHUNK_UNITS):
                    low(i * CHUNK_UNITS, u + AHEAD)
                evac_modT(i)
            dve.wait_ge(modT_evac, 8 + ONE)
            finish_mods(0, 1, 4, 1)

            def split_h(n):
                for b in range(8):
                    s, kg = b % NS, b // NS
                    dve.wait_ge(htmp_ready, 8 * (n - 1) + b + 1)
                    hi = h_hi[:, 4 * kg:4 * kg + 4, s]
                    chained(v.tensor_copy(hi, htmp[:, b % 2]))
                    v.tensor_tensor(h_lo[:, 4 * kg:4 * kg + 4, s], htmp[:, b % 2], hi.bitcast(F32), ALU.subtract
                                    ).then_inc(h_ready, 1)

            split_h(1)
            with dve.Fori(0, 4) as i:
                n0 = i * (4 * CHUNK_UNITS) + U_PROJ
                for q in range(4):
                    for u in range(CHUNK_UNITS):
                        low(n0, q * CHUNK_UNITS + u + AHEAD)
                    if q % 2:
                        j = q // 2
                        dve.wait_ge(unit_used, n0 + (q + 1) * CHUNK_UNITS)
                        dve.wait_ge(bin_landed[j], i * 16 + 16)
                        for s in range(NS):
                            ins = v.tensor_tensor(uqkv[:, s, bass.ds(i * (2 * COL) + j * COL, COL)], bank[2 * j + s][:],
                                                  bin_[:, j], ALU.add)
                        ins.then_inc(proj_evac, 1)
                evac_modT(i + 8)
            for b in range(1, 8, 2):
                dve.wait_ge(dft1_done, b + 1)
                v.tensor_copy(fa[:, b % 2, :, b // 2].rearrange("p c s t -> p s c t"),
                              bank[b][:].rearrange("p (s c t) -> p s c t", s=2, c=2)).then_inc(dft1_dve, 1)
            for o in range(4):
                hh, gp = o % 2, o // 2
                dve.wait_ge(dft2_hi, o + 1)
                sl = slice(4 * gp + hh, 4 * gp + hh + 3, 2)
                v.tensor_tensor(f_lo[:, sl], bank[o][:].rearrange("p (g s t) -> p g s t", g=2, s=2),
                                f_hi[:, sl].bitcast(F32), ALU.subtract).then_inc(dft2_lo, 1)
            with dve.Fori(0, 4) as i:
                step.enter(i, 2 * 7)
                n0 = i * (2 * CHUNK_UNITS) + U_ATT
                for j in range(2):
                    h = i * 2 + j
                    for u in range(CHUNK_UNITS):
                        low(n0, j * CHUNK_UNITS + u + AHEAD)
                        if u == 0:
                            dve.wait_ge(qk_done, h + 1)
                            v.tensor_copy(kcT[:], bank[1][:, 0:P]).then_inc(kcT_ready, 1)
                        if u == 2:
                            dve.wait_ge(scores_done, h + 1)
                            chained(v.tensor_scalar(scr[:, 0:2], bank[2][:, 0:2 * P].rearrange("p (c t) -> p c t", c=2), SCALE, None, ALU.mult))
                            chained(v.scalar_tensor_tensor(
                                out=scr[:, 2], in0=bank[2][:, 2 * P:3 * P], scalar=SCALE,
                                in1=bias[:, bass.ds(h, 1)].rearrange("p h r c -> p (h r c)"), op0=ALU.mult, op1=ALU.add))
                            chained(v.tensor_reduce(smx[:, 0:1], scr[:, 0], X, ALU.max, negate=True))
                            chained(v.tensor_reduce(smx[:, 1:2], scr[:, 1:3].rearrange("p a t -> p (a t)"), X, ALU.max,
                                                    negate=True))
                            dve.sem_inc(scores_ready, 1)
                        if u == 4:
                            dve.wait_ge(exp_done, h + 1)
                            chained(v.reciprocal(smx[:, 4:6], smx[:, 2:4]))
                            chained(v.tensor_scalar(prb[:, 0], prb[:, 0], smx[:, 4:5], None, ALU.mult))
                            chained(v.tensor_scalar(prb[:, 1:3], prb[:, 1:3], smx[:, 5:6], None, ALU.mult))
                            dve.sem_inc(probs_ready, 1)
                        if u == 7:
                            dve.wait_ge(o_hi_ready, h + 1)
                            v.tensor_tensor(o_lo[:, bass.ds(h, 1)], bank[4][:, 0:2 * P].rearrange("p (a s t) -> p a s t", a=1, s=2),
                                            o_hi[:, bass.ds(h, 1)].bitcast(F32), ALU.subtract).then_inc(o_ready, 1)
                    if j == 0:
                        evac_modT(i + 12)
            step.leave(4)
            dve.wait_ge(modT_evac, 16 + ONE)
            finish_mods(2, 3, 5, 2)
            with dve.Fori(0, 4) as i:
                step.enter(i, 2)
                n0 = i * 24 + U_MERGE
                for u in range(24):
                    low(n0, u + AHEAD)
                    if u in (7, 15):
                        j = u // 8
                        g = (ma, mb)[j]
                        dve.wait_ge(unit_used, n0 + u + 1)
                        dve.wait_ge(bin_landed[j], i * 16 + 16 * 5)
                        if j == 0:
                            dve.wait_ge(mT_done, i * 2 + ONE)
                        for s in range(NS):
                            ins = v.tensor_tensor(g[:, s], bank[2 * j + s][:], bin_[:, j], ALU.add)
                        ins.then_inc(gate_pre, 1)
                    if u in (19, 23):
                        j = u // 23
                        g = (ma, mb)[j]
                        dve.wait_ge(unit_used, n0 + u + 1)
                        dve.wait_ge(gate_sig, i * 2 + j + 1)
                        for s in range(NS):
                            ins = v.tensor_tensor(g[:, s], g[:, s], bank[4 + 2 * j + s][:], ALU.mult)
                        chained(ins)
                v.tensor_tensor(ma[:], ma[:], mb[:], ALU.add).then_inc(merged_ready, 1)
                for s in range(NS):
                    dve.wait_ge(m_hi_ready, i * 2 + s + 1)
                    v.tensor_tensor(m_lo[:, bass.ds(i * 4, 4), s], bank[4 + s][:].rearrange("p (k t) -> p k t", k=4),
                                    m_hi[:, bass.ds(i * 4, 4), s].bitcast(F32), ALU.subtract).then_inc(m_ready, 1)
            step.leave(4)
            dve.wait_ge(x1_in, 32)
            with dve.Fori(0, 2) as i:
                step.enter(i, 2)
                for j in range(2):
                    n0 = i * 16 + U_OUT
                    for u in range(CHUNK_UNITS):
                        low(n0, 8 * j + u + AHEAD)
                    dve.wait_ge(unit_used, n0 + 8 * j + 8)
                    dve.wait_ge(gab_ready, i * 2 + j + 1)
                    for s in range(NS):
                        ins = v.tensor_tensor(t2[:, j, s], gab[:, j, s], bank[4 * j + s][:], ALU.mult)
                    chained(ins)
                    xs = x1[:, :, bass.ds(i * (2 * COL) + j * COL, COL)]
                    v.tensor_tensor(xs, xs, t2[:, j], ALU.add).then_inc(x1_ready, 1)
            step.leave(2)
            inverse_rms(4, 2)
            for s in range(NS):
                chained(v.tensor_scalar(diag[:, s], ident, rms[:, 6 + s:7 + s], None, ALU.mult))
            dve.sem_inc(diag_ready, 1)
            split_h(2)

            def exponential(n):
                dve.sem_inc(route_arg, 1)
                dve.wait_ge(route_exp, n + 1)

            dve.wait_ge(route_done, 1)
            for s in range(NS):
                chained(v.tensor_tensor(lg[:, s], bank[s][:, 0:NG + NE], br[:], ALU.add))
                chained(v.tensor_tensor(lg[:, s], lg[:, s], bank[s][:, NG + NE:2 * (NG + NE)], ALU.add))
                L = lg[:, s]

                def pick(values, best, one_hot, scratch):
                    chained(v.tensor_reduce(best, values, X, ALU.max))
                    chained(v.scalar_tensor_tensor(out=scratch, in0=values, scalar=best, in1=first,
                                                   op0=ALU.is_equal, op1=ALU.mult))
                    chained(v.tensor_reduce(rt[:, 100:101], scratch, X, ALU.max))
                    chained(v.tensor_scalar(one_hot, scratch, rt[:, 100:101], None, ALU.is_equal))

                pick(L[:, 0:NG], rt[:, 4:5], rt[:, 8:12], rt[:, 104:108])
                chained(v.tensor_scalar(rt[:, 12:16], L[:, 0:NG], rt[:, 4:5], None, ALU.subtract))
                exponential(2 * s)
                chained(v.tensor_reduce(rt[:, 5:6], rt[:, 16:20], X, ALU.add))
                chained(v.reciprocal(rt[:, 6:7], rt[:, 5:6]))
                for g in range(NG):
                    chained(v.tensor_scalar(rt[:, 20 + 4 * g:24 + 4 * g], L[:, NG + 4 * g:NG + 4 * g + 4],
                                            rt[:, 8 + g:9 + g], None, ALU.mult))
                chained(v.tensor_reduce(rt[:, 36:40], rt[:, 20:36].rearrange("p (g e) -> p e g", g=NG), X, ALU.add))
                pick(rt[:, 36:40], rt[:, 40:41], rt[:, 44:48], rt[:, 104:108])
                chained(v.scalar_tensor_tensor(out=rt[:, 48:52], in0=rt[:, 44:48], scalar=-3e38, in1=rt[:, 36:40],
                                               op0=ALU.mult, op1=ALU.add))
                pick(rt[:, 48:52], rt[:, 52:53], rt[:, 56:60], rt[:, 104:108])
                chained(v.tensor_scalar(rt[:, 12:13], rt[:, 52:53], rt[:, 40:41], None, ALU.subtract))
                exponential(2 * s + 1)
                chained(v.tensor_scalar(rt[:, 60:61], rt[:, 16:17], 1.0, None, ALU.add))
                chained(v.reciprocal(rt[:, 61:62], rt[:, 60:61]))
                chained(v.tensor_tensor(rt[:, 62:63], rt[:, 61:62], rt[:, 6:7], ALU.mult))
                chained(v.tensor_tensor(rt[:, 63:64], rt[:, 62:63], rt[:, 16:17], ALU.mult))
                chained(v.tensor_scalar(rt[:, 64:68], rt[:, 44:48], rt[:, 62:63], None, ALU.mult))
                chained(v.scalar_tensor_tensor(out=rt[:, 68:72], in0=rt[:, 56:60], scalar=rt[:, 63:64],
                                               in1=rt[:, 64:68], op0=ALU.mult, op1=ALU.add))
                for g in range(NG):
                    chained(v.tensor_scalar(comb[:, 4 * g:4 * g + 4, s], rt[:, 68:72], rt[:, 8 + g:9 + g], None, ALU.mult))
            dve.sem_inc(comb_ready, 1)
            dve.wait_ge(y_zero, 1)

            def expert(e, ahead):
                n0 = e * 24 + U_MOE
                for u in range(24):
                    if u < ahead:
                        low(n0, u + AHEAD)
                    if u == 15:
                        dve.wait_ge(unit_used, n0 + 16)
                        dve.wait_ge(silu_ready, e + 1)
                        for s in range(NS):
                            ins = v.scalar_tensor_tensor(out=hid[:, s], in0=bank[2 + s][:],
                                                         scalar=comb[:, bass.ds(e, 1), s], in1=sg[:, s],
                                                         op0=ALU.mult, op1=ALU.mult)
                        ins.then_inc(hid_ready, 1)
                        for s in range(NS):
                            dve.wait_ge(hid_hi_ready, e * 2 + s + 1)
                            v.tensor_tensor(hid_lo[:, :, s], bank[4 + s][:].rearrange("p (k t) -> p k t", k=KE),
                                            hid_hi[:, :, s].bitcast(F32), ALU.subtract).then_inc(hid_lo_ready, 1)
                    if u >= 17 and u % 2:
                        n = (u - 17) // 2
                        dve.wait_ge(unit_used, n0 + u + 1)
                        for s in range(NS):
                            ys = ysum[:, s, n * COL:(n + 1) * COL]
                            b = bank[(6 if n % 2 == 0 else 0) + s]
                            ins = v.tensor_tensor(ys, ys, b[:], ALU.add)
                        ins.then_inc(y_added, 1)

            with dve.Fori(0, NE - 1) as e:
                dve.wait_ge(y_added, e * 4 + ONE)
                expert(e, 24)
            dve.wait_ge(y_added, 4 * (NE - 1) + ONE)
            expert(NE - 1, 24 - AHEAD)
            dve.wait_ge(y_added, NE * 4 + ONE)
            for n in range(D // COL):
                for s in range(NS):
                    dve.wait_ge(ga2_done, NS * n + s + 1)
                    cols = slice(n * COL, (n + 1) * COL)
                    chained(v.tensor_tensor(ysum[:, s, cols], ysum[:, s, cols], bank[NS * n + s][:], ALU.mult))
                    chained(v.tensor_tensor(x1[:, s, cols], x1[:, s, cols], ysum[:, s, cols], ALU.add))
            for s in range(NS):
                chained(v.tensor_tensor(ysum[:, s], x1[:, s], x1[:, s], ALU.mult))
                chained(v.tensor_reduce(rms[:, 8 + s:9 + s], ysum[:, s], X, ALU.add))
            dve.sem_inc(squares_done, 1)
            inverse_rms(8, 3)
            dve.wait_ge(gfin_in, 16)
            for n in range(D // COL):
                for s in range(NS):
                    cols = slice(n * COL, (n + 1) * COL)
                    v.scalar_tensor_tensor(out=x1[:, s, cols], in0=x1[:, s, cols], scalar=rms[:, 10 + s:11 + s],
                                           in1=gfin[:, cols], op0=ALU.mult, op1=ALU.mult).then_inc(y_ready, 1)


_INS = ["x_prompt", "x_sample", "cache_k_ctx", "cache_v_ctx", "c", "c_ctx", "norm1_g", "norm2_g", "w_ada", "b_ada",
        "w_in", "b_in", "w_fourier", "w_na_o", "rpb", "w_out", "w_router_group", "b_router_group",
        "w_router_expert", "b_router_expert", "w_exp_gate", "w_exp_up", "w_exp_down", "final_norm_g"]
_OUTS = [(1, TOK, D), (1, TOK, D), (1, 1, TOK, HEADS, HD), (1, 1, TOK, HEADS, HD)]


def kernel(**inputs):
    import concourse.bacc as bacc
    from concourse.bass_utils import run_bass_kernel_spmd

    nc = bacc.Bacc("TRN2", target_bir_lowering=False, num_devices=1)
    arrays, args = {}, []
    for name in _INS:
        a = np.ascontiguousarray(inputs[name])
        arrays[f"in_{name}"] = a
        args.append(nc.dram_tensor(f"in_{name}", a.shape, mybir.dt.from_np(a.dtype), kind="ExternalInput").ap())
    arrays["shape_constants"] = shape_constants()
    args.append(nc.dram_tensor("shape_constants", (P, C_ALL), F32, kind="ExternalInput").ap())
    for i, shape in enumerate(_OUTS):
        args.append(nc.dram_tensor(f"out_{i}", shape, F32, kind="ExternalOutput").ap())
    backbone_step(nc, *args)
    result = run_bass_kernel_spmd(nc, [arrays], core_ids=[0])
    return tuple(result.results[0][f"out_{i}"] for i in range(len(_OUTS)))
```

```python
from contextlib import ExitStack

import numpy as np

import concourse.bass as bass
from concourse import mybir

ALU = mybir.AluOpType
ACT = mybir.ActivationFunctionType
F32 = mybir.dt.float32
F32R = mybir.dt.float32r
X = mybir.AxisListType.X

P = 128
TOK = 128
NS = 2
D = 2048
KD = D // P
COL = 512
HEADS, HD = 8, 128
NA = HEADS * HD
FW, FG, FGD = 1024, 4, 256
KF = FW // P
GRID_W, ROWS, WIN = 64, 2, 16
NG, EPG, NE, EH = 4, 4, 16, 512
KE = EH // P
SCALE = float(HD) ** -0.5
EPS = 1e-6

LOAD_K, UNIT_K = 4, 2
RAW, AHEAD = 4, 4
CHUNK_UNITS = KD // UNIT_K
ONE = 1

C_ID = 0
C_DFTN = C_ID + P
C_DFTC = C_DFTN + 2 * TOK
C_MASK = C_DFTC + 2 * 2 * FGD
C_SEL = C_MASK + TOK
C_SELB = C_SEL + NS
C_FIRST = C_SELB + NS * P
C_ALL = C_FIRST + EPG
R_BEFORE = 0
R_ONES = R_BEFORE + TOK
R_SLOT = R_ONES + TOK
R_SUM = R_SLOT + 2 * 64
R_ALL = R_SUM + 64

CAP, PAIR = 64, 2
PAIRS = NE // PAIR


def shape_constants():
    c = np.zeros((P, C_ALL), np.float64)
    c[:, C_ID:C_ID + P] = np.eye(P)
    n = np.arange(TOK)
    ang = 2 * np.pi * (np.outer(n, n) % TOK) / TOK
    c[:, C_DFTN:C_DFTN + TOK] = np.cos(ang) / np.sqrt(TOK)
    c[:, C_DFTN + TOK:C_DFTC] = np.sin(ang) / np.sqrt(TOK)
    m = np.arange(FGD)
    ang = 2 * np.pi * (np.outer(m, m) % FGD) / FGD
    both = np.stack([np.cos(ang), -np.sin(ang)], 1) / np.sqrt(FGD)
    c[:, C_DFTC:C_MASK] = both.reshape(2, P, 2, FGD).transpose(1, 0, 2, 3).reshape(P, -1)
    col = np.arange(GRID_W)
    start = np.clip(col - WIN // 2, 0, GRID_W - WIN)
    ok = (col[None, :] >= start[:, None]) & (col[None, :] < start[:, None] + WIN)
    c[:, C_MASK:C_SEL] = np.where(np.tile(ok, (ROWS, ROWS)), 0.0, -1e30)
    for r in range(4):
        c[r, C_SEL + r % NS] = 1.0
    for base in (0, 32):
        for r in range(5):
            for s in range(NS):
                if r == 4 or r % NS == s:
                    c[base + r, C_SELB + s * P:C_SELB + (s + 1) * P] = 1.0
    c[:, C_FIRST:C_ALL] = np.arange(EPG, 0, -1)
    return c.astype(np.float32)


def routing_constants():
    c = np.ones((P, R_ALL), np.float32)
    c[:, R_BEFORE:R_ONES] = np.triu(np.ones((TOK, TOK)), 1)
    c[:, R_SLOT:R_SUM] = np.tile(np.arange(CAP), 2)
    c[:, R_SUM:] = np.tile(np.eye(CAP), (2, 1))
    return c


class Tally:

    def __init__(self, engine, sem):
        self.engine, self.sem, self.base, self.n = engine, sem, 0, 0

    def mark(self, instruction):
        instruction.then_inc(self.sem, 1)
        self.n += 1

    def settle(self):
        self.engine.wait_ge(self.sem, self.base + self.n)

    def enter(self, i, per):
        self.start, self.per = self.base + self.n, per
        self.base, self.n = i * per + self.start, 0

    def leave(self, count):
        assert self.n == self.per, (self.n, self.per)
        self.base, self.n = self.start + count * self.per, 0


def backbone_step(nc, x_prompt, x_sample, cache_k, cache_v, c, c_ctx, norm1_g, norm2_g, w_ada, b_ada,
                  w_in, b_in, w_fourier, w_na_o, rpb, w_out, w_rg, b_rg, w_re, b_re, w_gate, w_up,
                  w_down, final_g, constants, routing, y_prompt, y_sample, new_k, new_v):
    ada_v = w_ada.rearrange("l (p k) n -> p (l k) n", k=KD)
    in_v = w_in.rearrange("l (k p) n -> p (l k) n", p=P)
    fo_v = w_fourier.rearrange("l (k p) n -> p (l k) n", p=P)
    na_v = w_na_o.rearrange("l (k p) n -> p (l k) n", p=P)
    out_v = w_out.rearrange("l (k p) n -> p (l k) n", p=P)
    gate_v = w_gate.rearrange("l e (k p) n -> p (l e k) n", p=P)
    up_v = w_up.rearrange("l e (k p) n -> p (l e k) n", p=P)
    down_v = w_down.rearrange("l e (k p) n -> p (l e k) n", p=P)
    rg_v = w_rg.rearrange("l (k p) n -> p (l k) n", p=P)
    re_v = w_re.rearrange("l (k p) n -> p (l k) n", p=P)
    kc_v = cache_k.rearrange("a l t h d -> t (a l h) d")
    vc_v = cache_v.rearrange("a l t h d -> t (a l h) d")
    x_v = [x_prompt.rearrange("a t n -> (a t) n"), x_sample.rearrange("a t n -> (a t) n")]
    y_v = [y_prompt.rearrange("a t n -> (a t) n"), y_sample.rearrange("a t n -> (a t) n")]
    NR = HEADS * 3
    skew = nc.dram_tensor("bias_rows", [GRID_W, NR, P], F32, kind="Internal")

    with ExitStack() as ctx:
        at = [16512]

        def region(size):
            at[0] += size
            return at[0] - size

        def place(name, shape, offset, dt=F32):
            return nc.alloc_sbuf_tensor_at(name, shape, dt, offset=offset).ap()

        def own(name, shape, dt=F32):
            size = 4 * int(np.prod(shape[1:]))
            return place(name, shape, region((size + 31) // 32 * 32), dt)

        def sem(name):
            return ctx.enter_context(nc.semaphore(name))

        KB = 1024
        h_hi = own("h_hi", [P, KD, NS, TOK], F32R)
        h_lo = own("h_lo", [P, KD, NS, TOK], F32R)
        H = 16512
        raw = own("raw", [P, RAW, LOAD_K, COL])
        w_hi = own("w_hi", [P, AHEAD, UNIT_K, COL], F32R)
        w_lo = own("w_lo", [P, AHEAD, UNIT_K, COL], F32R)
        A, F, B = region(32 * KB), region(32 * KB), region(16 * KB)
        x0 = place("x0", [P, NS, D], A)
        uqkv = place("uqkv", [P, NS, FW + 3 * NA], A)
        m_hi = place("m_hi", [P, KD, NS, TOK], A, F32R)
        m_lo = place("m_lo", [P, KD, NS, TOK], A + 16 * KB, F32R)
        t_hi = place("t_hi", [P, NS, D], A, F32R)
        t_lo = place("t_lo", [P, NS, D], A + 16 * KB, F32R)
        f_hi = place("f_hi", [P, KF, NS, TOK], F, F32R)
        f_lo = place("f_lo", [P, KF, NS, TOK], F + 8 * KB, F32R)
        o_hi = place("o_hi", [P, KF, NS, TOK], F + 16 * KB, F32R)
        o_lo = place("o_lo", [P, KF, NS, TOK], F + 24 * KB, F32R)
        x1 = place("x1", [P, NS, D], F)
        ysum = place("ysum", [P, NS, D], F + 16 * KB)
        xg = place("xg", [P, KD, PAIR, 2, CAP], H, F32R)
        hidT = place("hidT", [P, PAIR, KE, 2, CAP], H + 16 * KB, F32R)
        sgT = place("sgT", [P, KE, CAP], H + 20 * KB)
        hidf = place("hidf", [P, KE, CAP], H + 21 * KB)
        gfin = place("gfin", [P, D], H + 24 * KB)
        squares = place("squares", [P, D], B)
        htmp = place("htmp", [P, 2, 4, TOK], B + 8 * KB)
        vecrows = place("vecrows", [6 * KD, P], B + 12 * KB)
        rpbpad = place("rpbpad", [NR, P], B + 12 * KB + 512)
        fa = place("fa", [P, 2, 2, FG, NS, TOK], B)
        st = place("st", [P, 2, NS, 3, HD], B)
        cst = place("cst", [P, 2, 2, HD], B + 6 * KB)
        qkT = place("qkT", [P, 4, TOK], B + 8 * KB)
        kcT = place("kcT", [P, TOK], B + 10 * KB)
        scr = place("scr", [P, 3, TOK], B + 10 * KB + 512)
        prb = place("prb", [P, 3, TOK], B + 12 * KB)
        prT = place("prT", [P, 3, TOK], B + 13 * KB + 512)
        ma = place("ma", [P, NS, COL], B)
        mb = place("mb", [P, NS, COL], B + 4 * KB)
        pick_ = place("pick", [P, NS, PAIR, 2, CAP], B, F32R)
        pickT = place("pickT", [P, PAIR, NS, TOK], B + 2 * KB)
        dsb = place("dsb", [P, PAIR, 2, COL], B + 4 * KB)
        gu = place("gu", [P, 2, EH], B + 12 * KB)
        gab = place("gab", [P, 2, NS, COL], B)
        t2 = place("t2", [P, 2, NS, COL], B + 8 * KB)

        garow = own("garow", [37, D])
        bias = own("bias", [P, HEADS, ROWS, GRID_W])
        C = region((4 * C_ALL + 31) // 32 * 32)
        cst_all = place("cst_all", [P, C_ALL], C)
        cst_route = place("cst_route", [P, R_ALL], C + 4 * C_DFTN)
        bin_ = own("bin", [P, 2, COL])
        modrow = place("modrow", [4, COL], region(COL * 4))
        ccol = own("ccol", [P, NS, KD])
        csilu = own("csilu", [P, NS, KD])
        cvec = own("cvec", [P, 4 * (KD - 1) + P], F32R)
        mod = own("mod", [P, 4, KD, NS])
        vecT = own("vecT", [P, 6, KD])
        rms = own("rms", [P, 16])
        diag = own("diag", [P, NS, P])
        wr = place("wr", [P, KD, NG + NE], B + 13 * KB)
        wrs = own("wrs", [P, KD, 2, NG + NE], F32R)
        br = own("br", [P, NG + NE])
        lg = own("lg", [P, NS, NG + NE])
        rt = own("rt", [P, 160])
        comb = own("comb", [P, NS, NE])
        chosen = own("chosen", [P, NS, NE])
        key = own("key", [P, NS, NE + PAIR])
        slot_w = own("slot_w", [P, PAIR])
        rounds = own("rounds", [P, 1], mybir.dt.int32)
        smx = own("smx", [P, 8])

        ident = cst_all[:, C_ID:C_ID + P]
        dftn = cst_all[:, C_DFTN:C_DFTC]
        dftc = cst_all[:, C_DFTC:C_MASK].rearrange("p (h c n) -> p h c n", h=2, c=2)
        mask = cst_all[:, C_MASK:C_SEL]
        first = cst_all[:, C_FIRST:C_ALL]

        bank = [ctx.enter_context(nc.psum_tensor(f"bank{i}", [P, COL], F32)) for i in range(8)]
        adaP, modP = bank[7], bank[6]

        raw_landed = [sem(f"raw_landed{i}") for i in range(RAW)]
        hi_ready, lo_ready, unit_used = sem("hi_ready"), sem("lo_ready"), sem("unit_used")
        slots_freed = sem("slots_freed")
        consts_in, cond_in, x_in, rows_in, router_in = (
            sem("consts_in"), sem("cond_in"), sem("x_in"), sem("rows_in"), sem("router_in"))
        rpb_in, skew_out, bias_in = sem("rpb_in"), sem("skew_out"), sem("bias_in")
        pad_zero, cvec_ready, csilu_ready = sem("pad_zero"), sem("cvec_ready"), sem("csilu_ready")
        vecT_done, vecT_ready = sem("vecT_done"), sem("vecT_ready")
        squares_done, diag_ready, mod_ready = sem("squares_done"), sem("diag_ready"), sem("mod_ready")
        var_ready, root_ready = sem("var_ready"), sem("root_ready")
        norm_done, htmp_ready, h_ready = sem("norm_done"), sem("htmp_ready"), sem("h_ready")
        ada_evac, modrow_ready, modT_done, modT_evac = (
            sem("ada_evac"), sem("modrow_ready"), sem("modT_done"), sem("modT_evac"))
        bin_landed = [sem("bin_landed0"), sem("bin_landed1")]
        proj_evac = sem("proj_evac")
        dft1_done, dft1_act, dft1_dve = sem("dft1_done"), sem("dft1_act"), sem("dft1_dve")
        dft2_done, dft2_hi, dft2_lo = sem("dft2_done"), sem("dft2_hi"), sem("dft2_lo")
        head_staged = sem("head_staged")
        ctx_landed = [sem("ctx_landed0"), sem("ctx_landed1")]
        qk_done, qkT_ready, kcT_ready = sem("qk_done"), sem("qkT_ready"), sem("kcT_ready")
        scores_done, scores_ready, exp_done, probs_ready = (
            sem("scores_done"), sem("scores_ready"), sem("exp_done"), sem("probs_ready"))
        prT_done, prT_ready, pv_done, o_hi_ready, o_ready = (
            sem("prT_done"), sem("prT_ready"), sem("pv_done"), sem("o_hi_ready"), sem("o_ready"))
        gate_pre, gate_sig, merged_ready = sem("gate_pre"), sem("gate_sig"), sem("merged_ready")
        mT_done, m_hi_ready, m_ready = sem("mT_done"), sem("m_hi_ready"), sem("m_ready")
        x1_in, gab_ready, x1_ready = (
            sem("x1_in"), sem("gab_ready"), sem("x1_ready"))
        wrs_ready, route_done, comb_ready, y_zero = (
            sem("wrs_ready"), sem("route_done"), sem("comb_ready"), sem("y_zero"))
        silu_ready, hid_ready = sem("silu_ready"), sem("hid_ready")
        routing_in, chosen_ready, rank_done, rounds_ready = (
            sem("routing_in"), sem("chosen_ready"), sem("rank_done"), sem("rounds_ready"))
        back_done, back_act, back_dve = sem("back_done"), sem("back_act"), sem("back_dve")
        pick_ready, pickT_done, pickT_ready, slot_w_done, slot_w_ready = (
            sem("pick_ready"), sem("pickT_done"), sem("pickT_ready"), sem("slot_w_done"), sem("slot_w_ready"))
        gather_done, xg_ready, gu_ready, guT_done = (
            sem("gather_done"), sem("xg_ready"), sem("gu_ready"), sem("guT_done"))
        key_moved, rounds_done, tail_step = sem("key_moved"), sem("rounds_done"), sem("tail_step")
        d_ready, scatter_done = sem("d_ready"), sem("scatter_done")
        y_added = sem("y_added")
        route_arg, route_exp = sem("route_arg"), sem("route_exp")
        gfin_in, ga2_done, y_ready, out_sent, kv_sent = (
            sem("gfin_in"), sem("ga2_done"), sem("y_ready"), sem("out_sent"), sem("kv_sent"))
        dve_step, act_step, pool_step = sem("dve_step"), sem("act_step"), sem("pool_step")

        U_ADA1 = 0
        U_PROJ = U_ADA1 + 8 * CHUNK_UNITS
        U_ATT = U_PROJ + 16 * CHUNK_UNITS
        U_MERGE = U_ATT + 8 * CHUNK_UNITS
        U_OUT = U_MERGE + 4 * 24
        U_MOE = U_OUT + 4 * CHUNK_UNITS
        U_PAIR = PAIR * 3 * CHUNK_UNITS
        DOWN = [(0, 0), (0, 1), (1, 0), (1, 1), (0, 2), (0, 3), (1, 2), (1, 3)]

        def round_count(engine):
            engine.wait_ge(rounds_ready, 1)
            return engine.value_load(rounds[0:1, 0:1], min_val=1, max_val=NS * TOK // CAP)

        block = ctx.enter_context(nc.Block())

        @block.sync
        def _(sp):
            def load(view, k0, col, first_load, j, wait=True):
                if wait:
                    sp.wait_ge(lo_ready, 2 * (first_load + j - RAW + 1))
                    sp.sem_inc(slots_freed, 1)
                sp.dma_start(raw[:, j % RAW], view[:, bass.ds(k0, LOAD_K), bass.ds(col, COL)]
                             ).then_inc(raw_landed[j % RAW], 16)

            def chunk(view, tiles, col, first_load, j, k0=0, wait=True):
                for n in range(tiles // LOAD_K):
                    load(view, k0 + LOAD_K * n, col, first_load, j + n, wait)

            chunk(ada_v, KD, 0, 0, 0, wait=False)
            with sp.Fori(1, 8) as i:
                chunk(ada_v, KD, i * COL, i * 4, 0)
            with sp.Fori(0, 4) as i:
                base = i * 16 + U_PROJ // 2
                chunk(ada_v, KD, i * COL + 2 * D, base, 0)
                chunk(in_v, KD, i * (2 * COL), base, 4)
                chunk(ada_v, KD, i * COL + 3 * D, base, 8)
                chunk(in_v, KD, i * (2 * COL) + COL, base, 12)
            with sp.Fori(0, 4) as i:
                base = i * 8 + U_ATT // 2
                chunk(ada_v, KD, i * COL + 4 * D, base, 0)
                chunk(ada_v, KD, i * COL + 5 * D, base, 4)
            with sp.Fori(0, 4) as i:
                base = i * 12 + U_MERGE // 2
                chunk(in_v, KD, i * COL + FW + 3 * NA, base, 0)
                chunk(in_v, KD, i * COL + FW + 3 * NA + D, base, 4)
                chunk(fo_v, KF, i * COL, base, 8)
                chunk(na_v, KF, i * COL, base, 10)
            with sp.Fori(0, 4) as i:
                chunk(out_v, KD, i * COL, i * 4 + U_OUT // 2, 0)
            def pair_load(p, base, n):
                e, n = (p, n) if n < 24 else (p + 1, n - 24)
                if n < 16:
                    view = (gate_v, up_v)[n // 4 % 2]
                    load(view, (e * PAIR + n // 8) * KD + n % 4 * LOAD_K, 0, base, n)
                else:
                    x, col = DOWN[n - 16]
                    load(down_v, (e * PAIR + x) * KE, col * COL, base, n)

            for n in range(2):
                pair_load(0, U_MOE // 2, n)
            with sp.Fori(0, round_count(sp)) as r:
                with sp.Fori(0, PAIRS - 1) as p:
                    for n in range(2, 24):
                        pair_load(p, (r * PAIRS + p) * 24 + U_MOE // 2, n)
                    for n in range(2):
                        pair_load(p + 1, (r * PAIRS + p) * 24 + U_MOE // 2 + 24, n)
                for n in range(2, 24):
                    pair_load(PAIRS - 1, (r * PAIRS + PAIRS - 1) * 24 + U_MOE // 2, n)
                for n in range(2):
                    pair_load(0, (r * PAIRS + PAIRS) * 24 + U_MOE // 2, n)
            for n in range(D // COL):
                for s in range(NS):
                    sp.wait_ge(y_ready, n * NS + s + 1)
                    sp.dma_start(y_v[s][:, n * COL:(n + 1) * COL],
                                 x1[:, s, n * COL:(n + 1) * COL]).then_inc(out_sent, 16)
            sp.wait_ge(out_sent, 16 * NS * (D // COL))
            sp.wait_ge(kv_sent, 32)

        @block.gpsimd
        def _(pool):
            step = Tally(pool, pool_step)
            nc.gpsimd.memset(rpbpad[:], 0.0).then_inc(pad_zero, 1)
            pool.dma_start(cst_all[:], constants).then_inc(consts_in, 16)
            pool.wait_ge(pad_zero, 1)
            for h in range(HEADS):
                pool.dma_start(rpbpad[3 * h:3 * h + 3, 48:48 + 2 * WIN - 1], rpb[0, h, 6:9, :]).then_inc(rpb_in, 16)
            pool.dma_start(wr[:, :, 0:NG], rg_v).then_inc(router_in, 16)
            pool.dma_start(wr[:, :, NG:], re_v).then_inc(router_in, 16)
            pool.dma_start(br[:, 0:NG], b_rg[0].partition_broadcast(P)).then_inc(router_in, 16)
            pool.dma_start(br[:, NG:], b_re[0].partition_broadcast(P)).then_inc(router_in, 16)
            pool.wait_ge(rpb_in, 16 * HEADS)
            sk = skew.ap()
            pool.dma_start(sk.rearrange("c r j -> r c j"),
                           bass.AP(rpbpad.tensor, rpbpad.offset, [list(rpbpad.ap[0]), [0, GRID_W], [1, P]])
                           ).then_inc(skew_out, 16)
            pool.wait_ge(skew_out, 16)
            for r in range(ROWS):
                for kr in range(ROWS):
                    pool.dma_start(bias[r * GRID_W:(r + 1) * GRID_W, :, kr],
                                   bass.AP(sk.tensor, (1 - r + kr) * P + GRID_W - 1,
                                           [[NR * P - 1, GRID_W], [3 * P, HEADS], [1, GRID_W]])
                                   ).then_inc(bias_in, 16)

            def load_bin(col, j):
                pool.dma_start(bin_[:, j], b_in[0, bass.ds(col, COL)].partition_broadcast(P)
                               ).then_inc(bin_landed[j], 16)

            for j in range(2):
                load_bin(j * COL, j)
            with pool.Fori(0, 3) as i:
                for j in range(2):
                    pool.wait_ge(proj_evac, i * 2 + j + 1 + ONE)
                    load_bin(i * (2 * COL) + (2 + j) * COL, j)
            pool.wait_ge(proj_evac, 8 + ONE)
            for n, dst in enumerate((new_k, new_v)):
                pool.dma_start(dst.rearrange("a l t h d -> (a l t) (h d)"),
                               uqkv[:, 0, FW + (1 + n) * NA:FW + (2 + n) * NA]).then_inc(kv_sent, 16)

            heads = uqkv[:].rearrange("p s (c h d) -> p s c h d", c=4, h=HEADS)

            def stage(h, j):
                for s in range(NS):
                    copy = nc.gpsimd.tensor_copy(st[:, j, s].rearrange("p c (a d) -> p c a d", a=1), heads[:, s, 1:4, bass.ds(h, 1), :])
                copy.then_inc(head_staged, 1)
                pool.dma_start(cst[:, j, 0:1], kc_v[:, bass.ds(h, 1), :]).then_inc(ctx_landed[j], 16)
                pool.dma_start(cst[:, j, 1:2], vc_v[:, bass.ds(h, 1), :]).then_inc(ctx_landed[j], 16)

            pool.wait_ge(dft2_done, 4)
            pool.dma_start(cst_route[:], routing).then_inc(routing_in, 16)
            pool.wait_ge(dft2_done, 4)
            for j in range(2):
                stage(j, j)
            with pool.Fori(0, 3) as i:
                for j in range(2):
                    pool.wait_ge(pv_done, i * 2 + j + 1)
                    stage(i * 2 + 2 + j, j)
            load_col = FW + 3 * NA
            for j in range(2):
                load_bin(load_col + j * D, j)
            with pool.Fori(0, 3) as i:
                for j in range(2):
                    pool.wait_ge(gate_pre, i * 2 + j + 1)
                    load_bin(i * COL + COL + load_col + j * D, j)
            pool.wait_ge(unit_used, U_OUT)
            for s in range(NS):
                pool.dma_start(x1[:, s], x_v[s]).then_inc(x1_in, 16)
            nc.gpsimd.memset(ysum[:], 0.0).then_inc(y_zero, 1)
            pool.wait_ge(back_done, 16)
            pool.dma_start(gfin[:], final_g.partition_broadcast(P)).then_inc(gfin_in, 16)
            pool.wait_ge(routing_in, 16)
            pool.wait_ge(skew_out, 16)

        @block.tensor
        def _(pe):
            def unit(n0, u, products):
                pe.wait_ge(lo_ready, n0 + u + 1)
                for t in range(UNIT_K):
                    last = products(t, w_hi[:, u % AHEAD, t], w_lo[:, u % AHEAD, t])
                last.then_inc(unit_used, 1)
                return last

            def ada_chunk(n0, u0, chunk):
                pe.wait_ge(ada_evac, chunk + ONE)
                for u in range(CHUNK_UNITS):
                    def products(t, wh, wl):
                        k = UNIT_K * u + t
                        lhs = cvec[:, 4 * k:4 * k + P]
                        nc.tensor.matmul(adaP[:], lhs, wh, start=k == 0, stop=False)
                        return nc.tensor.matmul(adaP[:], lhs, wl, start=False, stop=k == KD - 1)
                    unit(n0, u0 + u, products)

            def split_units(n0, u0, units, hi, lo, banks, k_all, k0=0, done=None):
                for u in range(units):
                    def products(t, wh, wl):
                        k = UNIT_K * u + t
                        for s in range(NS):
                            o = bank[banks[s]][:]
                            nc.tensor.matmul(o, hi[:, k0 + k, s], wh, start=k == 0, stop=False)
                            nc.tensor.matmul(o, hi[:, k0 + k, s], wl, start=False, stop=False)
                            last = nc.tensor.matmul(o, lo[:, k0 + k, s], wh, start=False, stop=k == k_all - 1)
                        return last
                    unit(n0, u0 + u, products)

            for starts_at_one in (modT_done, mT_done, scatter_done):
                pe.sem_inc(starts_at_one, ONE)
            pe.wait_ge(consts_in, 16)
            pe.wait_ge(rows_in, 16 * 4)
            nc.tensor.transpose(bank[0][:, 0:6 * KD], vecrows[:], ident[0:6 * KD, 0:6 * KD]).then_inc(vecT_done, 1)
            pe.wait_ge(cvec_ready, 1)

            def modT(n):
                pe.wait_ge(modrow_ready, n + 1)
                pe.wait_ge(modT_evac, n + ONE)
                for b in range(COL // P):
                    last = nc.tensor.matmul(modP[:, b * NS:(b + 1) * NS], modrow[0:4, b * P:(b + 1) * P],
                                            cst_all[0:4, C_SEL:C_SEL + NS], start=True, stop=True)
                last.then_inc(modT_done, 1)

            with pe.Fori(0, 8) as i:
                ada_chunk(i * CHUNK_UNITS, 0, i)
                modT(i)

            def norm_transposes(x, n):
                pe.wait_ge(diag_ready, n)
                for b in range(8):
                    s, g = b % NS, b // NS
                    for j in range(4):
                        k = 4 * g + j
                        last = nc.tensor.matmul(bank[b][:, j * P:(j + 1) * P], x[:, s, k * P:(k + 1) * P],
                                                diag[:, s], start=True, stop=True)
                    last.then_inc(norm_done, 1)

            pe.wait_ge(ada_evac, 8 + ONE)
            pe.wait_ge(modT_evac, 8 + ONE)
            pe.wait_ge(vecT_ready, 1)
            norm_transposes(x0, 1)
            pe.wait_ge(h_ready, 8)
            with pe.Fori(0, 4) as i:
                n0 = i * (4 * CHUNK_UNITS) + U_PROJ
                for j in range(2):
                    ada_chunk(n0, 2 * j * CHUNK_UNITS, i * 2 + 8 + j)
                    pe.wait_ge(proj_evac, i * 2 + j - j + ONE)
                    split_units(n0, (2 * j + 1) * CHUNK_UNITS, CHUNK_UNITS, h_hi, h_lo, (2 * j, 2 * j + 1), KD)
                modT(i + 8)
            pe.wait_ge(proj_evac, 8 + ONE)
            pe.wait_ge(ada_evac, 16 + ONE)
            pe.wait_ge(modT_evac, 12 + ONE)
            for b in range(8):
                for s in range(NS):
                    last = nc.tensor.matmul(bank[b][:, s * 256:(s + 1) * 256], uqkv[:, s, b * P:(b + 1) * P],
                                            dftn, start=True, stop=True)
                last.then_inc(dft1_done, 1)
            pe.wait_ge(dft1_act, 4)
            pe.wait_ge(dft1_dve, 4)
            for o in range(4):
                hh, gp = o % 2, o // 2
                for n in range(4):
                    half, cs = n // 2, n % 2
                    last = nc.tensor.matmul(bank[o][:], dftc[:, half, cs, hh * P:(hh + 1) * P],
                                            fa[:, half, cs, 2 * gp:2 * gp + 2], start=n == 0, stop=n == 3)
                last.then_inc(dft2_done, 1)
            pe.wait_ge(dft2_lo, 4)
            with pe.Fori(0, 4) as i:
                n0 = i * (2 * CHUNK_UNITS) + U_ATT
                for j in range(2):
                    h = i * 2 + j
                    pe.wait_ge(ada_evac, i * 2 + 16 + j + ONE)
                    for u in range(CHUNK_UNITS):
                        if u == 1:
                            pe.wait_ge(head_staged, h + 1)
                            pe.wait_ge(ctx_landed[j], (i + 1) * 32)
                            for n in range(4):
                                nc.tensor.transpose(bank[0][:, n * P:(n + 1) * P], st[:, j, n // 2, n % 2], ident)
                            nc.tensor.transpose(bank[1][:, 0:P], cst[:, j, 0], ident).then_inc(qk_done, 1)
                        if u == 3:
                            pe.wait_ge(qkT_ready, h + 1)
                            pe.wait_ge(kcT_ready, h + 1)
                            nc.tensor.matmul(bank[2][:, 0:P], qkT[:, 0], qkT[:, 1], start=True, stop=True)
                            nc.tensor.matmul(bank[2][:, P:2 * P], qkT[:, 2], kcT[:], start=True, stop=True)
                            nc.tensor.matmul(bank[2][:, 2 * P:3 * P], qkT[:, 2], qkT[:, 3],
                                             start=True, stop=True).then_inc(scores_done, 1)
                        if u == 6:
                            pe.wait_ge(probs_ready, h + 1)
                            for n in range(3):
                                last = nc.tensor.transpose(bank[3][:, n * P:(n + 1) * P], prb[:, n], ident)
                            last.then_inc(prT_done, 1)
                        if u == 7:
                            pe.wait_ge(prT_ready, h + 1)
                            pe.wait_ge(o_ready, h + ONE)
                            nc.tensor.matmul(bank[4][:, 0:P], st[:, j, 0, 2], prT[:, 0], start=True, stop=True)
                            nc.tensor.matmul(bank[4][:, P:2 * P], cst[:, j, 1], prT[:, 1], start=True, stop=False)
                            nc.tensor.matmul(bank[4][:, P:2 * P], st[:, j, 1, 2], prT[:, 2],
                                             start=False, stop=True).then_inc(pv_done, 1)

                        def products(t, wh, wl):
                            k = UNIT_K * u + t
                            lhs = cvec[:, 4 * k:4 * k + P]
                            nc.tensor.matmul(adaP[:], lhs, wh, start=k == 0, stop=False)
                            return nc.tensor.matmul(adaP[:], lhs, wl, start=False, stop=k == KD - 1)
                        unit(n0, j * CHUNK_UNITS + u, products)
                    if j == 0:
                        modT(i + 12)
            pe.wait_ge(o_ready, HEADS + ONE)
            pe.wait_ge(ada_evac, 24 + ONE)
            pe.wait_ge(modT_evac, 16 + ONE)
            with pe.Fori(0, 4) as i:
                n0 = i * 24 + U_MERGE
                split_units(n0, 0, 8, h_hi, h_lo, (0, 1), KD)
                split_units(n0, 8, 8, h_hi, h_lo, (2, 3), KD)
                pe.wait_ge(m_ready, i * 2 + ONE)
                split_units(n0, 16, 4, f_hi, f_lo, (4, 5), KF)
                split_units(n0, 20, 4, o_hi, o_lo, (6, 7), KF)
                pe.wait_ge(merged_ready, i + 1)
                for s in range(NS):
                    for b in range(4):
                        last = nc.tensor.transpose(bank[4 + s][:, b * P:(b + 1) * P],
                                                   ma[:, s, b * P:(b + 1) * P], ident)
                    last.then_inc(mT_done, 1)
            pe.wait_ge(m_ready, 8 + ONE)
            with pe.Fori(0, 2) as i:
                for j in range(2):
                    n0 = i * 16 + U_OUT
                    pe.wait_ge(x1_ready, i * 2 + j - j + ONE)
                    for s in range(NS):
                        nc.tensor.matmul(bank[4 * j + 2 + s][:], cst_all[0:5, C_SELB + s * P:C_SELB + (s + 1) * P],
                                         garow[0:5, bass.ds(i * (2 * COL) + j * COL, COL)], start=True, stop=True)
                    split_units(n0, 8 * j, 8, m_hi, m_lo, (4 * j, 4 * j + 1), KD)
            pe.wait_ge(x1_ready, 4 + ONE)
            norm_transposes(x1, 2)
            pe.wait_ge(h_ready, 16)
            pe.wait_ge(wrs_ready, 1)
            for s in range(NS):
                for k in range(KD):
                    for part in (h_hi, h_lo):
                        last = nc.tensor.matmul(bank[s][:, 0:2 * (NG + NE)], part[:, k, s], wrs[:, k],
                                                start=k == 0 and part is h_hi, stop=k == KD - 1 and part is h_lo)
            last.then_inc(route_done, 1)
            pe.wait_ge(comb_ready, 1)
            for f in range(16):
                s, part, g = f // 8, f // 4 % 2, f % 4
                if f >= 8:
                    pe.wait_ge(back_act if f % 2 == 0 else back_dve, (f - 8) // 2 + 1)
                for j in range(4):
                    last = nc.tensor.transpose(bank[f % 8][:, j * P:(j + 1) * P],
                                               (h_hi, h_lo)[part][:, 4 * g + j, s].bitcast(F32), ident)
                last.then_inc(back_done, 1)
            pe.wait_ge(chosen_ready, 1)
            pe.wait_ge(routing_in, 16)
            pe.wait_ge(back_act, 8)
            before, ones = cst_route[:, R_BEFORE:R_ONES], cst_route[:, R_ONES:R_SLOT]
            nc.tensor.matmul(bank[0][:, 0:NE], before, chosen[:, 0], start=True, stop=True)
            nc.tensor.matmul(bank[0][:, NE:2 * NE], before, chosen[:, 1], start=True, stop=False)
            nc.tensor.matmul(bank[0][:, NE:2 * NE], ones, chosen[:, 0], start=False, stop=True)
            nc.tensor.matmul(bank[0][:, 2 * NE:3 * NE], ones, chosen[:, 0], start=True, stop=False)
            nc.tensor.matmul(bank[0][:, 2 * NE:3 * NE], ones, chosen[:, 1], start=False, stop=True
                             ).then_inc(rank_done, 1)
            pe.wait_ge(back_dve, 8)

            def gather(f, fill):
                pe.wait_ge(xg_ready, fill + ONE)
                for kk in range(2):
                    for part in range(2):
                        o = bank[7][:, kk * 256:(kk + 1) * 256].rearrange("p (e h c) -> p e h c", e=PAIR, h=2)
                        for s in range(NS):
                            last = nc.tensor.matmul(o[:, :, part], (t_hi, t_lo)[part][:, s, (2 * f + kk) * P:(2 * f + kk + 1) * P],
                                                    pick_[:, s, :, 0], start=s == 0, stop=s == 1)
                last.then_inc(gather_done, 1)

            R = round_count(pe)
            with pe.Fori(0, R) as r:
                pe.wait_ge(pick_ready, r * (PAIRS + 1) + 1)
                for f in range(8):
                    gather(f, r * (8 * PAIRS + 8) + f)
                with pe.Fori(0, PAIRS) as p:
                    n = r * PAIRS + p
                    n0 = n * U_PAIR + U_MOE
                    fill = r * (8 * PAIRS + 8) + p * 8 + 8
                    pe.wait_ge(xg_ready, fill + ONE)

                    def parts(u, stationary, out, k, k_all):
                        def products(t, wh, wl):
                            lhs = stationary(k + t)
                            nc.tensor.matmul(out, lhs, wh, start=k + t == 0, stop=False)
                            return nc.tensor.matmul(out, lhs, wl, start=False, stop=k + t == k_all - 1)
                        unit(n0, u, products)

                    def transpose_sum(x):
                        pe.wait_ge(gu_ready, n * 4 + 2 * x + 2 + ONE)
                        pe.wait_ge(hid_ready, n * 2 + x + ONE)
                        for m in range(2):
                            for k in range(KE):
                                o = bank[2][:, m * 256 + k * CAP:m * 256 + (k + 1) * CAP]
                                last = nc.tensor.matmul(o, gu[:, m, k * P:(k + 1) * P],
                                                        cst_route[:, R_SUM:R_ALL], start=True, stop=True)
                        last.then_inc(guT_done, 1)

                    def scatter(c):
                        pe.wait_ge(d_ready, n * 8 + (3, 4, 7, 8)[c])
                        pe.wait_ge(y_added, n * 4 + c + ONE)
                        for s in range(NS):
                            for x in range(PAIR):
                                last = nc.tensor.matmul(bank[5 + s][:], pickT[:, x, s], dsb[:, x, c % 2],
                                                        start=x == 0, stop=x == 1)
                        last.then_inc(scatter_done, 1)

                    for u in range(32):
                        x, m = u // 16, u // 8 % 2
                        if u % 8 == 0:
                            pe.wait_ge(gu_ready, n * 4 + (2 * x + m - 1 if x else 0) + ONE)
                        parts(u, lambda k: xg[:, k, x].rearrange("p h c -> p (h c)"), bank[m][:], UNIT_K * (u % 8), KD)
                        if u == 1:
                            for s in range(NS):
                                for y in range(PAIR):
                                    last = nc.tensor.transpose(bank[7][:, (y * NS + s) * P:(y * NS + s + 1) * P],
                                                               pick_[:, s, y].bitcast(F32).rearrange("p h c -> p (h c)"), ident)
                            last.then_inc(pickT_done, 1)
                        if u == 4:
                            pe.wait_ge(pickT_ready, n + 1)
                            for y in range(PAIR):
                                for s in range(NS):
                                    last = nc.tensor.matmul(bank[7][:, y:y + 1],
                                                            pick_[:, s, y].bitcast(F32).rearrange("p h c -> p (h c)"),
                                                            comb[:, s, bass.ds(p * PAIR + y, 1)], start=s == 0, stop=s == 1)
                            last.then_inc(slot_w_done, 1)
                        if u == 17:
                            transpose_sum(0)
                    for q, (x, c) in enumerate(DOWN):
                        for uu in range(2):
                            u = 32 + 2 * q + uu
                            if uu == 0:
                                if q == 0:
                                    pe.wait_ge(hid_ready, n * 2 + 1 + ONE)
                                    pe.wait_ge(slot_w_ready, n + 1)
                                    pe.wait_ge(pick_ready, n + r + 2)
                                if q == 2:
                                    pe.wait_ge(hid_ready, n * 2 + 2 + ONE)
                                if q >= 2:
                                    pe.wait_ge(d_ready, n * 8 + q - 1)
                            parts(u, lambda k: hidT[:, x, k].rearrange("p h c -> p (h c)"), bank[3 + q % 2][:], UNIT_K * uu, KE)
                            if uu == 0:
                                gather(q, fill + q)
                            if u == 33:
                                transpose_sum(1)
                            if u in (38, 40, 46, 47):
                                scatter((38, 40, 46, 47).index(u))
            pe.wait_ge(rounds_done, 1)
            pe.wait_ge(xg_ready, R * (8 * PAIRS + 8) + ONE)
            for n in range(D // COL):
                for s in range(NS):
                    nc.tensor.matmul(bank[NS * n + s][:], cst_all[32:37, C_SELB + s * P:C_SELB + (s + 1) * P],
                                     garow[32:37, n * COL:(n + 1) * COL], start=True, stop=True).then_inc(ga2_done, 1)

        @block.scalar
        def _(act):
            step = Tally(act, act_step)
            for starts_at_one in (ada_evac, gu_ready, xg_ready):
                act.sem_inc(starts_at_one, ONE)

            def high(n0, u, wait=True):
                if u % 2 == 0:
                    slot = (u // 2) % RAW
                    act.wait_ge(raw_landed[slot], landed(n0, u))
                if wait:
                    act.wait_ge(unit_used, n0 + u - AHEAD + 1)
                r = raw[:, (u // 2) % RAW, (u % 2) * UNIT_K:(u % 2) * UNIT_K + UNIT_K]
                nc.scalar.activation(w_hi[:, u % AHEAD], r, ACT.Copy).then_inc(hi_ready, 1)

            def landed(n0, u):
                return n0 * 2 + 16 * (u // (2 * RAW) + 1)

            for s in range(NS):
                act.dma_start(ccol[:, s], (c_ctx, c)[s].rearrange("(p k) -> p k", k=KD) if s == 0
                              else c.rearrange("a (p k) -> p (a k)", k=KD)).then_inc(cond_in, 16)
            for s in range(NS):
                act.dma_start(x0[:, s], x_v[s]).then_inc(x_in, 16)
            for n, src in enumerate((b_ada[0, 0:2 * D], b_ada[0, 3 * D:5 * D])):
                act.dma_start(vecrows[2 * KD * n:2 * KD * (n + 1)], src.rearrange("(r c) -> r c", c=P)
                              ).then_inc(rows_in, 16)
            for n, src in enumerate((norm1_g, norm2_g)):
                act.dma_start(vecrows[(4 + n) * KD:(5 + n) * KD], src.rearrange("l (r c) -> (l r) c", c=P)
                              ).then_inc(rows_in, 16)
            act.dma_start(garow[4:5], b_ada[0:1, 2 * D:3 * D]).then_inc(x_in, 16)
            act.dma_start(garow[36:37], b_ada[0:1, 5 * D:6 * D]).then_inc(x_in, 16)
            act.wait_ge(cond_in, 32)
            nc.scalar.activation(csilu[:], ccol[:], ACT.Silu).then_inc(csilu_ready, 1)

            def root(col, n):
                act.wait_ge(var_ready, n)
                nc.scalar.activation(rms[:, col + 2:col + 4], rms[:, col:col + 2], ACT.Sqrt).then_inc(root_ready, 1)

            def sum_squares(x, col, n):
                for s in range(NS):
                    ins = nc.scalar.activation(squares[:], x[:, s], ACT.Square, accum_out=rms[:, col + s:col + s + 1])
                    if s == 0:
                        step.mark(ins)
                        step.settle()
                ins.then_inc(squares_done, 1)
                root(col, n)

            for u in range(AHEAD):
                high(0, u, wait=False)
            act.wait_ge(x_in, 64)
            sum_squares(x0, 0, 1)

            def evac_mod_rows(end, n):
                act.wait_ge(unit_used, end)
                act.wait_ge(modT_done, n + ONE)
                nc.scalar.activation(modrow[0:4], adaP[0:4, :], ACT.Copy).then_inc(modrow_ready, 1)
                act.wait_ge(modrow_ready, n + 1)
                act.sem_inc(ada_evac, 1)

            def evac_gate_rows(end, row, col):
                act.wait_ge(unit_used, end)
                nc.scalar.activation(garow[row:row + 4, bass.ds(col, COL)], adaP[0:4, :], ACT.Copy
                                     ).then_inc(ada_evac, 1)

            with act.Fori(0, 8) as i:
                for u in range(CHUNK_UNITS):
                    high(i * CHUNK_UNITS, u + AHEAD)
                evac_mod_rows(i * CHUNK_UNITS + CHUNK_UNITS, i)

            def apply_norm(g, sh, n):
                act.wait_ge(mod_ready, n)
                for b in range(8):
                    s, kg = b % NS, b // NS
                    act.wait_ge(norm_done, 8 * (n - 1) + b + 1)
                    if b >= 2:
                        act.wait_ge(h_ready, 8 * (n - 1) + b - 1)
                    for j in range(4):
                        k = 4 * kg + j
                        ins = nc.scalar.activation(htmp[:, b % 2, j], bank[b][:, j * P:(j + 1) * P], ACT.Identity,
                                                   bias=mod[:, sh, k, s:s + 1], scale=mod[:, g, k, s:s + 1])
                    ins.then_inc(htmp_ready, 1)

            apply_norm(1, 0, 1)
            with act.Fori(0, 4) as i:
                n0 = i * (4 * CHUNK_UNITS) + U_PROJ
                for q in range(4):
                    for u in range(CHUNK_UNITS):
                        high(n0, q * CHUNK_UNITS + u + AHEAD)
                    if q == 0:
                        evac_gate_rows(n0 + CHUNK_UNITS, 0, i * COL)
                    if q == 2:
                        evac_mod_rows(n0 + 3 * CHUNK_UNITS, i + 8)
            for b in range(0, 8, 2):
                act.wait_ge(dft1_done, b + 1)
                nc.scalar.activation(fa[:, b % 2, :, b // 2].rearrange("p c s t -> p s c t"),
                                     bank[b][:].rearrange("p (s c t) -> p s c t", s=2, c=2), ACT.Copy
                                     ).then_inc(dft1_act, 1)
            for o in range(4):
                hh, gp = o % 2, o // 2
                act.wait_ge(dft2_done, o + 1)
                nc.scalar.activation(f_hi[:, 4 * gp + hh:4 * gp + hh + 3:2], bank[o][:].rearrange("p (g s t) -> p g s t", g=2, s=2),
                                     ACT.Copy).then_inc(dft2_hi, 1)
            with act.Fori(0, 4) as i:
                n0 = i * (2 * CHUNK_UNITS) + U_ATT
                for j in range(2):
                    h = i * 2 + j
                    for u in range(CHUNK_UNITS):
                        high(n0, j * CHUNK_UNITS + u + AHEAD)
                        if u == 0:
                            act.wait_ge(qk_done, h + 1)
                            nc.scalar.activation(qkT[:].rearrange("p c t -> p (c t)"), bank[0][:], ACT.Copy).then_inc(qkT_ready, 1)
                        if u == 3:
                            act.wait_ge(scores_ready, h + 1)
                            nc.scalar.activation(prb[:, 0], scr[:, 0], ACT.Exp, bias=smx[:, 0:1],
                                                 accum_out=smx[:, 2:3])
                            nc.scalar.activation(prb[:, 1:3], scr[:, 1:3], ACT.Exp, bias=smx[:, 1:2],
                                                 accum_out=smx[:, 3:4]).then_inc(exp_done, 1)
                        if u == 5:
                            act.wait_ge(prT_done, h + 1)
                            nc.scalar.activation(prT[:].rearrange("p c t -> p (c t)"), bank[3][:, 0:3 * P], ACT.Copy).then_inc(prT_ready, 1)
                        if u == 6:
                            act.wait_ge(pv_done, h + 1)
                            nc.scalar.activation(o_hi[:, bass.ds(h, 1)],
                                                 bank[4][:, 0:2 * P].rearrange("p (a s t) -> p a s t", a=1, s=2), ACT.Copy
                                                 ).then_inc(o_hi_ready, 1)
                    if j == 0:
                        evac_mod_rows(n0 + CHUNK_UNITS, i + 12)
                    else:
                        evac_gate_rows(n0 + 2 * CHUNK_UNITS, 32, i * COL)
            act.wait_ge(kv_sent, 32)
            with act.Fori(0, 4) as i:
                n0 = i * 24 + U_MERGE
                for u in range(24):
                    high(n0, u + AHEAD)
                    if u in (8, 16):
                        g = ma if u == 8 else mb
                        act.wait_ge(gate_pre, i * 2 + u // 8)
                        nc.scalar.activation(g[:], g[:], ACT.Sigmoid).then_inc(gate_sig, 1)
                for s in range(NS):
                    act.wait_ge(mT_done, i * 2 + s + 1 + ONE)
                    nc.scalar.activation(m_hi[:, bass.ds(i * 4, 4), s], bank[4 + s][:].rearrange("p (k t) -> p k t", k=4),
                                         ACT.Copy).then_inc(m_hi_ready, 1)
            with act.Fori(0, 2) as i:
                for j in range(2):
                    n0 = i * 16 + U_OUT
                    for u in range(CHUNK_UNITS):
                        high(n0, 8 * j + u + AHEAD)
                    act.wait_ge(unit_used, n0 + 8 * j + 8)
                    for s in range(NS):
                        ins = nc.scalar.activation(gab[:, j, s], bank[4 * j + 2 + s][:], ACT.Copy)
                    ins.then_inc(gab_ready, 1)
            act.wait_ge(x1_ready, 4 + ONE)
            sum_squares(x1, 4, 2)
            apply_norm(3, 2, 2)

            for n in range(2 * NS):
                act.wait_ge(route_arg, n + 1)
                nc.scalar.activation(rt[:, 16:20], rt[:, 12:16], ACT.Exp).then_inc(route_exp, 1)

            for f in range(0, 16, 2):
                s, part, g = f // 8, f // 4 % 2, f % 4
                act.wait_ge(back_done, f + 1)
                nc.scalar.activation((t_hi, t_lo)[part][:, s, g * COL:(g + 1) * COL], bank[f % 8][:], ACT.Copy
                                     ).then_inc(back_act, 1)

            def evac_gather(f, fill):
                act.wait_ge(gather_done, fill + 1)
                nc.scalar.activation(xg[:, 2 * f:2 * f + 2].rearrange("p k e h c -> p (k e h c)"), bank[7][:],
                                     ACT.Copy).then_inc(xg_ready, 1)

            with act.Fori(0, round_count(act)) as r:
                for f in range(8):
                    evac_gather(f, r * (8 * PAIRS + 8) + f)
                with act.Fori(0, PAIRS) as p:
                    n = r * PAIRS + p
                    n0 = n * U_PAIR + U_MOE
                    fill = r * (8 * PAIRS + 8) + p * 8 + 8
                    for u in range(U_PAIR):
                        high(n0, u + AHEAD)
                        if u == 2:
                            act.wait_ge(pickT_done, n + 1)
                            nc.scalar.activation(pickT[:].rearrange("p e s t -> p (e s t)"), bank[7][:], ACT.Copy
                                                 ).then_inc(pickT_ready, 1)
                        if u == 5:
                            act.wait_ge(slot_w_done, n + 1)
                            nc.scalar.activation(slot_w[:], bank[7][:, 0:PAIR], ACT.Copy).then_inc(slot_w_ready, 1)
                        if u in (7, 15, 23, 31):
                            m = u // 8 % 2
                            act.wait_ge(unit_used, n0 + u + 1)
                            nc.scalar.activation(gu[:, m], bank[m][:], ACT.Copy).then_inc(gu_ready, 1)
                        if u in (17, 33):
                            x = u // 32
                            act.wait_ge(guT_done, n * 2 + x + 1)
                            nc.scalar.activation(sgT[:].rearrange("p k c -> p (k c)"), bank[2][:, 0:256], ACT.Silu
                                                 ).then_inc(silu_ready, 1)
                        if u >= 32 and u % 2:
                            q = (u - 33) // 2
                            x, col = DOWN[q]
                            act.wait_ge(unit_used, n0 + u + 1)
                            if q == 0:
                                act.wait_ge(slot_w_ready, n + 1)
                                act.wait_ge(scatter_done, n * 4 + ONE)
                            if q in (4, 5):
                                act.wait_ge(scatter_done, n * 4 + q - 3 + ONE)
                            nc.scalar.activation(dsb[:, x, col % 2], bank[3 + q % 2][:], ACT.Copy, scale=slot_w[:, x:x + 1]
                                                 ).then_inc(d_ready, 1)
                            evac_gather(q, fill + q)
            root(8, 3)

        @block.vector
        def _(dve):
            step = Tally(dve, dve_step)
            for starts_at_one in (modT_evac, proj_evac, m_ready, x1_ready, o_ready, y_added, hid_ready):
                dve.sem_inc(starts_at_one, ONE)
            v = nc.vector

            def low(n0, u):
                dve.wait_ge(hi_ready, n0 + u + 1)
                r = raw[:, (u // 2) % RAW, (u % 2) * UNIT_K:(u % 2) * UNIT_K + UNIT_K]
                v.tensor_tensor(w_lo[:, u % AHEAD], r, w_hi[:, u % AHEAD].bitcast(F32), ALU.subtract
                                ).then_inc(lo_ready, 1)

            def chained(ins):
                step.mark(ins)
                step.settle()

            chained(v.memset(cvec[:].bitcast(F32), 0.0))
            dve.wait_ge(csilu_ready, 1)
            parts = cvec[:, 0:4 * KD].rearrange("p (k c) -> p c k", c=4)
            chained(v.tensor_copy(parts[:, 0:2], csilu[:]))
            v.tensor_tensor(parts[:, 2:4], csilu[:], parts[:, 0:2].bitcast(F32), ALU.subtract).then_inc(cvec_ready, 1)
            for u in range(AHEAD):
                low(0, u)
            dve.wait_ge(vecT_done, 1)
            v.tensor_copy(vecT[:].rearrange("p v k -> p (v k)"), bank[0][:, 0:6 * KD]).then_inc(vecT_ready, 1)

            def inverse_rms(col, n):
                dve.wait_ge(squares_done, n)
                var, y, t = rms[:, col:col + 2], rms[:, col + 2:col + 4], rms[:, 12:14]
                v.tensor_scalar(var, var, 1.0 / D, EPS, ALU.mult, ALU.add).then_inc(var_ready, 1)
                dve.wait_ge(root_ready, n)
                chained(v.reciprocal(y, y))
                chained(v.tensor_tensor(t, y, y, ALU.mult))
                chained(v.tensor_tensor(t, t, var, ALU.mult))
                chained(v.tensor_scalar(t, t, -0.5, 1.5, ALU.mult, ALU.add))
                chained(v.tensor_tensor(y, y, t, ALU.mult))

            dve.wait_ge(consts_in, 16)
            inverse_rms(0, 1)
            for s in range(NS):
                chained(v.tensor_scalar(diag[:, s], ident, rms[:, 2 + s:3 + s], None, ALU.mult))
            dve.sem_inc(diag_ready, 1)
            dve.wait_ge(bias_in, 16 * ROWS * ROWS)
            for h in range(HEADS):
                b = bias[:, h].rearrange("p r c -> p (r c)")
                ins = v.tensor_tensor(b, b, mask, ALU.add)
            chained(ins)
            dve.wait_ge(router_in, 64)
            chained(v.tensor_copy(wrs[:, :, 0], wr[:]))
            v.tensor_tensor(wrs[:, :, 1], wr[:], wrs[:, :, 0].bitcast(F32), ALU.subtract).then_inc(wrs_ready, 1)

            def evac_modT(n):
                dve.wait_ge(modT_done, n + 1 + ONE)
                v.tensor_copy(modf[:, bass.ds(n * 4, 4)], modP[:, 0:4 * NS].rearrange("p (k s) -> p k s", s=NS)
                              ).then_inc(modT_evac, 1)

            modf = mod[:].rearrange("p v k s -> p (v k) s")

            def finish_mods(shift, scale, g, n):
                for s in range(NS):
                    v.tensor_tensor(mod[:, shift, :, s], mod[:, shift, :, s], vecT[:, shift], ALU.add)
                    chained(v.tensor_tensor(mod[:, scale, :, s], mod[:, scale, :, s], vecT[:, scale], ALU.add))
                    chained(v.scalar_tensor_tensor(out=mod[:, scale, :, s], in0=mod[:, scale, :, s], scalar=1.0,
                                                   in1=vecT[:, g], op0=ALU.add, op1=ALU.mult))
                dve.sem_inc(mod_ready, 1)

            with dve.Fori(0, 8) as i:
                for u in range(CHUNK_UNITS):
                    low(i * CHUNK_UNITS, u + AHEAD)
                evac_modT(i)
            dve.wait_ge(modT_evac, 8 + ONE)
            finish_mods(0, 1, 4, 1)

            def split_h(n):
                for b in range(8):
                    s, kg = b % NS, b // NS
                    dve.wait_ge(htmp_ready, 8 * (n - 1) + b + 1)
                    hi = h_hi[:, 4 * kg:4 * kg + 4, s]
                    chained(v.tensor_copy(hi, htmp[:, b % 2]))
                    v.tensor_tensor(h_lo[:, 4 * kg:4 * kg + 4, s], htmp[:, b % 2], hi.bitcast(F32), ALU.subtract
                                    ).then_inc(h_ready, 1)

            split_h(1)
            with dve.Fori(0, 4) as i:
                n0 = i * (4 * CHUNK_UNITS) + U_PROJ
                for q in range(4):
                    for u in range(CHUNK_UNITS):
                        low(n0, q * CHUNK_UNITS + u + AHEAD)
                    if q % 2:
                        j = q // 2
                        dve.wait_ge(unit_used, n0 + (q + 1) * CHUNK_UNITS)
                        dve.wait_ge(bin_landed[j], i * 16 + 16)
                        for s in range(NS):
                            ins = v.tensor_tensor(uqkv[:, s, bass.ds(i * (2 * COL) + j * COL, COL)], bank[2 * j + s][:],
                                                  bin_[:, j], ALU.add)
                        ins.then_inc(proj_evac, 1)
                evac_modT(i + 8)
            for b in range(1, 8, 2):
                dve.wait_ge(dft1_done, b + 1)
                v.tensor_copy(fa[:, b % 2, :, b // 2].rearrange("p c s t -> p s c t"),
                              bank[b][:].rearrange("p (s c t) -> p s c t", s=2, c=2)).then_inc(dft1_dve, 1)
            for o in range(4):
                hh, gp = o % 2, o // 2
                dve.wait_ge(dft2_hi, o + 1)
                sl = slice(4 * gp + hh, 4 * gp + hh + 3, 2)
                v.tensor_tensor(f_lo[:, sl], bank[o][:].rearrange("p (g s t) -> p g s t", g=2, s=2),
                                f_hi[:, sl].bitcast(F32), ALU.subtract).then_inc(dft2_lo, 1)
            with dve.Fori(0, 4) as i:
                step.enter(i, 2 * 7)
                n0 = i * (2 * CHUNK_UNITS) + U_ATT
                for j in range(2):
                    h = i * 2 + j
                    for u in range(CHUNK_UNITS):
                        low(n0, j * CHUNK_UNITS + u + AHEAD)
                        if u == 0:
                            dve.wait_ge(qk_done, h + 1)
                            v.tensor_copy(kcT[:], bank[1][:, 0:P]).then_inc(kcT_ready, 1)
                        if u == 2:
                            dve.wait_ge(scores_done, h + 1)
                            chained(v.tensor_scalar(scr[:, 0:2], bank[2][:, 0:2 * P].rearrange("p (c t) -> p c t", c=2), SCALE, None, ALU.mult))
                            chained(v.scalar_tensor_tensor(
                                out=scr[:, 2], in0=bank[2][:, 2 * P:3 * P], scalar=SCALE,
                                in1=bias[:, bass.ds(h, 1)].rearrange("p h r c -> p (h r c)"), op0=ALU.mult, op1=ALU.add))
                            chained(v.tensor_reduce(smx[:, 0:1], scr[:, 0], X, ALU.max, negate=True))
                            chained(v.tensor_reduce(smx[:, 1:2], scr[:, 1:3].rearrange("p a t -> p (a t)"), X, ALU.max,
                                                    negate=True))
                            dve.sem_inc(scores_ready, 1)
                        if u == 4:
                            dve.wait_ge(exp_done, h + 1)
                            chained(v.reciprocal(smx[:, 4:6], smx[:, 2:4]))
                            chained(v.tensor_scalar(prb[:, 0], prb[:, 0], smx[:, 4:5], None, ALU.mult))
                            chained(v.tensor_scalar(prb[:, 1:3], prb[:, 1:3], smx[:, 5:6], None, ALU.mult))
                            dve.sem_inc(probs_ready, 1)
                        if u == 6:
                            dve.wait_ge(o_hi_ready, h + 1)
                            v.tensor_tensor(o_lo[:, bass.ds(h, 1)], bank[4][:, 0:2 * P].rearrange("p (a s t) -> p a s t", a=1, s=2),
                                            o_hi[:, bass.ds(h, 1)].bitcast(F32), ALU.subtract).then_inc(o_ready, 1)
                    if j == 0:
                        evac_modT(i + 12)
            step.leave(4)
            dve.wait_ge(modT_evac, 16 + ONE)
            finish_mods(2, 3, 5, 2)
            with dve.Fori(0, 4) as i:
                step.enter(i, 2)
                n0 = i * 24 + U_MERGE
                for u in range(24):
                    low(n0, u + AHEAD)
                    if u in (7, 15):
                        j = u // 8
                        g = (ma, mb)[j]
                        dve.wait_ge(unit_used, n0 + u + 1)
                        dve.wait_ge(bin_landed[j], i * 16 + 16 * 5)
                        if j == 0:
                            dve.wait_ge(mT_done, i * 2 + ONE)
                        for s in range(NS):
                            ins = v.tensor_tensor(g[:, s], bank[2 * j + s][:], bin_[:, j], ALU.add)
                        ins.then_inc(gate_pre, 1)
                    if u in (19, 23):
                        j = u // 23
                        g = (ma, mb)[j]
                        dve.wait_ge(unit_used, n0 + u + 1)
                        dve.wait_ge(gate_sig, i * 2 + j + 1)
                        for s in range(NS):
                            ins = v.tensor_tensor(g[:, s], g[:, s], bank[4 + 2 * j + s][:], ALU.mult)
                        chained(ins)
                v.tensor_tensor(ma[:], ma[:], mb[:], ALU.add).then_inc(merged_ready, 1)
                for s in range(NS):
                    dve.wait_ge(m_hi_ready, i * 2 + s + 1)
                    v.tensor_tensor(m_lo[:, bass.ds(i * 4, 4), s], bank[4 + s][:].rearrange("p (k t) -> p k t", k=4),
                                    m_hi[:, bass.ds(i * 4, 4), s].bitcast(F32), ALU.subtract).then_inc(m_ready, 1)
            step.leave(4)
            dve.wait_ge(x1_in, 32)
            with dve.Fori(0, 2) as i:
                step.enter(i, 2)
                for j in range(2):
                    n0 = i * 16 + U_OUT
                    for u in range(CHUNK_UNITS):
                        low(n0, 8 * j + u + AHEAD)
                    dve.wait_ge(unit_used, n0 + 8 * j + 8)
                    dve.wait_ge(gab_ready, i * 2 + j + 1)
                    for s in range(NS):
                        ins = v.tensor_tensor(t2[:, j, s], gab[:, j, s], bank[4 * j + s][:], ALU.mult)
                    chained(ins)
                    xs = x1[:, :, bass.ds(i * (2 * COL) + j * COL, COL)]
                    v.tensor_tensor(xs, xs, t2[:, j], ALU.add).then_inc(x1_ready, 1)
            step.leave(2)
            inverse_rms(4, 2)
            for s in range(NS):
                chained(v.tensor_scalar(diag[:, s], ident, rms[:, 6 + s:7 + s], None, ALU.mult))
            dve.sem_inc(diag_ready, 1)
            split_h(2)

            def exponential(n):
                dve.sem_inc(route_arg, 1)
                dve.wait_ge(route_exp, n + 1)

            dve.wait_ge(route_done, 1)
            for s in range(NS):
                chained(v.tensor_tensor(lg[:, s], bank[s][:, 0:NG + NE], br[:], ALU.add))
                chained(v.tensor_tensor(lg[:, s], lg[:, s], bank[s][:, NG + NE:2 * (NG + NE)], ALU.add))
                L = lg[:, s]

                def pick(values, best, one_hot, scratch):
                    chained(v.tensor_reduce(best, values, X, ALU.max))
                    chained(v.scalar_tensor_tensor(out=scratch, in0=values, scalar=best, in1=first,
                                                   op0=ALU.is_equal, op1=ALU.mult))
                    chained(v.tensor_reduce(rt[:, 100:101], scratch, X, ALU.max))
                    chained(v.tensor_scalar(one_hot, scratch, rt[:, 100:101], None, ALU.is_equal))

                pick(L[:, 0:NG], rt[:, 4:5], rt[:, 8:12], rt[:, 104:108])
                chained(v.tensor_scalar(rt[:, 12:16], L[:, 0:NG], rt[:, 4:5], None, ALU.subtract))
                exponential(2 * s)
                chained(v.tensor_reduce(rt[:, 5:6], rt[:, 16:20], X, ALU.add))
                chained(v.reciprocal(rt[:, 6:7], rt[:, 5:6]))
                for g in range(NG):
                    chained(v.tensor_scalar(rt[:, 20 + 4 * g:24 + 4 * g], L[:, NG + 4 * g:NG + 4 * g + 4],
                                            rt[:, 8 + g:9 + g], None, ALU.mult))
                chained(v.tensor_reduce(rt[:, 36:40], rt[:, 20:36].rearrange("p (g e) -> p e g", g=NG), X, ALU.add))
                pick(rt[:, 36:40], rt[:, 40:41], rt[:, 44:48], rt[:, 104:108])
                chained(v.scalar_tensor_tensor(out=rt[:, 48:52], in0=rt[:, 44:48], scalar=-3e38, in1=rt[:, 36:40],
                                               op0=ALU.mult, op1=ALU.add))
                pick(rt[:, 48:52], rt[:, 52:53], rt[:, 56:60], rt[:, 104:108])
                chained(v.tensor_scalar(rt[:, 12:13], rt[:, 52:53], rt[:, 40:41], None, ALU.subtract))
                exponential(2 * s + 1)
                chained(v.tensor_scalar(rt[:, 60:61], rt[:, 16:17], 1.0, None, ALU.add))
                chained(v.reciprocal(rt[:, 61:62], rt[:, 60:61]))
                chained(v.tensor_tensor(rt[:, 62:63], rt[:, 61:62], rt[:, 6:7], ALU.mult))
                chained(v.tensor_tensor(rt[:, 63:64], rt[:, 62:63], rt[:, 16:17], ALU.mult))
                chained(v.tensor_scalar(rt[:, 64:68], rt[:, 44:48], rt[:, 62:63], None, ALU.mult))
                chained(v.scalar_tensor_tensor(out=rt[:, 68:72], in0=rt[:, 56:60], scalar=rt[:, 63:64],
                                               in1=rt[:, 64:68], op0=ALU.mult, op1=ALU.add))
                for g in range(NG):
                    chained(v.tensor_scalar(comb[:, s, 4 * g:4 * g + 4], rt[:, 68:72], rt[:, 8 + g:9 + g], None, ALU.mult))
                    chained(v.scalar_tensor_tensor(out=chosen[:, s, 4 * g:4 * g + 4], in0=rt[:, 44:48], scalar=1.0,
                                                   in1=rt[:, 56:60], op0=ALU.mult, op1=ALU.add))
                    chained(v.tensor_scalar(chosen[:, s, 4 * g:4 * g + 4], chosen[:, s, 4 * g:4 * g + 4],
                                            rt[:, 8 + g:9 + g], None, ALU.mult))
            dve.sem_inc(comb_ready, 1)
            dve.sem_inc(chosen_ready, 1)
            dve.wait_ge(y_zero, 1)
            for f in range(1, 16, 2):
                s, part, g = f // 8, f // 4 % 2, f % 4
                dve.wait_ge(back_done, f + 1)
                v.tensor_copy((t_hi, t_lo)[part][:, s, g * COL:(g + 1) * COL], bank[f % 8][:]).then_inc(back_dve, 1)
            dve.wait_ge(rank_done, 1)
            chained(v.memset(key[:], -1.0))
            for s in range(NS):
                chained(v.scalar_tensor_tensor(out=key[:, s, 0:NE], in0=bank[0][:, s * NE:(s + 1) * NE], scalar=1000.0,
                                               in1=chosen[:, s], op0=ALU.add, op1=ALU.mult))
                chained(v.tensor_scalar(key[:, s, 0:NE], key[:, s, 0:NE], -1000.0, None, ALU.add))
            most, more = rt[:, 110:111], rt[:, 111:112]
            chained(v.tensor_reduce(most, bank[0][:, 2 * NE:3 * NE], X, ALU.max))
            chained(v.tensor_scalar(more, most, float(CAP), 1.0, ALU.is_gt, ALU.add))
            for n in range(2, NS * TOK // CAP):
                chained(v.tensor_scalar(rt[:, 112:113], most, float(n * CAP), None, ALU.is_gt))
                chained(v.tensor_tensor(more, more, rt[:, 112:113], ALU.add))
            v.tensor_copy(rounds[:], more).then_inc(rounds_ready, 1)

            slots = cst_route[:, R_SLOT:R_SUM].rearrange("p (h c) -> p h c", h=2)

            def build_pick(p):
                for s in range(NS):
                    for x in range(PAIR):
                        ins = v.tensor_scalar(pick_[:, s, x], slots, key[:, s, bass.ds(p * PAIR + x, 1)], None, ALU.is_equal)
                ins.then_inc(pick_ready, 1)

            R = round_count(dve)
            with dve.Fori(0, R) as r:
                build_pick(0)
                with dve.Fori(0, PAIRS) as p:
                    n = r * PAIRS + p
                    n0 = n * U_PAIR + U_MOE
                    dve.wait_ge(y_added, n * 4 + ONE)

                    def add(c):
                        dve.wait_ge(scatter_done, n * 4 + c + 1 + ONE)
                        for s in range(NS):
                            ys = ysum[:, s, c * COL:(c + 1) * COL]
                            ins = v.tensor_tensor(ys, ys, bank[5 + s][:], ALU.add)
                        ins.then_inc(y_added, 1)

                    for u in range(U_PAIR):
                        low(n0, u + AHEAD)
                        if u == 30:
                            dve.wait_ge(slot_w_done, n + 1)
                            build_pick(p + 1)
                        if u in (17, 33):
                            x = u // 32
                            dve.wait_ge(silu_ready, n * 2 + x + 1)
                            step.enter((n * 2 + x), 2)
                            chained(v.tensor_tensor(hidf[:].rearrange("p k c -> p (k c)"), bank[2][:, 256:512],
                                                    sgT[:].rearrange("p k c -> p (k c)"), ALU.mult))
                            chained(v.tensor_copy(hidT[:, x, :, 0], hidf[:]))
                            step.base, step.n = step.start, 0
                            v.tensor_tensor(hidT[:, x, :, 1], hidf[:], hidT[:, x, :, 0].bitcast(F32), ALU.subtract
                                            ).then_inc(hid_ready, 1)
                        if u in (39, 41, 47):
                            add((39, 41, 47).index(u))
                    add(3)
                dve.wait_ge(pick_ready, r * (PAIRS + 1) + PAIRS + 1)
                v.tensor_scalar(key[:], key[:], -float(CAP), None, ALU.add).then_inc(key_moved, 1)
                dve.wait_ge(key_moved, r + 1)
            dve.wait_ge(y_added, R * (4 * PAIRS) + ONE)
            dve.sem_inc(rounds_done, 1)
            step = Tally(dve, tail_step)
            for n in range(D // COL):
                for s in range(NS):
                    dve.wait_ge(ga2_done, NS * n + s + 1)
                    cols = slice(n * COL, (n + 1) * COL)
                    chained(v.tensor_tensor(ysum[:, s, cols], ysum[:, s, cols], bank[NS * n + s][:], ALU.mult))
                    chained(v.tensor_tensor(x1[:, s, cols], x1[:, s, cols], ysum[:, s, cols], ALU.add))
            for s in range(NS):
                chained(v.tensor_tensor(ysum[:, s], x1[:, s], x1[:, s], ALU.mult))
                chained(v.tensor_reduce(rms[:, 8 + s:9 + s], ysum[:, s], X, ALU.add))
            dve.sem_inc(squares_done, 1)
            inverse_rms(8, 3)
            dve.wait_ge(gfin_in, 16)
            for n in range(D // COL):
                for s in range(NS):
                    cols = slice(n * COL, (n + 1) * COL)
                    v.scalar_tensor_tensor(out=x1[:, s, cols], in0=x1[:, s, cols], scalar=rms[:, 10 + s:11 + s],
                                           in1=gfin[:, cols], op0=ALU.mult, op1=ALU.mult).then_inc(y_ready, 1)


_INS = ["x_prompt", "x_sample", "cache_k_ctx", "cache_v_ctx", "c", "c_ctx", "norm1_g", "norm2_g", "w_ada", "b_ada",
        "w_in", "b_in", "w_fourier", "w_na_o", "rpb", "w_out", "w_router_group", "b_router_group",
        "w_router_expert", "b_router_expert", "w_exp_gate", "w_exp_up", "w_exp_down", "final_norm_g"]
_OUTS = [(1, TOK, D), (1, TOK, D), (1, 1, TOK, HEADS, HD), (1, 1, TOK, HEADS, HD)]


def kernel(**inputs):
    import concourse.bacc as bacc
    from concourse.bass_utils import run_bass_kernel_spmd

    nc = bacc.Bacc("TRN2", target_bir_lowering=False, num_devices=1)
    arrays, args = {}, []
    for name in _INS:
        a = np.ascontiguousarray(inputs[name])
        arrays[f"in_{name}"] = a
        args.append(nc.dram_tensor(f"in_{name}", a.shape, mybir.dt.from_np(a.dtype), kind="ExternalInput").ap())
    for name, a in (("shape_constants", shape_constants()), ("routing_constants", routing_constants())):
        arrays[name] = a
        args.append(nc.dram_tensor(name, a.shape, F32, kind="ExternalInput").ap())
    for i, shape in enumerate(_OUTS):
        args.append(nc.dram_tensor(f"out_{i}", shape, F32, kind="ExternalOutput").ap())
    backbone_step(nc, *args)
    result = run_bass_kernel_spmd(nc, [arrays], core_ids=[0])
    return tuple(result.results[0][f"out_{i}"] for i in range(len(_OUTS)))
```

```python
from contextlib import ExitStack

import numpy as np

import concourse.bass as bass
from concourse import mybir

ALU = mybir.AluOpType
ACT = mybir.ActivationFunctionType
F32 = mybir.dt.float32
F32R = mybir.dt.float32r
X = mybir.AxisListType.X

P = 128
TOK = 128
NS = 2
D = 2048
KD = D // P
COL = 512
HEADS, HD = 8, 128
NA = HEADS * HD
FW, FG, FGD = 1024, 4, 256
KF = FW // P
GRID_W, ROWS, WIN = 64, 2, 16
NG, EPG, NE, EH = 4, 4, 16, 512
KE = EH // P
SCALE = float(HD) ** -0.5
EPS = 1e-6

LOAD_K, UNIT_K = 4, 2
RAW, AHEAD = 4, 4
CHUNK_UNITS = KD // UNIT_K
ONE = 1

C_ID = 0
C_DFTN = C_ID + P
C_DFTC = C_DFTN + 2 * TOK
C_MASK = C_DFTC + 2 * 2 * FGD
C_SEL = C_MASK + TOK
C_SELB = C_SEL + NS
C_FIRST = C_SELB + NS * P
C_ALL = C_FIRST + EPG
R_BEFORE = 0
R_ONES = R_BEFORE + TOK
R_SLOT = R_ONES + TOK
R_SUM = R_SLOT + 2 * 64
R_ALL = R_SUM + 64

CAP, PAIR = 64, 2
PAIRS = NE // PAIR


def shape_constants():
    c = np.zeros((P, C_ALL), np.float64)
    c[:, C_ID:C_ID + P] = np.eye(P)
    n = np.arange(TOK)
    ang = 2 * np.pi * (np.outer(n, n) % TOK) / TOK
    c[:, C_DFTN:C_DFTN + TOK] = np.cos(ang) / np.sqrt(TOK)
    c[:, C_DFTN + TOK:C_DFTC] = np.sin(ang) / np.sqrt(TOK)
    m = np.arange(FGD)
    ang = 2 * np.pi * (np.outer(m, m) % FGD) / FGD
    both = np.stack([np.cos(ang), -np.sin(ang)], 1) / np.sqrt(FGD)
    c[:, C_DFTC:C_MASK] = both.reshape(2, P, 2, FGD).transpose(1, 0, 2, 3).reshape(P, -1)
    col = np.arange(GRID_W)
    start = np.clip(col - WIN // 2, 0, GRID_W - WIN)
    ok = (col[None, :] >= start[:, None]) & (col[None, :] < start[:, None] + WIN)
    c[:, C_MASK:C_SEL] = np.where(np.tile(ok, (ROWS, ROWS)), 0.0, -1e30)
    for r in range(4):
        c[r, C_SEL + r % NS] = 1.0
    for base in (0, 32):
        for r in range(5):
            for s in range(NS):
                if r == 4 or r % NS == s:
                    c[base + r, C_SELB + s * P:C_SELB + (s + 1) * P] = 1.0
    c[:, C_FIRST:C_ALL] = np.arange(EPG, 0, -1)
    return c.astype(np.float32)


def routing_constants():
    c = np.ones((P, R_ALL), np.float32)
    c[:, R_BEFORE:R_ONES] = np.triu(np.ones((TOK, TOK)), 1)
    c[:, R_SLOT:R_SUM] = np.tile(np.arange(CAP), 2)
    c[:, R_SUM:] = np.tile(np.eye(CAP), (2, 1))
    return c


class Tally:

    def __init__(self, engine, sem):
        self.engine, self.sem, self.base, self.n = engine, sem, 0, 0

    def mark(self, instruction):
        instruction.then_inc(self.sem, 1)
        self.n += 1

    def settle(self):
        self.engine.wait_ge(self.sem, self.base + self.n)

    def enter(self, i, per, first=0):
        self.start, self.per = self.base + self.n, per
        self.base, self.n = i * per + (self.start - first * per), 0

    def leave(self, count):
        assert self.n == self.per, (self.n, self.per)
        self.base, self.n = self.start + count * self.per, 0


def backbone_step(nc, x_prompt, x_sample, cache_k, cache_v, c, c_ctx, norm1_g, norm2_g, w_ada, b_ada,
                  w_in, b_in, w_fourier, w_na_o, rpb, w_out, w_rg, b_rg, w_re, b_re, w_gate, w_up,
                  w_down, final_g, constants, routing, y_prompt, y_sample, new_k, new_v):
    ada_v = w_ada.rearrange("l (p k) n -> p (l k) n", k=KD)
    in_v = w_in.rearrange("l (k p) n -> p (l k) n", p=P)
    fo_v = w_fourier.rearrange("l (k p) n -> p (l k) n", p=P)
    na_v = w_na_o.rearrange("l (k p) n -> p (l k) n", p=P)
    out_v = w_out.rearrange("l (k p) n -> p (l k) n", p=P)
    gate_v = w_gate.rearrange("l e (k p) n -> p (l e k) n", p=P)
    up_v = w_up.rearrange("l e (k p) n -> p (l e k) n", p=P)
    down_v = w_down.rearrange("l e (k p) n -> p (l e k) n", p=P)
    rg_v = w_rg.rearrange("l (k p) n -> p (l k) n", p=P)
    re_v = w_re.rearrange("l (k p) n -> p (l k) n", p=P)
    kc_v = cache_k.rearrange("a l t h d -> t (a l h) d")
    vc_v = cache_v.rearrange("a l t h d -> t (a l h) d")
    x_v = [x_prompt.rearrange("a t n -> (a t) n"), x_sample.rearrange("a t n -> (a t) n")]
    y_v = [y_prompt.rearrange("a t n -> (a t) n"), y_sample.rearrange("a t n -> (a t) n")]
    NR = HEADS * 3
    skew = nc.dram_tensor("bias_rows", [GRID_W, NR, P], F32, kind="Internal")

    with ExitStack() as ctx:
        at = [16512]

        def region(size):
            at[0] += size
            return at[0] - size

        def place(name, shape, offset, dt=F32):
            return nc.alloc_sbuf_tensor_at(name, shape, dt, offset=offset).ap()

        def own(name, shape, dt=F32):
            size = 4 * int(np.prod(shape[1:]))
            return place(name, shape, region((size + 31) // 32 * 32), dt)

        def sem(name):
            return ctx.enter_context(nc.semaphore(name))

        KB = 1024
        h_hi = own("h_hi", [P, KD, NS, TOK], F32R)
        h_lo = own("h_lo", [P, KD, NS, TOK], F32R)
        H = 16512
        raw = own("raw", [P, RAW, LOAD_K, COL])
        w_hi = own("w_hi", [P, AHEAD, UNIT_K, COL], F32R)
        w_lo = own("w_lo", [P, AHEAD, UNIT_K, COL], F32R)
        A, F, B = region(32 * KB), region(32 * KB), region(16 * KB)
        x0 = place("x0", [P, NS, D], A)
        uqkv = place("uqkv", [P, NS, FW + 3 * NA], A)
        m_hi = place("m_hi", [P, KD, NS, TOK], A, F32R)
        m_lo = place("m_lo", [P, KD, NS, TOK], A + 16 * KB, F32R)
        t_hi = place("t_hi", [P, NS, D], A, F32R)
        t_lo = place("t_lo", [P, NS, D], A + 16 * KB, F32R)
        f_hi = place("f_hi", [P, KF, NS, TOK], F, F32R)
        f_lo = place("f_lo", [P, KF, NS, TOK], F + 8 * KB, F32R)
        o_hi = place("o_hi", [P, KF, NS, TOK], F + 16 * KB, F32R)
        o_lo = place("o_lo", [P, KF, NS, TOK], F + 24 * KB, F32R)
        x1 = place("x1", [P, NS, D], F)
        ysum = place("ysum", [P, NS, D], F + 16 * KB)
        xg = place("xg", [P, PAIR, KD, 2, CAP], H, F32R)
        hidT = place("hidT", [P, PAIR, KE, 2, CAP], H + 16 * KB, F32R)
        sgT = place("sgT", [P, KE, CAP], H + 20 * KB)
        hidf = place("hidf", [P, PAIR, KE, CAP], H + 21 * KB)
        gfin = place("gfin", [P, D], H + 24 * KB)
        squares = place("squares", [P, D], B)
        htmp = place("htmp", [P, 2, 4, TOK], B + 8 * KB)
        vecrows = place("vecrows", [6 * KD, P], B + 12 * KB)
        rpbpad = place("rpbpad", [NR, P], B + 12 * KB + 512)
        fa = place("fa", [P, 2, 2, FG, NS, TOK], B)
        st = place("st", [P, 2, NS, 3, HD], B)
        cst = place("cst", [P, 2, 2, HD], B + 6 * KB)
        qkT = place("qkT", [P, 4, TOK], B + 8 * KB)
        kcT = place("kcT", [P, TOK], B + 10 * KB)
        scr = place("scr", [P, 3, TOK], B + 10 * KB + 512)
        prb = place("prb", [P, 3, TOK], B + 12 * KB)
        prT = place("prT", [P, 3, TOK], B + 13 * KB + 512)
        ma = place("ma", [P, NS, COL], B)
        mb = place("mb", [P, NS, COL], B + 4 * KB)
        pick_ = place("pick", [P, PAIR, NS, CAP], H + 23 * KB, F32R)
        pickd = place("pickd", [P, PAIR, NS, 2, CAP], B)
        pickT = place("pickT", [P, PAIR, NS, TOK], B + 2 * KB)
        dsb = place("dsb", [P, PAIR, 2, COL], B + 4 * KB)
        gu = place("gu", [P, 2, EH], B + 12 * KB)
        gab = place("gab", [P, 2, NS, COL], B)
        t2 = place("t2", [P, 2, NS, COL], B + 8 * KB)

        garow = own("garow", [37, D])
        bias = own("bias", [P, HEADS, ROWS, GRID_W])
        C = region((4 * C_ALL + 31) // 32 * 32)
        cst_all = place("cst_all", [P, C_ALL], C)
        cst_route = place("cst_route", [P, R_ALL], C + 4 * C_DFTN)
        bin_ = own("bin", [P, 2, COL])
        modrow = place("modrow", [4, COL], region(COL * 4))
        ccol = own("ccol", [P, NS, KD])
        csilu = own("csilu", [P, NS, KD])
        cvec = own("cvec", [P, 4 * (KD - 1) + P], F32R)
        mod = own("mod", [P, 4, KD, NS])
        vecT = own("vecT", [P, 6, KD])
        rms = own("rms", [P, 16])
        diag = own("diag", [P, NS, P])
        wr = place("wr", [P, KD, NG + NE], B + 13 * KB)
        wrs = own("wrs", [P, KD, 2, NG + NE], F32R)
        br = own("br", [P, NG + NE])
        lg = own("lg", [P, NS, NG + NE])
        rt = own("rt", [P, 160])
        comb = own("comb", [P, NS, NE])
        chosen = own("chosen", [P, NS, NE])
        key = own("key", [P, NS, NE + PAIR])
        slot_w = own("slot_w", [P, PAIR])
        rounds = own("rounds", [P, 1], mybir.dt.int32)
        smx = own("smx", [P, 8])

        ident = cst_all[:, C_ID:C_ID + P]
        dftn = cst_all[:, C_DFTN:C_DFTC]
        dftc = cst_all[:, C_DFTC:C_MASK].rearrange("p (h c n) -> p h c n", h=2, c=2)
        mask = cst_all[:, C_MASK:C_SEL]
        first = cst_all[:, C_FIRST:C_ALL]

        bank = [ctx.enter_context(nc.psum_tensor(f"bank{i}", [P, COL], F32)) for i in range(8)]
        adaP, modP = bank[7], bank[6]

        raw_landed = [sem(f"raw_landed{i}") for i in range(RAW)]
        hi_ready, lo_ready, unit_used = sem("hi_ready"), sem("lo_ready"), sem("unit_used")
        slots_freed = sem("slots_freed")
        consts_in, cond_in, x_in, rows_in, router_in = (
            sem("consts_in"), sem("cond_in"), sem("x_in"), sem("rows_in"), sem("router_in"))
        rpb_in, skew_out, bias_in = sem("rpb_in"), sem("skew_out"), sem("bias_in")
        pad_zero, cvec_ready, csilu_ready = sem("pad_zero"), sem("cvec_ready"), sem("csilu_ready")
        vecT_done, vecT_ready = sem("vecT_done"), sem("vecT_ready")
        squares_done, diag_ready, mod_ready = sem("squares_done"), sem("diag_ready"), sem("mod_ready")
        var_ready, root_ready = sem("var_ready"), sem("root_ready")
        norm_done, htmp_ready, h_ready = sem("norm_done"), sem("htmp_ready"), sem("h_ready")
        ada_evac, modrow_ready, modT_done, modT_evac = (
            sem("ada_evac"), sem("modrow_ready"), sem("modT_done"), sem("modT_evac"))
        bin_landed = [sem("bin_landed0"), sem("bin_landed1")]
        proj_evac = sem("proj_evac")
        dft1_done, dft1_act, dft1_dve = sem("dft1_done"), sem("dft1_act"), sem("dft1_dve")
        dft2_done, dft2_hi, dft2_lo = sem("dft2_done"), sem("dft2_hi"), sem("dft2_lo")
        head_staged = sem("head_staged")
        ctx_landed = [sem("ctx_landed0"), sem("ctx_landed1")]
        qk_done, qkT_ready, kcT_ready = sem("qk_done"), sem("qkT_ready"), sem("kcT_ready")
        scores_done, scores_ready, exp_done, probs_ready = (
            sem("scores_done"), sem("scores_ready"), sem("exp_done"), sem("probs_ready"))
        prT_done, prT_ready, pv_done, o_hi_ready, o_ready = (
            sem("prT_done"), sem("prT_ready"), sem("pv_done"), sem("o_hi_ready"), sem("o_ready"))
        gate_pre, gate_sig, merged_ready = sem("gate_pre"), sem("gate_sig"), sem("merged_ready")
        mT_done, m_hi_ready, m_ready = sem("mT_done"), sem("m_hi_ready"), sem("m_ready")
        x1_in, gab_ready, x1_ready = (
            sem("x1_in"), sem("gab_ready"), sem("x1_ready"))
        wrs_ready, route_done, y_zero = sem("wrs_ready"), sem("route_done"), sem("y_zero")
        silu_ready, hid_ready = sem("silu_ready"), sem("hid_ready")
        routing_in, chosen_ready, rank_done, rounds_ready = (
            sem("routing_in"), sem("chosen_ready"), sem("rank_done"), sem("rounds_ready"))
        back_done, back_act = sem("back_done"), sem("back_act")
        pick_ready, pickT_done, pickT_ready, slot_w_done, slot_w_ready = (
            sem("pick_ready"), sem("pickT_done"), sem("pickT_ready"), sem("slot_w_done"), sem("slot_w_ready"))
        gather_done, xg_ready, gu_ready, guT_done = (
            sem("gather_done"), sem("xg_ready"), sem("gu_ready"), sem("guT_done"))
        key_moved, rounds_done, tail_step = sem("key_moved"), sem("rounds_done"), sem("tail_step")
        x2_ready, chunk_squares = sem("x2_ready"), sem("chunk_squares")
        pickd_ready, hid_split, hidT_ready = sem("pickd_ready"), sem("hid_split"), sem("hidT_ready")
        d_ready, scatter_done = sem("d_ready"), sem("scatter_done")
        y_added = sem("y_added")
        route_arg, route_exp = sem("route_arg"), sem("route_exp")
        gfin_in, ga2_done, y_ready, out_sent, kv_sent = (
            sem("gfin_in"), sem("ga2_done"), sem("y_ready"), sem("out_sent"), sem("kv_sent"))
        dve_step, act_step = sem("dve_step"), sem("act_step")

        U_ADA1 = 0
        U_PROJ = U_ADA1 + 8 * CHUNK_UNITS
        U_ATT = U_PROJ + 16 * CHUNK_UNITS
        U_MERGE = U_ATT + 8 * CHUNK_UNITS
        U_OUT = U_MERGE + 4 * 24
        U_MOE = U_OUT + 4 * CHUNK_UNITS
        U_ROUND = NE * 3 * CHUNK_UNITS
        FILLS = 4 + 8 * PAIRS
        DOWN = [(0, 0), (0, 1), (1, 0), (1, 1), (0, 2), (0, 3), (1, 2), (1, 3)]

        def sequence(mode):
            gu = [[("gu", x, v) for v in range(16)] for x in range(PAIR)]
            dn = [("dn", q, uu) for q in range(8) for uu in range(2)]
            if mode == "first":
                return gu[0] + gu[1]
            if mode == "last":
                return dn
            return [unit for x in range(PAIR) for g in range(4)
                    for unit in gu[x][4 * g:4 * g + 4] + dn[2 * (4 * x + g):2 * (4 * x + g) + 2]]

        def steps(engine, r, run):
            first = r * U_ROUND + U_MOE
            run("first", 0, r * PAIRS, first)
            with engine.Fori(1, PAIRS) as p:
                run("both", p, r * PAIRS + p, p * 48 + first - 16)
            run("last", PAIRS, r * PAIRS + PAIRS, first + U_ROUND - 16)

        SCATTER = {"first": {}, "both": {("gu", 0, 13): 0, ("gu", 1, 1): 1, ("gu", 1, 13): 2},
                   "last": {("dn", 3, 0): 0, ("dn", 4, 0): 1, ("dn", 7, 0): 2}}
        ADD = {"first": {}, "both": {("gu", 0, 14): 0, ("gu", 1, 2): 1, ("gu", 1, 14): 2},
               "last": {("dn", 3, 1): 0, ("dn", 4, 1): 1, ("dn", 7, 1): 2}}

        def round_count(engine):
            engine.wait_ge(rounds_ready, 1)
            return engine.value_load(rounds[0:1, 0:1], min_val=1, max_val=NS * TOK // CAP)

        block = ctx.enter_context(nc.Block())

        @block.sync
        def _(sp):
            def load(view, k0, col, first_load, j, wait=True):
                if wait:
                    sp.wait_ge(lo_ready, 2 * (first_load + j - RAW + 1))
                    sp.sem_inc(slots_freed, 1)
                sp.dma_start(raw[:, j % RAW], view[:, bass.ds(k0, LOAD_K), bass.ds(col, COL)]
                             ).then_inc(raw_landed[j % RAW], 16)

            def chunk(view, tiles, col, first_load, j, k0=0, wait=True):
                for n in range(tiles // LOAD_K):
                    load(view, k0 + LOAD_K * n, col, first_load, j + n, wait)

            chunk(ada_v, KD, 0, 0, 0, wait=False)
            with sp.Fori(1, 8) as i:
                chunk(ada_v, KD, i * COL, i * 4, 0)
            with sp.Fori(0, 4) as i:
                base = i * 16 + U_PROJ // 2
                chunk(ada_v, KD, i * COL + 2 * D, base, 0)
                chunk(in_v, KD, i * (2 * COL), base, 4)
                chunk(ada_v, KD, i * COL + 3 * D, base, 8)
                chunk(in_v, KD, i * (2 * COL) + COL, base, 12)
            with sp.Fori(0, 4) as i:
                base = i * 8 + U_ATT // 2
                chunk(ada_v, KD, i * COL + 4 * D, base, 0)
                chunk(ada_v, KD, i * COL + 5 * D, base, 4)
            with sp.Fori(0, 4) as i:
                base = i * 12 + U_MERGE // 2
                chunk(in_v, KD, i * COL + FW + 3 * NA, base, 0)
                chunk(in_v, KD, i * COL + FW + 3 * NA + D, base, 4)
                chunk(fo_v, KF, i * COL, base, 8)
                chunk(na_v, KF, i * COL, base, 10)
            with sp.Fori(0, 4) as i:
                chunk(out_v, KD, i * COL, i * 4 + U_OUT // 2, 0)
            def step_loads(mode, p, first_load, numbers):
                for n in numbers:
                    kind, a, b = sequence(mode)[2 * n]
                    if kind == "gu":
                        load((gate_v, up_v)[b // 8], (p * PAIR + a) * KD + b % 8 // 2 * LOAD_K, 0, first_load, n)
                    else:
                        x, col = DOWN[a]
                        load(down_v, (p * PAIR + x - PAIR) * KE, col * COL, first_load, n)

            step_loads("first", 0, U_MOE // 2, range(2))
            with sp.Fori(0, round_count(sp)) as r:
                base = r * (U_ROUND // 2) + U_MOE // 2
                step_loads("first", 0, base, range(2, 16))
                with sp.Fori(1, PAIRS) as p:
                    step_loads("both", p, p * 24 + base - 8, range(24))
                step_loads("last", PAIRS, base + U_ROUND // 2 - 8, range(8))
                step_loads("first", 0, base + U_ROUND // 2, range(2))
            for n in range(D // COL):
                for s in range(NS):
                    sp.wait_ge(y_ready, n * NS + s + 1)
                    sp.dma_start(y_v[s][:, n * COL:(n + 1) * COL],
                                 x1[:, s, n * COL:(n + 1) * COL]).then_inc(out_sent, 16)
            sp.wait_ge(out_sent, 16 * NS * (D // COL))
            sp.wait_ge(kv_sent, 32)

        @block.gpsimd
        def _(pool):
            nc.gpsimd.memset(rpbpad[:], 0.0).then_inc(pad_zero, 1)
            pool.dma_start(cst_all[:], constants).then_inc(consts_in, 16)
            pool.wait_ge(h_ready, 1)
            pool.wait_ge(pad_zero, 1)
            for h in range(HEADS):
                pool.dma_start(rpbpad[3 * h:3 * h + 3, 48:48 + 2 * WIN - 1], rpb[0, h, 6:9, :]).then_inc(rpb_in, 16)
            pool.dma_start(wr[:, :, 0:NG], rg_v).then_inc(router_in, 16)
            pool.dma_start(wr[:, :, NG:], re_v).then_inc(router_in, 16)
            pool.dma_start(br[:, 0:NG], b_rg[0].partition_broadcast(P)).then_inc(router_in, 16)
            pool.dma_start(br[:, NG:], b_re[0].partition_broadcast(P)).then_inc(router_in, 16)
            pool.wait_ge(rpb_in, 16 * HEADS)
            sk = skew.ap()
            pool.dma_start(sk.rearrange("c r j -> r c j"),
                           bass.AP(rpbpad.tensor, rpbpad.offset, [list(rpbpad.ap[0]), [0, GRID_W], [1, P]])
                           ).then_inc(skew_out, 16)
            pool.wait_ge(skew_out, 16)
            for r in range(ROWS):
                for kr in range(ROWS):
                    pool.dma_start(bias[r * GRID_W:(r + 1) * GRID_W, :, kr],
                                   bass.AP(sk.tensor, (1 - r + kr) * P + GRID_W - 1,
                                           [[NR * P - 1, GRID_W], [3 * P, HEADS], [1, GRID_W]])
                                   ).then_inc(bias_in, 16)

            def load_bin(col, j):
                pool.dma_start(bin_[:, j], b_in[0, bass.ds(col, COL)].partition_broadcast(P)
                               ).then_inc(bin_landed[j], 16)

            for j in range(2):
                load_bin(j * COL, j)
            with pool.Fori(0, 3) as i:
                for j in range(2):
                    pool.wait_ge(proj_evac, i * 2 + j + 1 + ONE)
                    load_bin(i * (2 * COL) + (2 + j) * COL, j)
            pool.wait_ge(proj_evac, 8 + ONE)
            for n, dst in enumerate((new_k, new_v)):
                pool.dma_start(dst.rearrange("a l t h d -> (a l t) (h d)"),
                               uqkv[:, 0, FW + (1 + n) * NA:FW + (2 + n) * NA]).then_inc(kv_sent, 16)

            heads = uqkv[:].rearrange("p s (c h d) -> p s c h d", c=4, h=HEADS)

            def stage(h, j):
                pool.dma_start(cst[:, j, 0:1], kc_v[:, bass.ds(h, 1), :]).then_inc(ctx_landed[j], 16)
                pool.dma_start(cst[:, j, 1:2], vc_v[:, bass.ds(h, 1), :]).then_inc(ctx_landed[j], 16)
                for s in range(NS):
                    copy = nc.gpsimd.tensor_copy(st[:, j, s].rearrange("p c (a d) -> p c a d", a=1), heads[:, s, 1:4, bass.ds(h, 1), :])
                copy.then_inc(head_staged, 1)

            pool.wait_ge(dft2_done, 4)
            for j in range(2):
                stage(j, j)
            pool.dma_start(cst_route[:], routing).then_inc(routing_in, 16)
            with pool.Fori(0, 3) as i:
                for j in range(2):
                    pool.wait_ge(pv_done, i * 2 + j + 1)
                    stage(i * 2 + 2 + j, j)
            load_col = FW + 3 * NA
            for j in range(2):
                load_bin(load_col + j * D, j)
            with pool.Fori(0, 3) as i:
                for j in range(2):
                    pool.wait_ge(gate_pre, i * 2 + j + 1)
                    load_bin(i * COL + COL + load_col + j * D, j)
            pool.wait_ge(unit_used, U_OUT)
            for s in range(NS):
                pool.dma_start(x1[:, s], x_v[s]).then_inc(x1_in, 16)
            nc.gpsimd.memset(ysum[:], 0.0).then_inc(y_zero, 1)
            pool.wait_ge(back_done, 16)
            pool.dma_start(gfin[:], final_g.partition_broadcast(P)).then_inc(gfin_in, 16)
            pool.wait_ge(routing_in, 16)
            pool.wait_ge(skew_out, 16)

        @block.tensor
        def _(pe):
            def unit(n0, u, products):
                pe.wait_ge(lo_ready, n0 + u + 1)
                for t in range(UNIT_K):
                    last = products(t, w_hi[:, u % AHEAD, t], w_lo[:, u % AHEAD, t])
                last.then_inc(unit_used, 1)
                return last

            def ada_chunk(n0, u0, chunk):
                pe.wait_ge(ada_evac, chunk + ONE)
                for u in range(CHUNK_UNITS):
                    def products(t, wh, wl):
                        k = UNIT_K * u + t
                        lhs = cvec[:, 4 * k:4 * k + P]
                        nc.tensor.matmul(adaP[:], lhs, wh, start=k == 0, stop=False)
                        return nc.tensor.matmul(adaP[:], lhs, wl, start=False, stop=k == KD - 1)
                    unit(n0, u0 + u, products)

            def split_units(n0, u0, units, hi, lo, banks, k_all, between=None, last_tiles=None):
                for u in range(units):
                    if u == 2 and between:
                        between()
                    if u == units - 2 and last_tiles:
                        last_tiles()
                    def products(t, wh, wl):
                        k = UNIT_K * u + t
                        for s in range(NS):
                            o = bank[banks[s]][:]
                            nc.tensor.matmul(o, hi[:, k, s], wh, start=k == 0, stop=False)
                            nc.tensor.matmul(o, hi[:, k, s], wl, start=False, stop=False)
                            last = nc.tensor.matmul(o, lo[:, k, s], wh, start=False, stop=k == k_all - 1)
                        return last
                    unit(n0, u0 + u, products)

            for starts_at_one in (modT_done, mT_done, scatter_done, pickT_done):
                pe.sem_inc(starts_at_one, ONE)
            pe.wait_ge(consts_in, 16)
            pe.wait_ge(rows_in, 16 * 4)
            nc.tensor.transpose(bank[0][:, 0:6 * KD], vecrows[:], ident[0:6 * KD, 0:6 * KD]).then_inc(vecT_done, 1)
            pe.wait_ge(cvec_ready, 1)

            def modT(n):
                pe.wait_ge(modrow_ready, n + 1)
                pe.wait_ge(modT_evac, n + ONE)
                for b in range(COL // P):
                    last = nc.tensor.matmul(modP[:, b * NS:(b + 1) * NS], modrow[0:4, b * P:(b + 1) * P],
                                            cst_all[0:4, C_SEL:C_SEL + NS], start=True, stop=True)
                last.then_inc(modT_done, 1)

            with pe.Fori(0, 8) as i:
                ada_chunk(i * CHUNK_UNITS, 0, i)
                modT(i)

            def norm_transposes(x, n):
                pe.wait_ge(diag_ready, n)
                for b in range(8):
                    s, g = b % NS, b // NS
                    for j in range(4):
                        k = 4 * g + j
                        last = nc.tensor.matmul(bank[b][:, j * P:(j + 1) * P], x[:, s, k * P:(k + 1) * P],
                                                diag[:, s], start=True, stop=True)
                    last.then_inc(norm_done, 1)

            pe.wait_ge(ada_evac, 8 + ONE)
            pe.wait_ge(modT_evac, 8 + ONE)
            pe.wait_ge(vecT_ready, 1)
            norm_transposes(x0, 1)
            pe.wait_ge(h_ready, 8)
            with pe.Fori(0, 4) as i:
                n0 = i * (4 * CHUNK_UNITS) + U_PROJ
                for j in range(2):
                    ada_chunk(n0, 2 * j * CHUNK_UNITS, i * 2 + 8 + j)
                    pe.wait_ge(proj_evac, i * 2 + ONE)
                    split_units(n0, (2 * j + 1) * CHUNK_UNITS, CHUNK_UNITS, h_hi, h_lo, (2 * j, 2 * j + 1), KD)
                modT(i + 8)
            pe.wait_ge(proj_evac, 8 + ONE)
            pe.wait_ge(ada_evac, 16 + ONE)
            pe.wait_ge(modT_evac, 12 + ONE)
            pe.wait_ge(skew_out, 16)
            pe.wait_ge(wrs_ready, 1)
            for b in range(8):
                for s in range(NS):
                    last = nc.tensor.matmul(bank[b][:, s * 256:(s + 1) * 256], uqkv[:, s, b * P:(b + 1) * P],
                                            dftn, start=True, stop=True)
                last.then_inc(dft1_done, 1)
            pe.wait_ge(dft1_act, 4)
            pe.wait_ge(dft1_dve, 4)
            for o in range(4):
                hh, gp = o % 2, o // 2
                for n in range(4):
                    half, cs = n // 2, n % 2
                    last = nc.tensor.matmul(bank[o][:], dftc[:, half, cs, hh * P:(hh + 1) * P],
                                            fa[:, half, cs, 2 * gp:2 * gp + 2], start=n == 0, stop=n == 3)
                last.then_inc(dft2_done, 1)
            pe.wait_ge(dft2_lo, 4)
            def transpose_probs(h):
                pe.wait_ge(probs_ready, h + 1)
                for n in range(3):
                    last = nc.tensor.transpose(bank[3][:, n * P:(n + 1) * P], prb[:, n], ident)
                last.then_inc(prT_done, 1)

            def probs_values(h, j):
                pe.wait_ge(prT_ready, h + 1)
                pe.wait_ge(o_ready, h + ONE)
                nc.tensor.matmul(bank[4][:, 0:P], st[:, j, 0, 2], prT[:, 0], start=True, stop=True)
                nc.tensor.matmul(bank[4][:, P:2 * P], cst[:, j, 1], prT[:, 1], start=True, stop=False)
                nc.tensor.matmul(bank[4][:, P:2 * P], st[:, j, 1, 2], prT[:, 2],
                                 start=False, stop=True).then_inc(pv_done, 1)

            def head_pair(i, first):
                n0 = i * (2 * CHUNK_UNITS) + U_ATT
                for j in range(2):
                    h = i * 2 + j
                    pe.wait_ge(ada_evac, i * 2 + 16 + j + ONE)
                    for u in range(CHUNK_UNITS):
                        if u == 1:
                            pe.wait_ge(head_staged, h + 1)
                            pe.wait_ge(ctx_landed[j], (i + 1) * 32)
                            for n in range(4):
                                nc.tensor.transpose(bank[0][:, n * P:(n + 1) * P], st[:, j, n // 2, n % 2], ident)
                            nc.tensor.transpose(bank[1][:, 0:P], cst[:, j, 0], ident).then_inc(qk_done, 1)
                            if j or not first:
                                transpose_probs(h - 1)
                        if u == 3 and (j or not first):
                            probs_values(h - 1, 1 - j)
                        if u == 4:
                            pe.wait_ge(qkT_ready, h + 1)
                            pe.wait_ge(kcT_ready, h + 1)
                            nc.tensor.matmul(bank[2][:, 0:P], qkT[:, 0], qkT[:, 1], start=True, stop=True)
                            nc.tensor.matmul(bank[2][:, P:2 * P], qkT[:, 2], kcT[:], start=True, stop=True)
                            nc.tensor.matmul(bank[2][:, 2 * P:3 * P], qkT[:, 2], qkT[:, 3],
                                             start=True, stop=True).then_inc(scores_done, 1)
                        def products(t, wh, wl):
                            k = UNIT_K * u + t
                            lhs = cvec[:, 4 * k:4 * k + P]
                            nc.tensor.matmul(adaP[:], lhs, wh, start=k == 0, stop=False)
                            return nc.tensor.matmul(adaP[:], lhs, wl, start=False, stop=k == KD - 1)
                        unit(n0, j * CHUNK_UNITS + u, products)
                    if j == 0:
                        modT(i + 12)

            head_pair(0, True)
            with pe.Fori(1, HEADS // 2) as i:
                head_pair(i, False)

            def last_head():
                transpose_probs(HEADS - 1)
                probs_values(HEADS - 1, 1)

            pe.wait_ge(ada_evac, 24 + ONE)
            pe.wait_ge(modT_evac, 16 + ONE)
            def merged_transposes(i):
                pe.wait_ge(merged_ready, i + 1)
                for s in range(NS):
                    for b in range(4):
                        last = nc.tensor.transpose(bank[4 + s][:, b * P:(b + 1) * P],
                                                   ma[:, s, b * P:(b + 1) * P], ident)
                    last.then_inc(mT_done, 1)

            def merge_chunk(i, first):
                n0 = i * 24 + U_MERGE
                split_units(n0, 0, 8, h_hi, h_lo, (0, 1), KD,
                            last_head if first else lambda: merged_transposes(i - 1))
                split_units(n0, 8, 8, h_hi, h_lo, (2, 3), KD)
                pe.wait_ge(m_ready, i * 2 + ONE)
                pe.wait_ge(o_ready, HEADS + ONE)
                split_units(n0, 16, 4, f_hi, f_lo, (4, 5), KF)
                split_units(n0, 20, 4, o_hi, o_lo, (6, 7), KF)

            merge_chunk(0, True)
            with pe.Fori(1, D // COL) as i:
                merge_chunk(i, False)
            def last_merged():
                pe.wait_ge(m_ready, 8 + ONE)

            def out_pair(i, first):
                for j in range(2):
                    n0 = i * 16 + U_OUT
                    pe.wait_ge(x1_ready, i * 2 + ONE)
                    for s in range(NS):
                        nc.tensor.matmul(bank[4 * j + 2 + s][:], cst_all[0:5, C_SELB + s * P:C_SELB + (s + 1) * P],
                                         garow[0:5, bass.ds(i * (2 * COL) + j * COL, COL)], start=True, stop=True)
                    if first and j == 0:
                        split_units(n0, 0, 8, m_hi, m_lo, (0, 1), KD,
                                    lambda: merged_transposes(D // COL - 1), last_merged)
                    else:
                        split_units(n0, 8 * j, 8, m_hi, m_lo, (4 * j, 4 * j + 1), KD)

            out_pair(0, True)
            with pe.Fori(1, D // COL // 2) as i:
                out_pair(i, False)
            pe.wait_ge(x1_ready, 4 + ONE)
            norm_transposes(x1, 2)
            for b in range(8):
                s = b % NS
                pe.wait_ge(h_ready, 8 + max(b + 1, NS))
                for k in range(b // NS * 4, b // NS * 4 + 4):
                    for part in (h_hi, h_lo):
                        last = nc.tensor.matmul(bank[s][:, 0:2 * (NG + NE)], part[:, k, s], wrs[:, k],
                                                start=k == 0 and part is h_hi, stop=k == KD - 1 and part is h_lo)
            last.then_inc(route_done, 1)
            for f in range(16):
                s, part, g = f // 8, f // 4 % 2, f % 4
                if f >= 6:
                    pe.wait_ge(back_act, f - 5)
                for j in range(4):
                    last = nc.tensor.transpose(bank[2 + f % 6][:, j * P:(j + 1) * P],
                                               (h_hi, h_lo)[part][:, 4 * g + j, s].bitcast(F32), ident)
                last.then_inc(back_done, 1)
            pe.wait_ge(chosen_ready, 1)
            pe.wait_ge(routing_in, 16)
            before, ones = cst_route[:, R_BEFORE:R_ONES], cst_route[:, R_ONES:R_SLOT]
            nc.tensor.matmul(bank[0][:, 0:NE], before, chosen[:, 0], start=True, stop=True)
            nc.tensor.matmul(bank[0][:, NE:2 * NE], before, chosen[:, 1], start=True, stop=False)
            nc.tensor.matmul(bank[0][:, NE:2 * NE], ones, chosen[:, 0], start=False, stop=True)
            nc.tensor.matmul(bank[0][:, 2 * NE:3 * NE], ones, chosen[:, 0], start=True, stop=False)
            nc.tensor.matmul(bank[0][:, 2 * NE:3 * NE], ones, chosen[:, 1], start=False, stop=True
                             ).then_inc(rank_done, 1)
            pe.wait_ge(back_act, 16)

            def gather(x, f, out):
                o = out[:].rearrange("p (k h c) -> p k h c", k=4, h=2)
                for kk in range(4):
                    for part in range(2):
                        for s in range(NS):
                            last = nc.tensor.matmul(o[:, kk, part], (t_hi, t_lo)[part][:, s, (4 * f + kk) * P:(4 * f + kk + 1) * P],
                                                    pick_[:, x, s], start=s == 0, stop=s == 1)
                last.then_inc(gather_done, 1)

            R = round_count(pe)
            with pe.Fori(0, R) as r:
                pe.wait_ge(pick_ready, r * (2 * PAIRS + 2) + 1)
                pe.wait_ge(pickT_ready, r * PAIRS + ONE)
                for f in range(4):
                    gather(0, f, bank[(7, 3, 4, 2)[f]])

                def run(mode, p, n, n0):
                    fill = r * FILLS + p * 8 + 4

                    def product(u, stationary, out, k, k_all):
                        def products(t, wh, wl):
                            lhs = stationary(k + t)
                            nc.tensor.matmul(out, lhs, wh, start=k + t == 0, stop=False)
                            return nc.tensor.matmul(out, lhs, wl, start=False, stop=k + t == k_all - 1)
                        unit(n0, u, products)

                    def transpose_sum(x):
                        pe.wait_ge(gu_ready, n * 4 + 2 * x + 2 + ONE)
                        pe.wait_ge(hid_ready, n * 2 + x + ONE)
                        for m in range(2):
                            for k in range(KE):
                                last = nc.tensor.matmul(bank[2][:, m * 256 + k * CAP:m * 256 + (k + 1) * CAP],
                                                        gu[:, m, k * P:(k + 1) * P], cst_route[:, R_SUM:R_ALL],
                                                        start=True, stop=True)
                        last.then_inc(guT_done, 1)

                    def scatter(c):
                        pe.wait_ge(d_ready, n * 8 + (3, 4, 7, 8)[c] - 8)
                        pe.wait_ge(y_added, n * 4 + c - 4 + ONE)
                        for s in range(NS):
                            for x in range(PAIR):
                                last = nc.tensor.matmul(bank[5 + s][:], pickT[:, x, s], dsb[:, x, c % 2],
                                                        start=x == 0, stop=x == 1)
                        last.then_inc(scatter_done, 1)

                    for u, item in enumerate(sequence(mode)):
                        kind, a, b = item
                        if kind == "gu":
                            x, v = a, b
                            if v == 0:
                                pe.wait_ge(xg_ready, fill + 4 * x + ONE)
                            if v % 8 == 0:
                                pe.wait_ge(gu_ready, n * 4 + (x + v // 8 if x else 0) + ONE)
                            if x == 0 and v == 8:
                                pe.wait_ge(slot_w_ready, n + ONE)
                            product(u, lambda k: xg[:, x, k].rearrange("p h c -> p (h c)"), bank[v // 8][:],
                                    UNIT_K * (v % 8), KD)
                            if v % 4 == 1:
                                f = v // 4
                                if f == 0:
                                    pe.wait_ge(pick_ready, n * 2 + r * 2 + 2 + x)
                                    pe.wait_ge(pickT_ready, n + ONE)
                                pe.wait_ge(xg_ready, fill + 4 * x + f + ONE)
                                gather(1 - x, f, bank[7])
                            if (x, v) == (1, 1):
                                transpose_sum(0)
                        else:
                            q, uu = a, b
                            x, col = DOWN[q]
                            if q == 0 and uu == 0:
                                pe.wait_ge(hidT_ready, n)
                                pe.wait_ge(pickT_ready, n + ONE)
                            if q >= 2 and uu == 0:
                                pe.wait_ge(d_ready, n * 8 + q - 1 - 8)
                            product(u, lambda k: hidT[:, x, k].rearrange("p h c -> p (h c)"), bank[3 + q % 2][:],
                                    UNIT_K * uu, KE)
                        if item in SCATTER[mode]:
                            scatter(SCATTER[mode][item])
                    if mode != "last":
                        transpose_sum(1)
                        pe.wait_ge(pickd_ready, n + 1)
                        for x in range(PAIR):
                            for s in range(NS):
                                last = nc.tensor.matmul(bank[1][:, x:x + 1], pickd[:, x, s].rearrange("p h c -> p (h c)"),
                                                        comb[:, s, bass.ds(p * PAIR + x, 1)], start=s == 0, stop=s == 1)
                        last.then_inc(slot_w_done, 1)
                    if mode != "first":
                        scatter(3)
                    if mode != "last":
                        pe.wait_ge(xg_ready, fill + 8 + ONE)
                        for x in range(PAIR):
                            for s in range(NS):
                                last = nc.tensor.transpose(bank[7][:, (x * NS + s) * P:(x * NS + s + 1) * P],
                                                           pickd[:, x, s].rearrange("p h c -> p (h c)"), ident)
                        last.then_inc(pickT_done, 1)

                steps(pe, r, run)
            pe.wait_ge(rounds_done, 1)
            pe.wait_ge(pickT_ready, R * PAIRS + ONE)
            for n in range(D // COL):
                for s in range(NS):
                    nc.tensor.matmul(bank[NS * n + s][:], cst_all[32:37, C_SELB + s * P:C_SELB + (s + 1) * P],
                                     garow[32:37, n * COL:(n + 1) * COL], start=True, stop=True).then_inc(ga2_done, 1)

        @block.scalar
        def _(act):
            step = Tally(act, act_step)
            for starts_at_one in (ada_evac, gu_ready, xg_ready, slot_w_ready, pickT_ready):
                act.sem_inc(starts_at_one, ONE)

            def high(n0, u, wait=True):
                if u % 2 == 0:
                    slot = (u // 2) % RAW
                    act.wait_ge(raw_landed[slot], landed(n0, u))
                if wait:
                    act.wait_ge(unit_used, n0 + u - AHEAD + 1)
                r = raw[:, (u // 2) % RAW, (u % 2) * UNIT_K:(u % 2) * UNIT_K + UNIT_K]
                nc.scalar.activation(w_hi[:, u % AHEAD], r, ACT.Copy).then_inc(hi_ready, 1)

            def landed(n0, u):
                return n0 * 2 + 16 * (u // (2 * RAW) + 1)

            for s in range(NS):
                act.dma_start(ccol[:, s], (c_ctx, c)[s].rearrange("(p k) -> p k", k=KD) if s == 0
                              else c.rearrange("a (p k) -> p (a k)", k=KD)).then_inc(cond_in, 16)
            for s in range(NS):
                act.dma_start(x0[:, s], x_v[s]).then_inc(x_in, 16)
            for n, src in enumerate((b_ada[0, 0:2 * D], b_ada[0, 3 * D:5 * D])):
                act.dma_start(vecrows[2 * KD * n:2 * KD * (n + 1)], src.rearrange("(r c) -> r c", c=P)
                              ).then_inc(rows_in, 16)
            for n, src in enumerate((norm1_g, norm2_g)):
                act.dma_start(vecrows[(4 + n) * KD:(5 + n) * KD], src.rearrange("l (r c) -> (l r) c", c=P)
                              ).then_inc(rows_in, 16)
            act.dma_start(garow[4:5], b_ada[0:1, 2 * D:3 * D]).then_inc(x_in, 16)
            act.dma_start(garow[36:37], b_ada[0:1, 5 * D:6 * D]).then_inc(x_in, 16)
            act.wait_ge(cond_in, 32)
            nc.scalar.activation(csilu[:], ccol[:], ACT.Silu).then_inc(csilu_ready, 1)

            def root(col, n):
                act.wait_ge(var_ready, n)
                nc.scalar.activation(rms[:, col + 2:col + 4], rms[:, col:col + 2], ACT.Sqrt).then_inc(root_ready, 1)

            def sum_squares(x, col, n):
                for s in range(NS):
                    ins = nc.scalar.activation(squares[:], x[:, s], ACT.Square, accum_out=rms[:, col + s:col + s + 1])
                    if s == 0:
                        step.mark(ins)
                        step.settle()
                ins.then_inc(squares_done, 1)
                root(col, n)

            for u in range(AHEAD):
                high(0, u, wait=False)
            act.wait_ge(x_in, 64)
            sum_squares(x0, 0, 1)

            def evac_mod_rows(end, n):
                act.wait_ge(unit_used, end)
                act.wait_ge(modT_done, n + ONE)
                nc.scalar.activation(modrow[0:4], adaP[0:4, :], ACT.Copy).then_inc(modrow_ready, 1)
                act.wait_ge(modrow_ready, n + 1)
                act.sem_inc(ada_evac, 1)

            def evac_gate_rows(end, row, col):
                act.wait_ge(unit_used, end)
                nc.scalar.activation(garow[row:row + 4, bass.ds(col, COL)], adaP[0:4, :], ACT.Copy
                                     ).then_inc(ada_evac, 1)

            with act.Fori(0, 8) as i:
                for u in range(CHUNK_UNITS):
                    high(i * CHUNK_UNITS, u + AHEAD)
                evac_mod_rows(i * CHUNK_UNITS + CHUNK_UNITS, i)

            def apply_norm(g, sh, n):
                act.wait_ge(mod_ready, n)
                for b in range(8):
                    s, kg = b % NS, b // NS
                    act.wait_ge(norm_done, 8 * (n - 1) + b + 1)
                    if b >= 2:
                        act.wait_ge(h_ready, 8 * (n - 1) + b - 1)
                    for j in range(4):
                        k = 4 * kg + j
                        ins = nc.scalar.activation(htmp[:, b % 2, j], bank[b][:, j * P:(j + 1) * P], ACT.Identity,
                                                   bias=mod[:, sh, k, s:s + 1], scale=mod[:, g, k, s:s + 1])
                    ins.then_inc(htmp_ready, 1)

            apply_norm(1, 0, 1)
            with act.Fori(0, 4) as i:
                n0 = i * (4 * CHUNK_UNITS) + U_PROJ
                for q in range(4):
                    for u in range(CHUNK_UNITS):
                        high(n0, q * CHUNK_UNITS + u + AHEAD)
                    if q == 0:
                        evac_gate_rows(n0 + CHUNK_UNITS, 0, i * COL)
                    if q == 2:
                        evac_mod_rows(n0 + 3 * CHUNK_UNITS, i + 8)
            for b in range(0, 8, 2):
                act.wait_ge(dft1_done, b + 1)
                nc.scalar.activation(fa[:, b % 2, :, b // 2].rearrange("p c s t -> p s c t"),
                                     bank[b][:].rearrange("p (s c t) -> p s c t", s=2, c=2), ACT.Copy
                                     ).then_inc(dft1_act, 1)
            for o in range(4):
                hh, gp = o % 2, o // 2
                act.wait_ge(dft2_done, o + 1)
                nc.scalar.activation(f_hi[:, 4 * gp + hh:4 * gp + hh + 3:2], bank[o][:].rearrange("p (g s t) -> p g s t", g=2, s=2),
                                     ACT.Copy).then_inc(dft2_hi, 1)

            def evac_probs(h):
                act.wait_ge(prT_done, h + 1)
                nc.scalar.activation(prT[:].rearrange("p c t -> p (c t)"), bank[3][:, 0:3 * P], ACT.Copy
                                     ).then_inc(prT_ready, 1)

            def output_high(h):
                act.wait_ge(pv_done, h + 1)
                nc.scalar.activation(o_hi[:, bass.ds(h, 1)],
                                     bank[4][:, 0:2 * P].rearrange("p (a s t) -> p a s t", a=1, s=2), ACT.Copy
                                     ).then_inc(o_hi_ready, 1)

            def head_pair(i, first):
                n0 = i * (2 * CHUNK_UNITS) + U_ATT
                for j in range(2):
                    h = i * 2 + j
                    for u in range(CHUNK_UNITS):
                        high(n0, j * CHUNK_UNITS + u + AHEAD)
                        if u == 1:
                            act.wait_ge(qk_done, h + 1)
                            nc.scalar.activation(qkT[:].rearrange("p c t -> p (c t)"), bank[0][:], ACT.Copy
                                                 ).then_inc(qkT_ready, 1)
                            if j or not first:
                                evac_probs(h - 1)
                        if u == 4 and (j or not first):
                            output_high(h - 1)
                        if u == 6:
                            act.wait_ge(scores_ready, h + 1)
                            nc.scalar.activation(prb[:, 0], scr[:, 0], ACT.Exp, bias=smx[:, 0:1],
                                                 accum_out=smx[:, 2:3])
                            nc.scalar.activation(prb[:, 1:3], scr[:, 1:3], ACT.Exp, bias=smx[:, 1:2],
                                                 accum_out=smx[:, 3:4]).then_inc(exp_done, 1)
                    if j == 0:
                        evac_mod_rows(n0 + CHUNK_UNITS, i + 12)
                    else:
                        evac_gate_rows(n0 + 2 * CHUNK_UNITS, 32, i * COL)

            head_pair(0, True)
            with act.Fori(1, HEADS // 2) as i:
                head_pair(i, False)
            evac_probs(HEADS - 1)
            output_high(HEADS - 1)
            act.wait_ge(kv_sent, 32)
            with act.Fori(0, 4) as i:
                n0 = i * 24 + U_MERGE
                for u in range(24):
                    high(n0, u + AHEAD)
                    if u in (8, 16):
                        g = ma if u == 8 else mb
                        act.wait_ge(gate_pre, i * 2 + u // 8)
                        nc.scalar.activation(g[:], g[:], ACT.Sigmoid).then_inc(gate_sig, 1)
                for s in range(NS):
                    act.wait_ge(mT_done, i * 2 + s + 1 + ONE)
                    nc.scalar.activation(m_hi[:, bass.ds(i * 4, 4), s], bank[4 + s][:].rearrange("p (k t) -> p k t", k=4),
                                         ACT.Copy).then_inc(m_hi_ready, 1)
            with act.Fori(0, 2) as i:
                for j in range(2):
                    n0 = i * 16 + U_OUT
                    for u in range(CHUNK_UNITS):
                        high(n0, 8 * j + u + AHEAD)
                    act.wait_ge(unit_used, n0 + 8 * j + 8)
                    for s in range(NS):
                        ins = nc.scalar.activation(gab[:, j, s], bank[4 * j + 2 + s][:], ACT.Copy)
                    ins.then_inc(gab_ready, 1)
            act.wait_ge(x1_ready, 4 + ONE)
            sum_squares(x1, 4, 2)
            apply_norm(3, 2, 2)

            for f in range(16):
                s, part, g = f // 8, f // 4 % 2, f % 4
                act.wait_ge(back_done, f + 1)
                nc.scalar.activation((t_hi, t_lo)[part][:, s, g * COL:(g + 1) * COL], bank[2 + f % 6][:], ACT.Copy
                                     ).then_inc(back_act, 1)
                if f in (4, 15):
                    act.wait_ge(route_arg, f // 15 + 1)
                    nc.scalar.activation(rt[:, 8:16], rt[:, 0:8], ACT.Exp).then_inc(route_exp, 1)

            def evac_gather(x, f, source, fill):
                act.wait_ge(gather_done, fill + 1)
                nc.scalar.activation(xg[:, x, 4 * f:4 * f + 4].rearrange("p k h c -> p (k h c)"), source[:],
                                     ACT.Copy).then_inc(xg_ready, 1)

            with act.Fori(0, round_count(act)) as r:
                for f in range(4):
                    evac_gather(0, f, bank[(7, 3, 4, 2)[f]], r * FILLS + f)

                def run(mode, p, n, n0):
                    fill = r * FILLS + p * 8 + 4

                    def silu(x):
                        act.wait_ge(guT_done, n * 2 + x + 1)
                        nc.scalar.activation(sgT[:].rearrange("p k c -> p (k c)"), bank[2][:, 0:256], ACT.Silu
                                             ).then_inc(silu_ready, 1)

                    for u, (kind, a, b) in enumerate(sequence(mode)):
                        high(n0, u + AHEAD)
                        if kind == "gu":
                            x, v = a, b
                            if v % 8 == 7:
                                act.wait_ge(unit_used, n0 + u + 1)
                                nc.scalar.activation(gu[:, v // 8], bank[v // 8][:], ACT.Copy).then_inc(gu_ready, 1)
                            if v % 4 == 2:
                                evac_gather(1 - x, v // 4, bank[7], fill + 4 * x + v // 4)
                            if (x, v) == (1, 2):
                                silu(0)
                        elif b == 1:
                            x, col = DOWN[a]
                            act.wait_ge(unit_used, n0 + u + 1)
                            if a == 0:
                                act.wait_ge(slot_w_ready, n + ONE)
                                act.wait_ge(scatter_done, n * 4 - 4 + ONE)
                            if a in (4, 5):
                                act.wait_ge(scatter_done, n * 4 - 4 + a - 3 + ONE)
                            nc.scalar.activation(dsb[:, x, col % 2], bank[3 + a % 2][:], ACT.Copy,
                                                 scale=slot_w[:, x:x + 1]).then_inc(d_ready, 1)
                    if mode != "first":
                        act.wait_ge(d_ready, n * 8)
                    if mode != "last":
                        silu(1)
                        act.wait_ge(slot_w_done, n + 1)
                        nc.scalar.activation(slot_w[:], bank[1][:, 0:PAIR], ACT.Copy).then_inc(slot_w_ready, 1)
                        act.wait_ge(pickT_done, n + 1 + ONE)
                        nc.scalar.activation(pickT[:].rearrange("p e s t -> p (e s t)"), bank[7][:], ACT.Copy
                                             ).then_inc(pickT_ready, 1)

                steps(act, r, run)
            for n in range(D // COL):
                cols = slice(n * COL, (n + 1) * COL)
                act.wait_ge(x2_ready, n + 1)
                for s in range(NS):
                    ins = nc.scalar.activation(ysum[:, s, cols], x1[:, s, cols], ACT.Square,
                                               accum_out=smx[:, NS * n + s:NS * n + s + 1])
                ins.then_inc(chunk_squares, 1)
            root(8, 3)

        @block.vector
        def _(dve):
            step = Tally(dve, dve_step)
            for starts_at_one in (modT_evac, proj_evac, m_ready, x1_ready, o_ready, y_added, hid_ready):
                dve.sem_inc(starts_at_one, ONE)
            v = nc.vector

            def low(n0, u):
                dve.wait_ge(hi_ready, n0 + u + 1)
                r = raw[:, (u // 2) % RAW, (u % 2) * UNIT_K:(u % 2) * UNIT_K + UNIT_K]
                v.tensor_tensor(w_lo[:, u % AHEAD], r, w_hi[:, u % AHEAD].bitcast(F32), ALU.subtract
                                ).then_inc(lo_ready, 1)

            def chained(ins):
                step.mark(ins)
                step.settle()

            chained(v.memset(cvec[:].bitcast(F32), 0.0))
            dve.wait_ge(csilu_ready, 1)
            parts = cvec[:, 0:4 * KD].rearrange("p (k c) -> p c k", c=4)
            chained(v.tensor_copy(parts[:, 0:2], csilu[:]))
            v.tensor_tensor(parts[:, 2:4], csilu[:], parts[:, 0:2].bitcast(F32), ALU.subtract).then_inc(cvec_ready, 1)
            for u in range(AHEAD):
                low(0, u)
            dve.wait_ge(vecT_done, 1)
            v.tensor_copy(vecT[:].rearrange("p v k -> p (v k)"), bank[0][:, 0:6 * KD]).then_inc(vecT_ready, 1)

            def inverse_rms(col, n):
                dve.wait_ge(squares_done, n)
                var, y, t = rms[:, col:col + 2], rms[:, col + 2:col + 4], rms[:, 12:14]
                v.tensor_scalar(var, var, 1.0 / D, EPS, ALU.mult, ALU.add).then_inc(var_ready, 1)
                dve.wait_ge(root_ready, n)
                chained(v.reciprocal(y, y))
                chained(v.tensor_tensor(t, y, y, ALU.mult))
                chained(v.tensor_tensor(t, t, var, ALU.mult))
                chained(v.tensor_scalar(t, t, -0.5, 1.5, ALU.mult, ALU.add))
                chained(v.tensor_tensor(y, y, t, ALU.mult))

            dve.wait_ge(consts_in, 16)
            inverse_rms(0, 1)
            for s in range(NS):
                chained(v.tensor_scalar(diag[:, s], ident, rms[:, 2 + s:3 + s], None, ALU.mult))
            dve.sem_inc(diag_ready, 1)
            def evac_modT(n):
                dve.wait_ge(modT_done, n + 1 + ONE)
                v.tensor_copy(modf[:, bass.ds(n * 4, 4)], modP[:, 0:4 * NS].rearrange("p (k s) -> p k s", s=NS)
                              ).then_inc(modT_evac, 1)

            modf = mod[:].rearrange("p v k s -> p (v k) s")

            def finish_mods(shift, scale, g, n):
                for s in range(NS):
                    v.tensor_tensor(mod[:, shift, :, s], mod[:, shift, :, s], vecT[:, shift], ALU.add)
                    chained(v.tensor_tensor(mod[:, scale, :, s], mod[:, scale, :, s], vecT[:, scale], ALU.add))
                    chained(v.scalar_tensor_tensor(out=mod[:, scale, :, s], in0=mod[:, scale, :, s], scalar=1.0,
                                                   in1=vecT[:, g], op0=ALU.add, op1=ALU.mult))
                dve.sem_inc(mod_ready, 1)

            with dve.Fori(0, 8) as i:
                for u in range(CHUNK_UNITS):
                    low(i * CHUNK_UNITS, u + AHEAD)
                evac_modT(i)
            dve.wait_ge(modT_evac, 8 + ONE)
            finish_mods(0, 1, 4, 1)

            def split_h(n):
                for b in range(8):
                    s, kg = b % NS, b // NS
                    dve.wait_ge(htmp_ready, 8 * (n - 1) + b + 1)
                    hi = h_hi[:, 4 * kg:4 * kg + 4, s]
                    chained(v.tensor_copy(hi, htmp[:, b % 2]))
                    v.tensor_tensor(h_lo[:, 4 * kg:4 * kg + 4, s], htmp[:, b % 2], hi.bitcast(F32), ALU.subtract
                                    ).then_inc(h_ready, 1)

            split_h(1)
            with dve.Fori(0, 4) as i:
                n0 = i * (4 * CHUNK_UNITS) + U_PROJ
                for q in range(4):
                    for u in range(CHUNK_UNITS):
                        low(n0, q * CHUNK_UNITS + u + AHEAD)
                    if q % 2:
                        j = q // 2
                        dve.wait_ge(unit_used, n0 + (q + 1) * CHUNK_UNITS)
                        dve.wait_ge(bin_landed[j], i * 16 + 16)
                        for s in range(NS):
                            ins = v.tensor_tensor(uqkv[:, s, bass.ds(i * (2 * COL) + j * COL, COL)], bank[2 * j + s][:],
                                                  bin_[:, j], ALU.add)
                        ins.then_inc(proj_evac, 1)
                evac_modT(i + 8)
            dve.wait_ge(router_in, 64)
            chained(v.tensor_copy(wrs[:, :, 0], wr[:]))
            v.tensor_tensor(wrs[:, :, 1], wr[:], wrs[:, :, 0].bitcast(F32), ALU.subtract).then_inc(wrs_ready, 1)
            dve.wait_ge(bias_in, 16 * ROWS * ROWS)
            for h in range(HEADS):
                b = bias[:, h].rearrange("p r c -> p (r c)")
                ins = v.tensor_tensor(b, b, mask, ALU.add)
            chained(ins)
            for b in range(1, 8, 2):
                dve.wait_ge(dft1_done, b + 1)
                v.tensor_copy(fa[:, b % 2, :, b // 2].rearrange("p c s t -> p s c t"),
                              bank[b][:].rearrange("p (s c t) -> p s c t", s=2, c=2)).then_inc(dft1_dve, 1)
            for o in range(4):
                hh, gp = o % 2, o // 2
                dve.wait_ge(dft2_hi, o + 1)
                sl = slice(4 * gp + hh, 4 * gp + hh + 3, 2)
                v.tensor_tensor(f_lo[:, sl], bank[o][:].rearrange("p (g s t) -> p g s t", g=2, s=2),
                                f_hi[:, sl].bitcast(F32), ALU.subtract).then_inc(dft2_lo, 1)
            def output_low(h):
                dve.wait_ge(o_hi_ready, h + 1)
                v.tensor_tensor(o_lo[:, bass.ds(h, 1)], bank[4][:, 0:2 * P].rearrange("p (a s t) -> p a s t", a=1, s=2),
                                o_hi[:, bass.ds(h, 1)].bitcast(F32), ALU.subtract).then_inc(o_ready, 1)

            def head_pair(i, first):
                n0 = i * (2 * CHUNK_UNITS) + U_ATT
                for j in range(2):
                    h = i * 2 + j
                    for u in range(CHUNK_UNITS):
                        low(n0, j * CHUNK_UNITS + u + AHEAD)
                        if u == 1:
                            dve.wait_ge(qk_done, h + 1)
                            v.tensor_copy(kcT[:], bank[1][:, 0:P]).then_inc(kcT_ready, 1)
                        if u == 4:
                            dve.wait_ge(scores_done, h + 1)
                            chained(v.tensor_scalar(scr[:, 0:2], bank[2][:, 0:2 * P].rearrange("p (c t) -> p c t", c=2),
                                                    SCALE, None, ALU.mult))
                            chained(v.scalar_tensor_tensor(
                                out=scr[:, 2], in0=bank[2][:, 2 * P:3 * P], scalar=SCALE,
                                in1=bias[:, bass.ds(h, 1)].rearrange("p h r c -> p (h r c)"), op0=ALU.mult, op1=ALU.add))
                            chained(v.tensor_reduce(smx[:, 0:1], scr[:, 0], X, ALU.max, negate=True))
                            chained(v.tensor_reduce(smx[:, 1:2], scr[:, 1:3].rearrange("p a t -> p (a t)"), X, ALU.max,
                                                    negate=True))
                            dve.sem_inc(scores_ready, 1)
                        if u == 5 and (j or not first):
                            output_low(h - 1)
                        if u == 7:
                            dve.wait_ge(exp_done, h + 1)
                            chained(v.reciprocal(smx[:, 4:6], smx[:, 2:4]))
                            chained(v.tensor_scalar(prb[:, 0], prb[:, 0], smx[:, 4:5], None, ALU.mult))
                            chained(v.tensor_scalar(prb[:, 1:3], prb[:, 1:3], smx[:, 5:6], None, ALU.mult))
                            dve.sem_inc(probs_ready, 1)
                    if j == 0:
                        evac_modT(i + 12)

            step.enter(0, 2 * 7)
            head_pair(0, True)
            step.leave(1)
            with dve.Fori(1, HEADS // 2) as i:
                step.enter(i, 2 * 7, first=1)
                head_pair(i, False)
            step.leave(HEADS // 2 - 1)
            output_low(HEADS - 1)
            dve.wait_ge(modT_evac, 16 + ONE)
            finish_mods(2, 3, 5, 2)
            with dve.Fori(0, 4) as i:
                step.enter(i, 2)
                n0 = i * 24 + U_MERGE
                for u in range(24):
                    low(n0, u + AHEAD)
                    if u in (7, 15):
                        j = u // 8
                        g = (ma, mb)[j]
                        dve.wait_ge(unit_used, n0 + u + 1)
                        dve.wait_ge(bin_landed[j], i * 16 + 16 * 5)
                        if j == 0:
                            dve.wait_ge(mT_done, i * 2 + ONE)
                        for s in range(NS):
                            ins = v.tensor_tensor(g[:, s], bank[2 * j + s][:], bin_[:, j], ALU.add)
                        ins.then_inc(gate_pre, 1)
                    if u in (19, 23):
                        j = u // 23
                        g = (ma, mb)[j]
                        dve.wait_ge(unit_used, n0 + u + 1)
                        dve.wait_ge(gate_sig, i * 2 + j + 1)
                        for s in range(NS):
                            ins = v.tensor_tensor(g[:, s], g[:, s], bank[4 + 2 * j + s][:], ALU.mult)
                        chained(ins)
                v.tensor_tensor(ma[:], ma[:], mb[:], ALU.add).then_inc(merged_ready, 1)
                for s in range(NS):
                    dve.wait_ge(m_hi_ready, i * 2 + s + 1)
                    v.tensor_tensor(m_lo[:, bass.ds(i * 4, 4), s], bank[4 + s][:].rearrange("p (k t) -> p k t", k=4),
                                    m_hi[:, bass.ds(i * 4, 4), s].bitcast(F32), ALU.subtract).then_inc(m_ready, 1)
            step.leave(4)
            dve.wait_ge(x1_in, 32)
            with dve.Fori(0, 2) as i:
                step.enter(i, 2)
                for j in range(2):
                    n0 = i * 16 + U_OUT
                    for u in range(CHUNK_UNITS):
                        low(n0, 8 * j + u + AHEAD)
                    dve.wait_ge(unit_used, n0 + 8 * j + 8)
                    dve.wait_ge(gab_ready, i * 2 + j + 1)
                    for s in range(NS):
                        ins = v.tensor_tensor(t2[:, j, s], gab[:, j, s], bank[4 * j + s][:], ALU.mult)
                    chained(ins)
                    xs = x1[:, :, bass.ds(i * (2 * COL) + j * COL, COL)]
                    v.tensor_tensor(xs, xs, t2[:, j], ALU.add).then_inc(x1_ready, 1)
            step.leave(2)
            inverse_rms(4, 2)
            for s in range(NS):
                chained(v.tensor_scalar(diag[:, s], ident, rms[:, 6 + s:7 + s], None, ALU.mult))
            dve.sem_inc(diag_ready, 1)
            split_h(2)

            def exponential(n):
                dve.sem_inc(route_arg, 1)
                dve.wait_ge(route_exp, n + 1)

            def across(x, shape):
                return x.to_broadcast([P] + shape)

            def pick_first(values, best, one_hot):
                chained(v.tensor_reduce(best, values, X, ALU.max))
                chained(v.tensor_tensor(one_hot, values, across(best.unsqueeze(2), [NS, 4]), ALU.is_equal))
                chained(v.tensor_tensor(one_hot, one_hot, across(first.unsqueeze(1), [NS, 4]), ALU.mult))
                chained(v.tensor_reduce(top, one_hot, X, ALU.max))
                chained(v.tensor_tensor(one_hot, one_hot, across(top.unsqueeze(2), [NS, 4]), ALU.is_equal))

            def column(at, width=1):
                c = rt[:, at:at + NS * width]
                return c if width == 1 else c.rearrange("p (s e) -> p s e", s=NS)

            arg, expd = column(0, 4), column(8, 4)
            group, picked, one, two = column(16, 4), column(24, 4), column(32, 4), column(40, 4)
            prod = rt[:, 48:80].rearrange("p (s g e) -> p s g e", s=NS, g=NG)
            weights = column(80, 4)
            top, best_g, share, best_1, best_2, w1, w2 = (column(88 + 2 * n) for n in range(7))
            dve.wait_ge(route_done, 1)
            for s in range(NS):
                chained(v.tensor_tensor(lg[:, s], bank[s][:, 0:NG + NE], br[:], ALU.add))
                chained(v.tensor_tensor(lg[:, s], lg[:, s], bank[s][:, NG + NE:2 * (NG + NE)], ALU.add))
            groups, fine = lg[:, :, 0:NG], lg[:, :, NG:].rearrange("p s (g e) -> p s g e", g=NG)
            pick_first(groups, best_g, group)
            chained(v.tensor_tensor(arg, groups, across(best_g.unsqueeze(2), [NS, 4]), ALU.subtract))
            exponential(0)
            chained(v.tensor_reduce(share, expd, X, ALU.add))
            chained(v.reciprocal(share, share))
            chained(v.tensor_tensor(prod, fine, across(group.unsqueeze(3), [NS, 4, 4]), ALU.mult))
            chained(v.tensor_reduce(picked, prod.rearrange("p s g e -> p s e g"), X, ALU.add))
            pick_first(picked, best_1, one)
            chained(v.scalar_tensor_tensor(out=picked, in0=one, scalar=-3e38, in1=picked, op0=ALU.mult, op1=ALU.add))
            pick_first(picked, best_2, two)
            chained(v.tensor_tensor(chosen[:].rearrange("p s (g e) -> p s g e", g=NG),
                                    across(group.unsqueeze(3), [NS, 4, 4]), across(one.unsqueeze(2), [NS, 4, 4]), ALU.mult))
            chained(v.tensor_tensor(prod, across(group.unsqueeze(3), [NS, 4, 4]), across(two.unsqueeze(2), [NS, 4, 4]),
                                    ALU.mult))
            chained(v.tensor_tensor(chosen[:].rearrange("p s (g e) -> p s g e", g=NG),
                                    chosen[:].rearrange("p s (g e) -> p s g e", g=NG), prod, ALU.add))
            dve.sem_inc(chosen_ready, 1)
            chained(v.tensor_tensor(rt[:, 0:2], best_2, best_1, ALU.subtract))
            exponential(1)
            chained(v.tensor_scalar(w1, rt[:, 8:10], 1.0, None, ALU.add))
            chained(v.reciprocal(w1, w1))
            chained(v.tensor_tensor(w1, w1, share, ALU.mult))
            chained(v.tensor_tensor(w2, w1, rt[:, 8:10], ALU.mult))
            chained(v.tensor_tensor(weights, one, across(w1.unsqueeze(2), [NS, 4]), ALU.mult))
            chained(v.tensor_tensor(two, two, across(w2.unsqueeze(2), [NS, 4]), ALU.mult))
            chained(v.tensor_tensor(weights, weights, two, ALU.add))
            chained(v.tensor_tensor(comb[:].rearrange("p s (g e) -> p s g e", g=NG), across(group.unsqueeze(3), [NS, 4, 4]),
                                    across(weights.unsqueeze(2), [NS, 4, 4]), ALU.mult))
            dve.wait_ge(y_zero, 1)
            dve.wait_ge(rank_done, 1)
            chained(v.memset(key[:], -1.0))
            for s in range(NS):
                chained(v.scalar_tensor_tensor(out=key[:, s, 0:NE], in0=bank[0][:, s * NE:(s + 1) * NE], scalar=1000.0,
                                               in1=chosen[:, s], op0=ALU.add, op1=ALU.mult))
                chained(v.tensor_scalar(key[:, s, 0:NE], key[:, s, 0:NE], -1000.0, None, ALU.add))
            most, more = rt[:, 110:111], rt[:, 111:112]
            chained(v.tensor_reduce(most, bank[0][:, 2 * NE:3 * NE], X, ALU.max))
            chained(v.tensor_scalar(more, most, float(CAP), 1.0, ALU.is_gt, ALU.add))
            for n in range(2, NS * TOK // CAP):
                chained(v.tensor_scalar(rt[:, 112:113], most, float(n * CAP), None, ALU.is_gt))
                chained(v.tensor_tensor(more, more, rt[:, 112:113], ALU.add))
            v.tensor_copy(rounds[:], more).then_inc(rounds_ready, 1)

            slots = cst_route[:, R_SLOT:R_SUM].rearrange("p (h c) -> p h c", h=2)

            def build_pick(p, x):
                for s in range(NS):
                    ins = v.tensor_scalar(pick_[:, x, s], slots[:, 0], key[:, s, bass.ds(p * PAIR + x, 1)], None, ALU.is_equal)
                ins.then_inc(pick_ready, 1)

            R = round_count(dve)
            with dve.Fori(0, R) as r:
                build_pick(0, 0)
                build_pick(0, 1)

                def run(mode, p, n, n0):
                    if mode != "first":
                        dve.wait_ge(y_added, n * 4 - 4 + ONE)

                    def add(c):
                        dve.wait_ge(scatter_done, n * 4 - 4 + c + 1 + ONE)
                        for s in range(NS):
                            ys = ysum[:, s, c * COL:(c + 1) * COL]
                            ins = v.tensor_tensor(ys, ys, bank[5 + s][:], ALU.add)
                        ins.then_inc(y_added, 1)

                    def hidden(x):
                        dve.wait_ge(silu_ready, n * 2 + x + 1)
                        v.tensor_tensor(hidf[:, x].rearrange("p k c -> p (k c)"), bank[2][:, 256:512],
                                        sgT[:].rearrange("p k c -> p (k c)"), ALU.mult).then_inc(hid_ready, 1)

                    for u, item in enumerate(sequence(mode)):
                        low(n0, u + AHEAD)
                        if item in (("gu", 0, 14), ("gu", 1, 14)):
                            dve.wait_ge(gather_done, r * FILLS + p * 8 + 4 * item[1] + 4)
                            build_pick(p + 1, item[1])
                        if item == ("gu", 1, 10):
                            dve.wait_ge(pickT_done, n + ONE)
                            for x in range(PAIR):
                                for s in range(NS):
                                    ins = v.tensor_scalar(pickd[:, x, s], slots, key[:, s, bass.ds(p * PAIR + x, 1)],
                                                          None, ALU.is_equal)
                            ins.then_inc(pickd_ready, 1)
                        if item == ("gu", 1, 3):
                            hidden(0)
                        if item in ADD[mode]:
                            add(ADD[mode][item])
                    if mode != "last":
                        hidden(1)
                        dve.wait_ge(unit_used, n0 + len(sequence(mode)))
                        dve.wait_ge(hid_ready, n * 2 + 2 + ONE)
                        v.tensor_copy(hidT[:, :, :, 0], hidf[:]).then_inc(hid_split, 1)
                        dve.wait_ge(hid_split, n + 1)
                        v.tensor_tensor(hidT[:, :, :, 1], hidf[:], hidT[:, :, :, 0].bitcast(F32), ALU.subtract
                                        ).then_inc(hidT_ready, 1)
                    if mode != "first":
                        add(3)

                steps(dve, r, run)
                dve.wait_ge(pick_ready, r * (2 * PAIRS + 2) + 2 * PAIRS + 2)
                v.tensor_scalar(key[:], key[:], -float(CAP), None, ALU.add).then_inc(key_moved, 1)
                dve.wait_ge(key_moved, r + 1)
            dve.wait_ge(y_added, R * (4 * PAIRS) + ONE)
            dve.sem_inc(rounds_done, 1)
            step = Tally(dve, tail_step)
            for n in range(D // COL):
                for s in range(NS):
                    dve.wait_ge(ga2_done, NS * n + s + 1)
                    cols = slice(n * COL, (n + 1) * COL)
                    ins = v.tensor_tensor(ysum[:, s, cols], ysum[:, s, cols], bank[NS * n + s][:], ALU.mult)
                chained(ins)
                v.tensor_tensor(x1[:, :, cols], x1[:, :, cols], ysum[:, :, cols], ALU.add).then_inc(x2_ready, 1)
            dve.wait_ge(chunk_squares, D // COL)
            chained(v.tensor_reduce(rms[:, 8:10], smx[:].rearrange("p (n s) -> p s n", s=NS), X, ALU.add))
            dve.sem_inc(squares_done, 1)
            inverse_rms(8, 3)
            dve.wait_ge(gfin_in, 16)
            for n in range(D // COL):
                for s in range(NS):
                    cols = slice(n * COL, (n + 1) * COL)
                    v.scalar_tensor_tensor(out=x1[:, s, cols], in0=x1[:, s, cols], scalar=rms[:, 10 + s:11 + s],
                                           in1=gfin[:, cols], op0=ALU.mult, op1=ALU.mult).then_inc(y_ready, 1)


_INS = ["x_prompt", "x_sample", "cache_k_ctx", "cache_v_ctx", "c", "c_ctx", "norm1_g", "norm2_g", "w_ada", "b_ada",
        "w_in", "b_in", "w_fourier", "w_na_o", "rpb", "w_out", "w_router_group", "b_router_group",
        "w_router_expert", "b_router_expert", "w_exp_gate", "w_exp_up", "w_exp_down", "final_norm_g"]
_OUTS = [(1, TOK, D), (1, TOK, D), (1, 1, TOK, HEADS, HD), (1, 1, TOK, HEADS, HD)]


def kernel(**inputs):
    import concourse.bacc as bacc
    from concourse.bass_utils import run_bass_kernel_spmd

    nc = bacc.Bacc("TRN2", target_bir_lowering=False, num_devices=1)
    arrays, args = {}, []
    for name in _INS:
        a = np.ascontiguousarray(inputs[name])
        arrays[f"in_{name}"] = a
        args.append(nc.dram_tensor(f"in_{name}", a.shape, mybir.dt.from_np(a.dtype), kind="ExternalInput").ap())
    for name, a in (("shape_constants", shape_constants()), ("routing_constants", routing_constants())):
        arrays[name] = a
        args.append(nc.dram_tensor(name, a.shape, F32, kind="ExternalInput").ap())
    for i, shape in enumerate(_OUTS):
        args.append(nc.dram_tensor(f"out_{i}", shape, F32, kind="ExternalOutput").ap())
    backbone_step(nc, *args)
    result = run_bass_kernel_spmd(nc, [arrays], core_ids=[0])
    return tuple(result.results[0][f"out_{i}"] for i in range(len(_OUTS)))
```
